# Optimizing a Trainium2 kernel written in Bass

```python
import math
import jax, jax.numpy as jnp
from jax import lax
import numpy as np
import jax
import jax.numpy as jnp

D_MODEL = 1024
BATCH = 1
SEQ = 256
DEPTH = 1

GRID_W = 64
CTX_LEN = 256
N_MOD = 6
EPS = 1e-6

F_GROUPS = 8
F_GROUP_DIM = 128
F_WIDTH = F_GROUPS * F_GROUP_DIM

D_INNER = 2 * D_MODEL
HEAD_DIM = 64
N_HEADS = D_INNER // HEAD_DIM
N_GROUPS = 4
HEADS_PER_GROUP = N_HEADS // N_GROUPS
D_STATE = 128
BC_WIDTH = N_GROUPS * D_STATE
CONV_K = 5
CHUNK = 128

N_EXPERTS = 32
TOP_K = 4
D_FF = D_MODEL
SWIGLU_LIMIT = 7.0
SWIGLU_ALPHA = 1.702
MOE_BLOCK = 128

OFF_X = 0
OFF_BF = OFF_X + D_INNER
OFF_BB = OFF_BF + BC_WIDTH
OFF_DT = OFF_BB + BC_WIDTH
OFF_CF = OFF_DT + 2 * N_HEADS
OFF_CB = OFF_CF + BC_WIDTH
OFF_Z = OFF_CB + BC_WIDTH
OFF_F = OFF_Z + D_INNER
OFF_GF = OFF_F + F_WIDTH
OFF_GS = OFF_GF + D_MODEL
IN_COLS = OFF_GS + D_MODEL
XB_CH = OFF_DT
CONV_CH = XB_CH + 2 * BC_WIDTH


def rmsnorm(v, w):
    v32 = v.astype(jnp.float32)
    inv = lax.rsqrt(jnp.mean(v32 * v32, axis=-1, keepdims=True) + EPS)
    return (v32 * inv * w.astype(jnp.float32)).astype(v.dtype)

def dwconv_centred(u, w, bias):
    ch = u.shape[-1]
    y = lax.conv_general_dilated(u, w[:, None, :].astype(u.dtype), window_strides=(1,),
                                 padding=[(CONV_K // 2, CONV_K // 2)],
                                 dimension_numbers=('NWC', 'WIO', 'NWC'),
                                 feature_group_count=ch)
    return y + bias

def _decay_matrix(a_cs):
    q = a_cs.shape[-1]
    mask = jnp.tril(jnp.ones((q, q), dtype=bool))
    diff = a_cs[..., :, None] - a_cs[..., None, :]
    return jnp.exp(jnp.where(mask, diff, -jnp.inf))

def _ssd_chunks(x, dt, a, b_in):
    bsz, l = x.shape[:2]
    nc = l // CHUNK
    a_cs = jnp.cumsum((dt * a).reshape(bsz, nc, CHUNK, N_GROUPS, HEADS_PER_GROUP), axis=2)
    xdt = (x.astype(jnp.float32) * dt[..., None]).reshape(bsz, nc, CHUNK, N_GROUPS, HEADS_PER_GROUP, HEAD_DIM)
    bc = b_in.astype(jnp.float32).reshape(bsz, nc, CHUNK, N_GROUPS, D_STATE)
    decay_to_end = jnp.exp(a_cs[:, :, -1:] - a_cs)
    states = jnp.einsum('bcsgn,bcsgh,bcsghp->bcghpn', bc, decay_to_end, xdt)
    chunk_decay = jnp.exp(a_cs[:, :, -1])
    return a_cs, xdt, bc, states, chunk_decay

def _carry_states(states, chunk_decay, h0):
    def step(h, inp):
        s, dec = inp
        return h * dec[..., None, None] + s, h
    h_final, h_prev = lax.scan(step, h0, (jnp.moveaxis(states, 1, 0), jnp.moveaxis(chunk_decay, 1, 0)))
    return jnp.moveaxis(h_prev, 0, 1), h_final

def ssd_final_state(x, dt, a, b_in, h0):
    _, _, _, states, chunk_decay = _ssd_chunks(x, dt, a, b_in)
    return _carry_states(states, chunk_decay, h0)[1]

def ssd_scan(x, dt, a, b_in, c_in, h0):
    bsz, l = x.shape[:2]
    nc = l // CHUNK
    a_cs, xdt, bc, states, chunk_decay = _ssd_chunks(x, dt, a, b_in)
    h_prev, _ = _carry_states(states, chunk_decay, h0)
    cc = c_in.astype(jnp.float32).reshape(bsz, nc, CHUNK, N_GROUPS, D_STATE)
    decay_in = _decay_matrix(jnp.moveaxis(a_cs, 2, -1))
    cb = jnp.einsum('bclgn,bcsgn->bcgls', cc, bc)
    y_diag = jnp.einsum('bcgls,bcghls,bcsghp->bclghp', cb, decay_in, xdt)
    y_off = jnp.einsum('bclgn,bcghpn,bclgh->bclghp', cc, h_prev, jnp.exp(a_cs))
    return (y_diag + y_off).reshape(bsz, l, N_HEADS, HEAD_DIM)

def moe_ffn(h, w_router, b_router, w_gate_up, b_gate_up, w_down, b_down):
    bsz, n, d = h.shape
    tok = h.reshape(-1, d)
    n_tok = tok.shape[0]
    logits = (tok @ w_router + b_router).astype(jnp.float32)
    top_logit, top_idx = lax.top_k(logits, TOP_K)
    top_w = jax.nn.softmax(top_logit, axis=-1)
    flat_e = top_idx.reshape(-1)
    flat_w = top_w.reshape(-1)
    n_assign = flat_e.shape[0]
    order = jnp.argsort(flat_e)
    e_sorted = flat_e[order]
    tok_sorted = (order // TOP_K).astype(jnp.int32)
    counts = jnp.bincount(flat_e, length=N_EXPERTS)
    padded = (counts + MOE_BLOCK - 1) // MOE_BLOCK * MOE_BLOCK
    pad_end = jnp.cumsum(padded)
    pad_start = pad_end - padded
    start = jnp.cumsum(counts) - counts
    dest = pad_start[e_sorted] + jnp.arange(n_assign) - start[e_sorted]
    n_blocks = (n_assign + MOE_BLOCK - 1) // MOE_BLOCK + N_EXPERTS
    rows = n_blocks * MOE_BLOCK
    row_tok = jnp.full((rows,), n_tok, jnp.int32).at[dest].set(tok_sorted)
    row_w = jnp.zeros((rows,), jnp.float32).at[dest].set(flat_w[order])
    blk_e = jnp.minimum(jnp.searchsorted(pad_end, jnp.arange(n_blocks) * MOE_BLOCK, side='right'),
                        N_EXPERTS - 1)
    tok_ext = jnp.concatenate([tok, jnp.zeros((1, d), tok.dtype)], axis=0)
    xb = tok_ext[row_tok].reshape(n_blocks, MOE_BLOCK, d)

    def expert_block(args):
        xe, e = args
        gu = xe @ w_gate_up[e] + b_gate_up[e]
        gate = jnp.minimum(gu[:, :D_FF], SWIGLU_LIMIT)
        up = jnp.clip(gu[:, D_FF:], -SWIGLU_LIMIT, SWIGLU_LIMIT)
        act = (up + 1.0) * gate * jax.nn.sigmoid(SWIGLU_ALPHA * gate)
        return act @ w_down[e] + b_down[e]

    yb = lax.map(expert_block, (xb, blk_e)).reshape(rows, d)
    yb = yb * row_w[:, None].astype(yb.dtype)
    out = jnp.zeros_like(tok_ext).at[row_tok].add(yb)[:n_tok]
    return out.reshape(bsz, n, d)

def first_inputs(seed: int = 0) -> dict:
    key = jax.random.key(seed)
    ks = jax.random.split(key, 25)
    f32 = jnp.float32
    D = D_MODEL

    def nrm(k, shape, scale):
        return jax.random.normal(k, shape, f32) * scale

    dt0 = jnp.exp(jax.random.uniform(ks[11], (DEPTH, 2, N_HEADS), f32, math.log(1e-3), math.log(1e-1)))
    return {
        'x': nrm(ks[0], (BATCH, SEQ, D), 1.0),
        'c': nrm(ks[1], (BATCH, D), 1.0),
        'ctx': nrm(ks[2], (BATCH, CTX_LEN, D), 1.0),
        'c_ctx': nrm(ks[3], (D,), 1.0),
        'w_mod': nrm(ks[4], (DEPTH, D, N_MOD * D), 0.5 * D ** -0.5),
        'b_mod': nrm(ks[5], (DEPTH, N_MOD * D), 0.02),
        'norm1_w': 1.0 + nrm(ks[6], (DEPTH, D), 0.05),
        'norm2_w': 1.0 + nrm(ks[7], (DEPTH, D), 0.05),
        'w_in': nrm(ks[8], (DEPTH, D, IN_COLS), D ** -0.5),
        'conv_w': nrm(ks[9], (DEPTH, CONV_K, CONV_CH), CONV_K ** -0.5),
        'conv_b': nrm(ks[10], (DEPTH, CONV_CH), 0.02),
        'dt_bias': dt0 + jnp.log(-jnp.expm1(-dt0)),
        'a_log': jnp.log(jax.random.uniform(ks[12], (DEPTH, 2, N_HEADS), f32, 1.0, 16.0)),
        'd_skip': 1.0 + nrm(ks[13], (DEPTH, N_HEADS), 0.1),
        'ssd_norm_w': 1.0 + nrm(ks[14], (DEPTH, D_INNER), 0.05),
        'w_ssd_out': nrm(ks[15], (DEPTH, D_INNER, D), D_INNER ** -0.5),
        'w_four_out': nrm(ks[16], (DEPTH, F_WIDTH, D), F_WIDTH ** -0.5),
        'w_o': nrm(ks[17], (DEPTH, D, D), D ** -0.5),
        'w_router': nrm(ks[18], (DEPTH, D, N_EXPERTS), D ** -0.5),
        'b_router': nrm(ks[19], (DEPTH, N_EXPERTS), 0.01),
        'w_gate_up': nrm(ks[20], (DEPTH, N_EXPERTS, D, 2 * D_FF), D ** -0.5),
        'b_gate_up': nrm(ks[21], (DEPTH, N_EXPERTS, 2 * D_FF), 0.02),
        'w_down': nrm(ks[22], (DEPTH, N_EXPERTS, D_FF, D), D_FF ** -0.5),
        'b_down': nrm(ks[23], (DEPTH, N_EXPERTS, D), 0.02),
        'final_norm_w': 1.0 + nrm(ks[24], (D,), 0.05),
    }

def first_block(x, c, ctx, c_ctx, w_mod, b_mod, norm1_w, norm2_w, w_in, conv_w, conv_b, dt_bias,
              a_log, d_skip, ssd_norm_w, w_ssd_out, w_four_out, w_o, w_router, b_router,
              w_gate_up, b_gate_up, w_down, b_down, final_norm_w):
    bsz, n, D = x.shape
    n_ctx = ctx.shape[1]
    h0 = jnp.zeros((bsz, N_GROUPS, HEADS_PER_GROUP, HEAD_DIM, D_STATE), jnp.float32)
    for layer in range(DEPTH):
        mod = jax.nn.silu(c) @ w_mod[layer] + b_mod[layer]
        sh1, sc1, g1, sh2, sc2, g2 = jnp.split(mod[:, None, :], N_MOD, axis=-1)
        mod_c = jax.nn.silu(c_ctx) @ w_mod[layer][:, :2 * D] + b_mod[layer][:2 * D]
        sh1_c, sc1_c = mod_c[:D], mod_c[D:]
        a = -jnp.exp(a_log[layer].astype(jnp.float32))

        hc = rmsnorm(ctx, norm1_w[layer]) * (1.0 + sc1_c) + sh1_c
        pc = hc @ w_in[layer][:, :OFF_CF]
        xb_c = jax.nn.silu(dwconv_centred(pc[..., :XB_CH], conv_w[layer][:, :XB_CH], conv_b[layer][:XB_CH]))
        xc = xb_c[..., :D_INNER].reshape(bsz, n_ctx, N_HEADS, HEAD_DIM)
        bfc = xb_c[..., OFF_BF:OFF_BB].reshape(bsz, n_ctx, N_GROUPS, D_STATE)
        bbc = xb_c[..., OFF_BB:OFF_DT].reshape(bsz, n_ctx, N_GROUPS, D_STATE)
        dtc = jax.nn.softplus(pc[..., OFF_DT:OFF_CF].astype(jnp.float32).reshape(bsz, n_ctx, 2, N_HEADS)
                              + dt_bias[layer].astype(jnp.float32))
        hf_ctx = ssd_final_state(xc, dtc[:, :, 0], a[0], bfc, h0)
        hb_ctx = ssd_final_state(xc[:, ::-1], dtc[:, ::-1, 1], a[1], bbc[:, ::-1], h0)

        h = rmsnorm(x, norm1_w[layer]) * (1.0 + sc1) + sh1
        p = h @ w_in[layer]

        xl = jax.nn.silu(dwconv_centred(p[..., :XB_CH], conv_w[layer][:, :XB_CH], conv_b[layer][:XB_CH]))
        cl = jax.nn.silu(dwconv_centred(p[..., OFF_CF:OFF_Z], conv_w[layer][:, XB_CH:], conv_b[layer][XB_CH:]))
        xs = xl[..., :D_INNER].reshape(bsz, n, N_HEADS, HEAD_DIM)
        bf = xl[..., OFF_BF:OFF_BB].reshape(bsz, n, N_GROUPS, D_STATE)
        bb = xl[..., OFF_BB:OFF_DT].reshape(bsz, n, N_GROUPS, D_STATE)
        cf = cl[..., :BC_WIDTH].reshape(bsz, n, N_GROUPS, D_STATE)
        cb = cl[..., BC_WIDTH:].reshape(bsz, n, N_GROUPS, D_STATE)
        dtl = jax.nn.softplus(p[..., OFF_DT:OFF_CF].astype(jnp.float32).reshape(bsz, n, 2, N_HEADS)
                              + dt_bias[layer].astype(jnp.float32))
        y_f = ssd_scan(xs, dtl[:, :, 0], a[0], bf, cf, hf_ctx)
        y_b = ssd_scan(xs[:, ::-1], dtl[:, ::-1, 1], a[1], bb[:, ::-1], cb[:, ::-1], hb_ctx)[:, ::-1]
        y = y_f + y_b + d_skip[layer].astype(jnp.float32)[:, None] * xs.astype(jnp.float32)
        y = y.reshape(bsz, n, D_INNER).astype(x.dtype)
        z = p[..., OFF_Z:OFF_F]
        y_ssd = rmsnorm(y * jax.nn.silu(z), ssd_norm_w[layer]) @ w_ssd_out[layer]

        u = p[..., OFF_F:OFF_GF].astype(jnp.float32).reshape(bsz, n, F_GROUPS, F_GROUP_DIM)
        u = jnp.fft.fft2(u, axes=(1, 3), norm='ortho').real.reshape(bsz, n, F_WIDTH).astype(x.dtype)
        y_four = u @ w_four_out[layer]

        gate_f = jax.nn.sigmoid(p[..., OFF_GF:OFF_GS])
        gate_s = jax.nn.sigmoid(p[..., OFF_GS:IN_COLS])
        mix = (gate_f * y_four + gate_s * y_ssd) @ w_o[layer]
        x = x + g1 * mix

        h2 = rmsnorm(x, norm2_w[layer]) * (1.0 + sc2) + sh2
        x = x + g2 * moe_ffn(h2, w_router[layer], b_router[layer], w_gate_up[layer], b_gate_up[layer],
                             w_down[layer], b_down[layer])
    return rmsnorm(x, final_norm_w)


DEPTH_2 = 2

GROUP = D_MODEL // N_GROUPS
CHUNK_2 = 64

HGRN_HEADS = 4
GLA_HEADS = 4
GLA_KEY = GROUP // (2 * GLA_HEADS)
GLA_GATE_RANK = 16
GLA_GATE_NORM = 16.0
RWKV_HEADS = 4
RWKV_HEAD = GROUP // RWKV_HEADS
RWKV_DECAY_RANK = 64
RWKV_A_RANK = 64
RWKV_V_RANK = 32
RWKV_GATE_RANK = 160
RWKV_LNX_EPS = 64e-5
RET_HEADS = 4
RET_KEY = GROUP // RET_HEADS
ROPE_BASE = 10000.0

HGRN_COLS = (GROUP, GROUP, GROUP, GROUP)
GLA_COLS = (GLA_HEADS * GLA_KEY, GLA_HEADS * GLA_KEY, GROUP, GLA_GATE_RANK, GROUP)
RWKV_COLS = (GROUP, GROUP, GROUP, RWKV_DECAY_RANK, RWKV_A_RANK, RWKV_GATE_RANK)
RET_COLS = (GROUP, GROUP, GROUP, GROUP)
MIXER_COLS = (sum(HGRN_COLS), sum(GLA_COLS), sum(RWKV_COLS), sum(RET_COLS))
IN_COLS_2 = sum(MIXER_COLS)

FFN_DENSE = 2816
N_EXPERTS_2 = 8
TOP_K_2 = 2
FFN_EXPERT = 1408
N_DENSE = (DEPTH_2 + 1) // 2
N_MOE = DEPTH_2 // 2

DN_ALPHA = (2.0 * DEPTH_2) ** 0.25
DN_BETA = (8.0 * DEPTH_2) ** -0.25
LN_EPS = 1e-5
F32 = jnp.float32


def _split(p, sizes):
    return jnp.split(p, np.cumsum(sizes)[:-1].tolist(), axis=-1)

def _heads(t, n):
    return t.reshape(t.shape[:-1] + (n, t.shape[-1] // n))

def _merge(t):
    return t.reshape(t.shape[:-2] + (t.shape[-2] * t.shape[-1],))

def _layer_norm(x, g, b):
    x = x.astype(F32)
    mu = jnp.mean(x, -1, keepdims=True)
    var = jnp.mean(jnp.square(x - mu), -1, keepdims=True)
    return (x - mu) * lax.rsqrt(var + LN_EPS) * g + b

def _rms_norm(x, g, eps=1e-6):
    return x * lax.rsqrt(jnp.mean(jnp.square(x), -1, keepdims=True) + eps) * g

def _group_norm(x, eps):
    mu = jnp.mean(x, -1, keepdims=True)
    var = jnp.mean(jnp.square(x - mu), -1, keepdims=True)
    return (x - mu) * lax.rsqrt(var + eps)

def _to_chunks(t):
    b, s, h, d = t.shape
    return t.reshape(b, s // CHUNK_2, CHUNK_2, h, d).transpose(1, 0, 3, 2, 4)

def _from_chunks(t):
    n, b, h, c, d = t.shape
    return t.transpose(1, 0, 3, 2, 4).reshape(b, n * c, h, d)

def _chunked_gated_linear(q, k, v, log_f):
    b, _, h, kd = q.shape
    vd = v.shape[-1]
    qc, kc, vc, gc = (_to_chunks(t.astype(F32)) for t in (q, k, v, log_f))
    causal = jnp.tril(jnp.ones((CHUNK_2, CHUNK_2), dtype=bool))

    def step(state, inp):
        qi, ki, vi, gi = inp
        cum = jnp.cumsum(gi, axis=2)
        diff = cum[:, :, :, None, :] - cum[:, :, None, :, :]
        decay = jnp.exp(jnp.where(causal[:, :, None], diff, -jnp.inf))
        scores = jnp.einsum('bhik,bhjk,bhijk->bhij', qi, ki, decay)
        out = (jnp.einsum('bhij,bhjv->bhiv', scores, vi)
               + jnp.einsum('bhik,bhkv->bhiv', qi * jnp.exp(cum), state))
        cum_end = cum[:, :, -1:, :]
        state = (jnp.exp(cum_end[:, :, 0, :])[..., None] * state
                 + jnp.einsum('bhjk,bhjv->bhkv', ki * jnp.exp(cum_end - cum), vi))
        return state, out

    _, o = lax.scan(step, jnp.zeros((b, h, kd, vd), F32), (qc, kc, vc, gc))
    return _from_chunks(o)

def _retention_chunkwise(q, k, v, log_gamma):
    b, _, h, kd = q.shape
    vd = v.shape[-1]
    qc, kc, vc = (_to_chunks(t.astype(F32)) for t in (q, k, v))
    idx = jnp.arange(CHUNK_2, dtype=F32)
    rel = idx[:, None] - idx[None, :]
    intra = jnp.exp(jnp.where(rel >= 0, rel * log_gamma[:, None, None], -jnp.inf))
    q_dec = jnp.exp((idx + 1.0)[None, :] * log_gamma[:, None])
    k_dec = jnp.exp((CHUNK_2 - 1.0 - idx)[None, :] * log_gamma[:, None])
    c_dec = jnp.exp(CHUNK_2 * log_gamma)

    def step(state, inp):
        qi, ki, vi = inp
        scores = jnp.einsum('bhik,bhjk->bhij', qi, ki) * intra
        out = (jnp.einsum('bhij,bhjv->bhiv', scores, vi)
               + jnp.einsum('bhik,bhkv->bhiv', qi * q_dec[..., None], state))
        state = (c_dec[:, None, None] * state
                 + jnp.einsum('bhjk,bhjv->bhkv', ki * k_dec[..., None], vi))
        return state, out

    _, o = lax.scan(step, jnp.zeros((b, h, kd, vd), F32), (qc, kc, vc))
    return _from_chunks(o)

def _rotary(t, positions):
    half = t.shape[-1] // 2
    inv_freq = ROPE_BASE ** (-jnp.arange(half, dtype=F32) / half)
    ang = positions.astype(F32)[:, :, None, None] * inv_freq
    cos, sin = jnp.cos(ang), jnp.sin(ang)
    t1, t2 = t[..., :half], t[..., half:]
    return jnp.concatenate([t1 * cos - t2 * sin, t1 * sin + t2 * cos], axis=-1)

def _rwkv7_scan(r, w, k, v, kk, a):
    b, _, h, n = r.shape
    xs = tuple(jnp.moveaxis(t, 1, 0) for t in (r, w, k, v, kk, a))

    def step(state, inp):
        rt, wt, kt, vt, kkt, at = inp
        sa = jnp.einsum('bhvk,bhk->bhv', state, -kkt)
        state = (state * wt[:, :, None, :]
                 + sa[..., None] * (kkt * at)[:, :, None, :]
                 + vt[..., None] * kt[:, :, None, :])
        return state, jnp.einsum('bhvk,bhk->bhv', state, rt)

    _, o = lax.scan(step, jnp.zeros((b, h, n, n), F32), xs)
    return jnp.moveaxis(o, 0, 1)

def _hgrn2_mixer(p, lb, norm_g):
    q_raw, f_raw, i_raw, g_raw = _split(p, HGRN_COLS)
    f = lb + (1.0 - lb) * jax.nn.sigmoid(f_raw)
    hd = lambda t: _heads(t, HGRN_HEADS)
    o = _chunked_gated_linear(hd(jax.nn.silu(q_raw)), hd(1.0 - f), hd(i_raw), hd(jnp.log(f)))
    o = _rms_norm(o, norm_g) * jax.nn.silu(hd(g_raw))
    return _merge(o)

def _gla_mixer(p, gate_w2, gate_b, norm_g):
    q, k, v, g_lr, r = _split(p, GLA_COLS)
    log_f = jax.nn.log_sigmoid(g_lr @ gate_w2 + gate_b) / GLA_GATE_NORM
    hd = lambda t: _heads(t, GLA_HEADS)
    o = _chunked_gated_linear(hd(q) * GLA_KEY ** -0.5, hd(k), hd(v), hd(log_f))
    o = _rms_norm(o, norm_g) * jax.nn.silu(hd(r))
    return _merge(o)

def _rwkv7_mixer(p, v_first, v_mix, mu, w0, w2, a0, a2, g2, k_k, k_a, r_k, lnx_g, lnx_b):
    p_prev = jnp.pad(p, ((0, 0), (1, 0), (0, 0)))[:, :-1]
    p = p + (p_prev - p) * mu
    r, k, v, w_lr, a_lr, g_lr = _split(p, RWKV_COLS)
    w = -jax.nn.softplus(-(w0 + jnp.tanh(w_lr) @ w2)) - 0.5
    decay = jnp.exp(-jnp.exp(w))
    a = jax.nn.sigmoid(a0 + a_lr @ a2)
    g = jax.nn.sigmoid(g_lr) @ g2
    if v_mix is None:
        v_first = v
    else:
        v0, v1, v2 = v_mix
        v = v + (v_first - v) * jax.nn.sigmoid(v0 + (v @ v1) @ v2)
    hd = lambda t: _heads(t, RWKV_HEADS)
    kk = hd(k * k_k)
    kk = kk / jnp.maximum(jnp.sqrt(jnp.sum(jnp.square(kk), -1, keepdims=True)), 1e-12)
    k = k * (1.0 + (a - 1.0) * k_a)
    rh, kh, vh = hd(r), hd(k), hd(v)
    o = _rwkv7_scan(rh, hd(decay), kh, vh, kk, hd(a))
    o = _group_norm(o, RWKV_LNX_EPS) * hd(lnx_g) + hd(lnx_b)
    o = o + jnp.sum(rh * kh * r_k, -1, keepdims=True) * vh
    return _merge(o) * g, v_first

def _retnet_mixer(p, positions, log_gamma):
    q, k, v, g = _split(p, RET_COLS)
    hd = lambda t: _heads(t, RET_HEADS)
    qh = _rotary(hd(q), positions)
    kh = _rotary(hd(k), positions) * RET_KEY ** -0.5
    o = _group_norm(_retention_chunkwise(qh, kh, hd(v), log_gamma), LN_EPS)
    return jax.nn.silu(g) * _merge(o)

def _swiglu(h, wg, wu, wd):
    return (jax.nn.silu(h @ wg) * (h @ wu)) @ wd

def _moe(h, router, wg, wu, wd):
    b, s, d = h.shape
    hf = h.reshape(b * s, d)
    probs = jax.nn.softmax((hf @ router).astype(F32), axis=-1)
    top_p, top_i = lax.top_k(probs, TOP_K_2)
    top_p = top_p / jnp.sum(top_p, -1, keepdims=True)
    gates = jnp.sum(jax.nn.one_hot(top_i, N_EXPERTS_2, dtype=F32) * top_p[..., None], axis=1)
    out = jnp.zeros_like(hf)
    for e in range(N_EXPERTS_2):
        out = out + gates[:, e:e + 1] * _swiglu(hf, wg[e], wu[e], wd[e])
    return out.reshape(b, s, d)

def second_inputs(seed: int = 0) -> dict:
    key = jax.random.key(seed)
    ks = iter(jax.random.split(key, 48))

    def nrm(shape, scale):
        return scale * jax.random.normal(next(ks), shape, F32)

    D = D_MODEL
    decay_base = -6.0 + 5.0 * (jnp.arange(GROUP, dtype=F32) / (GROUP - 1)) ** 0.9
    return {
        'x': nrm((BATCH, SEQ, D), 1.0),
        'positions': jnp.broadcast_to(jnp.arange(SEQ, dtype=jnp.int32)[None, :], (BATCH, SEQ)),
        'w_in': nrm((DEPTH_2, D, IN_COLS_2), D ** -0.5),
        'w_out': nrm((DEPTH_2, D, D), DN_BETA * D ** -0.5),
        'ln1_g': 1.0 + nrm((DEPTH_2, D), 0.01),
        'ln1_b': nrm((DEPTH_2, D), 0.01),
        'ln2_g': 1.0 + nrm((DEPTH_2, D), 0.01),
        'ln2_b': nrm((DEPTH_2, D), 0.01),
        'hgrn_lb_logits': nrm((DEPTH_2, GROUP), 0.5),
        'hgrn_norm_g': 1.0 + nrm((DEPTH_2, GROUP // HGRN_HEADS), 0.01),
        'gla_gate_w2': nrm((DEPTH_2, GLA_GATE_RANK, GLA_HEADS * GLA_KEY), GLA_GATE_RANK ** -0.5),
        'gla_gate_b': nrm((DEPTH_2, GLA_HEADS * GLA_KEY), 0.1),
        'gla_norm_g': 1.0 + nrm((DEPTH_2, GROUP // GLA_HEADS), 0.01),
        'rwkv_mu': jax.random.uniform(next(ks), (DEPTH_2, sum(RWKV_COLS)), F32),
        'rwkv_w0': decay_base[None, :] + nrm((DEPTH_2, GROUP), 0.1),
        'rwkv_w2': nrm((DEPTH_2, RWKV_DECAY_RANK, GROUP), 0.5 * RWKV_DECAY_RANK ** -0.5),
        'rwkv_a0': nrm((DEPTH_2, GROUP), 0.1),
        'rwkv_a2': nrm((DEPTH_2, RWKV_A_RANK, GROUP), 0.5 * RWKV_A_RANK ** -0.5),
        'rwkv_g2': nrm((DEPTH_2, RWKV_GATE_RANK, GROUP), RWKV_GATE_RANK ** -0.5),
        'rwkv_k_k': 0.85 + nrm((DEPTH_2, GROUP), 0.02),
        'rwkv_k_a': 1.0 + nrm((DEPTH_2, GROUP), 0.02),
        'rwkv_r_k': -0.04 + nrm((DEPTH_2, RWKV_HEADS, RWKV_HEAD), 0.02),
        'rwkv_lnx_g': 1.0 + nrm((DEPTH_2, GROUP), 0.01),
        'rwkv_lnx_b': nrm((DEPTH_2, GROUP), 0.01),
        'rwkv_v0': 1.0 + nrm((DEPTH_2 - 1, GROUP), 0.1),
        'rwkv_v1': nrm((DEPTH_2 - 1, GROUP, RWKV_V_RANK), GROUP ** -0.5),
        'rwkv_v2': nrm((DEPTH_2 - 1, RWKV_V_RANK, GROUP), 0.5 * RWKV_V_RANK ** -0.5),
        'ffn_w_gate': nrm((N_DENSE, D, FFN_DENSE), D ** -0.5),
        'ffn_w_up': nrm((N_DENSE, D, FFN_DENSE), D ** -0.5),
        'ffn_w_down': nrm((N_DENSE, FFN_DENSE, D), DN_BETA * FFN_DENSE ** -0.5),
        'moe_router': nrm((N_MOE, D, N_EXPERTS_2), D ** -0.5),
        'moe_w_gate': nrm((N_MOE, N_EXPERTS_2, D, FFN_EXPERT), D ** -0.5),
        'moe_w_up': nrm((N_MOE, N_EXPERTS_2, D, FFN_EXPERT), D ** -0.5),
        'moe_w_down': nrm((N_MOE, N_EXPERTS_2, FFN_EXPERT, D), DN_BETA * FFN_EXPERT ** -0.5),
    }

def second_block(x, positions, w_in, w_out, ln1_g, ln1_b, ln2_g, ln2_b, hgrn_lb_logits, hgrn_norm_g,
              gla_gate_w2, gla_gate_b, gla_norm_g, rwkv_mu, rwkv_w0, rwkv_w2, rwkv_a0, rwkv_a2,
              rwkv_g2, rwkv_k_k, rwkv_k_a, rwkv_r_k, rwkv_lnx_g, rwkv_lnx_b, rwkv_v0, rwkv_v1,
              rwkv_v2, ffn_w_gate, ffn_w_up, ffn_w_down, moe_router, moe_w_gate, moe_w_up,
              moe_w_down):
    out_dtype = x.dtype
    h = x.astype(F32)
    lb_all = jnp.cumsum(jax.nn.softmax(hgrn_lb_logits.astype(F32), axis=0), axis=0)
    lb_all = lb_all - lb_all[:1]
    log_gamma = jnp.log(1.0 - 2.0 ** (-5.0 - jnp.arange(RET_HEADS, dtype=F32)))
    v_first = None
    for l in range(DEPTH_2):
        p = jnp.einsum('btd,dc->btc', h, w_in[l]).astype(F32)
        pa, pb, pc, pd = _split(p, MIXER_COLS)
        ya = _hgrn2_mixer(pa, lb_all[l], hgrn_norm_g[l])
        yb = _gla_mixer(pb, gla_gate_w2[l], gla_gate_b[l], gla_norm_g[l])
        v_mix = None if l == 0 else (rwkv_v0[l - 1], rwkv_v1[l - 1], rwkv_v2[l - 1])
        yc, v_first = _rwkv7_mixer(pc, v_first, v_mix, rwkv_mu[l], rwkv_w0[l], rwkv_w2[l],
                                   rwkv_a0[l], rwkv_a2[l], rwkv_g2[l], rwkv_k_k[l], rwkv_k_a[l],
                                   rwkv_r_k[l], rwkv_lnx_g[l], rwkv_lnx_b[l])
        yd = _retnet_mixer(pd, positions, log_gamma)
        mix = jnp.einsum('btc,cd->btd', jnp.concatenate([ya, yb, yc, yd], axis=-1), w_out[l])
        h = _layer_norm(DN_ALPHA * h + mix, ln1_g[l], ln1_b[l])
        if l % 2 == 0:
            i = l // 2
            f = _swiglu(h, ffn_w_gate[i], ffn_w_up[i], ffn_w_down[i])
        else:
            i = l // 2
            f = _moe(h, moe_router[i], moe_w_gate[i], moe_w_up[i], moe_w_down[i])
        h = _layer_norm(DN_ALPHA * h + f, ln2_g[l], ln2_b[l])
    return h.astype(out_dtype)


def setup_inputs(seed=0):
    out = dict(first_inputs(seed))
    for name, value in second_inputs(seed + 1).items():
        if name != "x":
            out[name + "_2"] = value
    return out


def reference(
    x, c, ctx, c_ctx, w_mod, b_mod, norm1_w, norm2_w, w_in, conv_w, conv_b, dt_bias, a_log,
    d_skip, ssd_norm_w, w_ssd_out, w_four_out, w_o, w_router, b_router, w_gate_up, b_gate_up,
    w_down, b_down, final_norm_w, positions_2, w_in_2, w_out_2, ln1_g_2, ln1_b_2, ln2_g_2,
    ln2_b_2, hgrn_lb_logits_2, hgrn_norm_g_2, gla_gate_w2_2, gla_gate_b_2, gla_norm_g_2,
    rwkv_mu_2, rwkv_w0_2, rwkv_w2_2, rwkv_a0_2, rwkv_a2_2, rwkv_g2_2, rwkv_k_k_2, rwkv_k_a_2,
    rwkv_r_k_2, rwkv_lnx_g_2, rwkv_lnx_b_2, rwkv_v0_2, rwkv_v1_2, rwkv_v2_2, ffn_w_gate_2,
    ffn_w_up_2, ffn_w_down_2, moe_router_2, moe_w_gate_2, moe_w_up_2, moe_w_down_2,
):
    x = first_block(
        x, c, ctx, c_ctx, w_mod, b_mod, norm1_w, norm2_w, w_in, conv_w, conv_b, dt_bias, a_log,
        d_skip, ssd_norm_w, w_ssd_out, w_four_out, w_o, w_router, b_router, w_gate_up,
        b_gate_up, w_down, b_down, final_norm_w,
    )
    return second_block(
        x, positions_2, w_in_2, w_out_2, ln1_g_2, ln1_b_2, ln2_g_2, ln2_b_2, hgrn_lb_logits_2,
        hgrn_norm_g_2, gla_gate_w2_2, gla_gate_b_2, gla_norm_g_2, rwkv_mu_2, rwkv_w0_2,
        rwkv_w2_2, rwkv_a0_2, rwkv_a2_2, rwkv_g2_2, rwkv_k_k_2, rwkv_k_a_2, rwkv_r_k_2,
        rwkv_lnx_g_2, rwkv_lnx_b_2, rwkv_v0_2, rwkv_v1_2, rwkv_v2_2, ffn_w_gate_2, ffn_w_up_2,
        ffn_w_down_2, moe_router_2, moe_w_gate_2, moe_w_up_2, moe_w_down_2,
    )


_drawn_inputs = setup_inputs


def setup_inputs(seed=0):
    import zlib

    import numpy as np

    out = dict(_drawn_inputs(seed))
    spreads = {}
    factors = {'ctx': 2.69,
     'c_ctx': 2.869,
     'conv_b': 4.05,
     'ssd_norm_w': 2.67,
     'b_router': 3.187,
     'b_gate_up': 8.0,
     'b_down': 6.454,
     'ln1_g_2': 2.701,
     'ln2_g_2': 3.417,
     'ln2_b_2': 3.505,
     'hgrn_lb_logits_2': 5.695,
     'hgrn_norm_g_2': 22.452,
     'gla_gate_b_2': 7.056,
     'gla_norm_g_2': 23.291,
     'rwkv_w2_2': 7.322,
     'rwkv_a0_2': 6.337,
     'rwkv_k_k_2': 26.453,
     'rwkv_k_a_2': 7.441,
     'rwkv_r_k_2': 5.085,
     'rwkv_lnx_g_2': 22.822,
     'rwkv_lnx_b_2': 31.46,
     'rwkv_v0_2': 8.0,
     'rwkv_v1_2': 3.509,
     'rwkv_v2_2': 3.426}
    for name, (base, spread) in spreads.items():
        noise = np.random.default_rng([zlib.crc32(name.encode()), seed]).standard_normal(out[name].shape)
        drawn = base * np.exp(spread * noise) if base else spread * noise
        out[name] = jnp.asarray(drawn.astype(out[name].dtype))
    for name, factor in factors.items():
        out[name] = (out[name] * factor).astype(out[name].dtype)
    return out
```

```python
import concourse.bass as bass
from concourse import mybir
from contextlib import ExitStack
import numpy as np

F32 = mybir.dt.float32
ALU = mybir.AluOpType
ACT = mybir.ActivationFunctionType

D = 1024
KT = D // 128
N = 256
NHEAD = 32
D_IN = 2048
XB = 3072
OFF_DT, OFF_CF, OFF_Z, OFF_F, OFF_GF, OFF_GS = 3072, 3136, 4160, 6208, 7232, 8256
NEXP, TOPK = 32, 4
FFE = 1408 // 128
ALPHA = 4.0 ** 0.25
GAMMA = [float(np.log(1.0 - 2.0 ** (-5.0 - h))) for h in range(4)]

TILES2 = ([(c, 128) for c in range(0, 1536, 128)] + [(1536, 16), (1552, 128), (1680, 128)]
          + [(1808 + 128 * i, 128) for i in range(8)] + [(2832, 32)] + [(2864 + 128 * i, 128) for i in range(8)])
CHUNKS2 = [(0, 4), (4, 8), (8, 12), (12, 16), (16, 20), (20, 24), (24, 28), (28, 32)]

VECS = [("b_mod", 48), ("c", 8), ("c_ctx", 8), ("norm1_w", 8), ("norm2_w", 8), ("conv_w", 160), ("conv_b", 32),
        ("ssd_norm_w", 16), ("final_norm_w", 8), ("ln1_g_2", 16), ("ln1_b_2", 16), ("ln2_g_2", 16),
        ("ln2_b_2", 16), ("hgrn_lb_logits_2", 4), ("gla_gate_b_2", 2), ("rwkv_w0_2", 4), ("rwkv_a0_2", 4),
        ("rwkv_k_k_2", 4), ("rwkv_k_a_2", 4), ("rwkv_r_k_2", 4), ("rwkv_lnx_g_2", 4), ("rwkv_lnx_b_2", 4),
        ("rwkv_v0_2", 2), ("mu0", 8), ("mu1", 8), ("mus", 2), ("hgrn_norm_g_2", 2), ("gla_norm_g_2", 2),
        ("b_gate_up", 512)]
COL, _at = {}, 0
for _n, _k in VECS:
    COL[_n] = _at
    _at += _k
NTAB = (_at + 127) // 128


def constants():
    i = np.arange(128)
    r, c = i[:, None], i[None, :]
    th = 2 * np.pi * np.outer(np.arange(256), np.arange(256)) / 256
    cs = np.concatenate([np.cos(th), -np.sin(th)], 1) / 16.0
    tf = 2 * np.pi * np.outer(i, i) / 128
    s = 1 / np.sqrt(128.0)
    one = [("ident", r == c), ("TU", r <= c), ("SL", r > c), ("TL", r >= c), ("SU", r < c), ("ones", r >= 0 * c),
           ("head", (r // 64 == c // 64) / 64.0), ("dft", np.concatenate([cs[:128], cs[128:]], 1)),
           ("dfc", np.cos(tf) * s), ("dfs", np.sin(tf) * s)]
    i2 = np.arange(256)
    rel = i2[None, :] - r
    dec = [np.where(rel >= 0, np.exp(np.minimum(np.maximum(rel, 0) * g, 0)), 0) / 8.0 for g in GAMMA]
    same = (r // 64) == (c // 64)
    su, iu = same & (r < c), same & (r <= c)
    lev = [((c // n) % 2 == 1) & (r // n == c // n - 1) for n in (1, 2, 4, 8, 16, 32)]
    z = np.arange(192)[None, :]
    rot = np.zeros((128, 128))
    for m in range(128):
        if m % 64 < 32:
            rot[m + 32, m] = -1
        else:
            rot[m - 32, m] = 1
    inv = (10000.0 ** (-(np.arange(32, dtype=np.float32)) / np.float32(32))).astype(np.float32)
    two = [("ret", np.concatenate(dec, 1)), ("rwm", np.concatenate([su, iu, su, iu], 1)),
           ("lev", np.concatenate(lev, 1)), ("keep", np.broadcast_to(i2[None, :] % 64 != 0, (128, 256))),
           ("zH", z == 64 * (r // 64) + 63), ("zG", z == 64 * ((r % 64) // 32) + 63), ("rot", rot),
           ("inv", np.tile(inv, 4)[:, None]), ("alpha", (r == c) * ALPHA)]
    out = []
    for part in (one, two):
        at, where, cols = 0, {}, []
        for n, v in part:
            v = np.asarray(v, np.float32)
            where[n] = (at, v.shape[1])
            at += v.shape[1]
            cols.append(v)
        out.append((np.ascontiguousarray(np.concatenate(cols, 1)), where))
    return out

def vector_rows(a):
    def rows(ap):
        names = " ".join("abc"[:len(ap.shape)])
        flat = ap.rearrange(f"{names} -> ({names})") if len(ap.shape) > 1 else ap
        return flat.rearrange("(r w) -> r w", w=128)

    out = []

    def add(at, ap, lo=0):
        while ap.shape[0]:
            k = min(ap.shape[0], 128 - at % 128)
            out.append((at, lo, ap[0:k]))
            if k == ap.shape[0]:
                return
            at, ap = at + k, ap[k:]

    for name, k in VECS:
        if name in ("mu0", "mu1"):
            l = int(name[2])
            add(COL[name], rows(a["rwkv_mu_2"][l:l + 1, 0:1024]))
        elif name == "mus":
            add(COL[name], a["rwkv_mu_2"][:, 1024:1056])
        elif name in ("hgrn_norm_g_2", "gla_norm_g_2"):
            add(COL[name], a[name])
            add(COL[name], a[name], 64)
        else:
            add(COL[name], rows(a[name]))
    return out


class Count:
    def __init__(self):
        self.n, self.i, self.per, self.at = 0, None, 0, 0

    def enter(self, i, per):
        self.i, self.per, self.at = i, per, self.n

    def leave(self, times):
        assert self.n - self.at == self.per, (self.n - self.at, self.per)
        self.n = self.at + self.per * times
        self.i = None

    def value(self, n):
        return n if self.i is None else self.i * self.per + n


def build(nc, a, out, where1, where2):
    ctx = ExitStack()
    with ctx:
        def sb(name, shape):
            return ctx.enter_context(nc.sbuf_tensor(name, shape, F32))[tuple(slice(None) for _ in shape)]

        sems = {}

        def S(name):
            if name not in sems:
                sems[name] = ctx.enter_context(nc.semaphore(name))
            return sems[name]

        P = [ctx.enter_context(nc.psum_tensor(f"P{i}", [128, 512], F32)) for i in range(8)]

        WS = sb("WS", [128, 6, 2048])
        xT = sb("xT", [128, KT, N])
        VC = sb("VC", [128, NTAB * 128])
        C1 = sb("C1", [128, a["const1"].shape[1]])
        modT = sb("modT", [128, 48, 2])
        small = sb("small", [128, 1024])
        R = sb("R", [128, 33290])

        def k1(n):
            at, w = where1[n]
            return C1[:, at:at + w]

        def reg(at, *dims):
            v = R[:, at:at + int(np.prod(dims))]
            if len(dims) == 2:
                v = v.rearrange("p (a b) -> p a b", a=dims[0])
            if len(dims) == 3:
                v = v.rearrange("p (a b c) -> p a b c", a=dims[0], b=dims[1])
            return v

        hT = reg(0, KT, 2 * N)
        XT = reg(4096, 4, D_IN)
        BT = reg(12288, 4, 1024)
        Bf = reg(16384, 8, N)
        Cf = reg(18432, 8, N)
        Y = reg(20480, 2, D_IN)
        H = reg(24576, 2, 4, 512)
        SCR = 28672
        craw = reg(SCR, 2, 2, 260)
        cacc = reg(SCR + 1040, 2, 512)
        csil = reg(SCR + 2064, 2, 512)
        xload = reg(12288, 4, D)
        vload = reg(20480, NTAB, 128)
        sq = reg(24576, 2, 512)
        A1 = reg(SCR, 1024)
        EX = reg(SCR + 1024, 1024)
        MT = reg(SCR + 2048, 1024)
        XD = reg(SCR + 3072, 512)
        XW = reg(SCR + 3584, 512)
        YO = reg(SCR + 4096, 512)
        dtt = small[:, 0:256].rearrange("p (c h) -> p c h", c=4)
        dA = small[:, 256:512].rearrange("p (c h) -> p c h", c=4)
        wst = small[:, 512:768].rearrange("p (c h) -> p c h", c=4)
        CBm = small[:, 768:896]
        av = small[:, 896:960]
        dskip = small[:, 960:992]
        ea = sb("ea", [128, 4, 192])
        dtb = sb("dtb", [128, 64])
        n1s = sb("n1s", [128, 2 * KT])
        cs = sb("cs", [128, 2 * KT])
        st = sb("st", [128, 16])
        inv = ea.rearrange("p c h -> p (c h)")[:, 0:512]
        vd = nc.dram_tensor("value_rows", [2, 4, 128, N], F32, kind="Internal").ap()
        zs = reg(SCR, 2, 512)
        junk = reg(SCR + 1024, 2048)
        YT = reg(4096, 16, N)
        GT = reg(8192, KT, N)
        MX = reg(10240, KT, N)
        U = reg(12288, 2, D)
        V_ = reg(14336, 8, 512)
        UT = reg(18432, 8, N)
        SPB = 2048 + 32 * N + 2048 + a["const2"].shape[1]
        B0 = SPB
        h2 = reg(0, KT, N)
        sqb = reg(0, KT, N)
        wB = reg(2048, NEXP, N)
        wBe = reg(B0, N)
        bge = reg(B0 + 256, 16)
        act = reg(B0 + 272, FFE, N)
        gl = reg(B0 + 3088, 2, N)
        ul = reg(B0 + 3600, 2, N)
        sg = reg(B0 + 4112, 2, N)
        wtok = reg(B0 + 4624, 2, 32)
        rt = reg(B0 + 4688, 12, 32)
        wr = reg(B0 + 5072, KT, 32)
        wTt = reg(B0 + 5328, N)
        bdn = reg(B0 + 5584, D)
        rb = reg(B0 + 6608, 32)
        xc = reg(B0 + 6640, KT, N)
        sc1 = reg(B0 + 8688, 8, N)
        PT = reg(2048, 32, N)
        mixT = reg(10240, KT, N)
        C2 = reg(12288, a["const2"].shape[1])

        def k2(n):
            at, w = where2[n]
            return C2[:, at:at + w]

        fT = reg(B0, 3, N)
        kT = reg(B0 + 768, 3, N)
        qT = reg(B0 + 1536, 3, N)
        f4 = reg(B0 + 2304, 1024)
        vb = reg(B0 + 3328, 2, 4, N)
        kv = reg(B0 + 5376, 2, 4, N)
        St = reg(B0 + 7424, 2, 4, N)
        qS = reg(B0 + 9472, 2, 4, N)
        g1t = reg(B0 + 11520, 4, N)
        g2t = reg(B0 + 12544, 4, N)
        r2 = reg(B0, 2, N)
        kp = reg(B0 + 512, 2, N)
        vv = reg(B0 + 1024, 2, N)
        AR = reg(B0 + 1536, 2, 2, N)
        Bt = reg(B0 + 2560, 2, N)
        Kt = reg(B0 + 3072, 2, N)
        cl = reg(B0 + 3584, 2, N)
        ga = reg(B0 + 4096, 2, N)
        tm = reg(B0 + 4608, 2, N)
        tn = reg(B0 + 5120, 2, N)
        LM = reg(B0 + 5632, 8, 512)
        TI = reg(B0 + 9728, 8, 128)
        TT = reg(B0 + 10752, 8, 128)
        XI = reg(B0 + 11776, 8, 128)
        YI = reg(B0 + 12800, 8, 128)
        tok = reg(B0 + 13824, 3, 2, N)
        Wt = reg(B0 + 15360, N)
        Ut = reg(B0 + 15616, N)
        Sr = reg(B0 + 15872, 2, 64)
        oT = reg(B0 + 16000, 2, N)
        cosT = reg(B0, N)
        sinT = reg(B0 + 256, N)
        ang = reg(B0 + 512, 3, N)
        qk = reg(B0 + 1280, 4, N)
        rsw = reg(B0 + 2304, 4, N)
        vtk = reg(B0 + 3328, 2, N)
        sc = reg(B0 + 3840, 4, 384)
        ro = reg(B0 + 5376, 2, N)
        rc = reg(B0 + 5888, 2, N)
        rq = reg(B0 + 6400, 2, N)
        res = reg(2048, 2, D)
        kkr = reg(B0 + 9728, 2, N)
        kks = reg(B0 + 10752, 2, N)
        t3 = reg(B0 + 11776, 2, N)
        t4 = reg(B0 + 12800, 2, N)
        vfk = reg(B0 + 16512, 2, N)
        w2s = reg(B0 + 17024, N)
        g2a = reg(B0 + 17280, N)
        g2b = reg(B0 + 17536, N)
        hg = kv.rearrange("p a b c -> p (a b) c")[:, 0:4, :]
        hr4 = St.rearrange("p a b c -> p (a b) c")[:, 0:4, :]
        v1s = small[:, 0:64].rearrange("p (t r) -> p t r", t=2)
        v2s = small[:, 64:320]
        gw2 = small[:, 320:448]
        posi = small[:, 704:960].bitcast(mybir.dt.int32)
        lbc = small[:, 960:964]
        LAYW = [16 * 5, 16 * 12]
        ROUTW = [16 * 3, 16 * 5]

        def col(name, i=0, n=1):
            return VC[:, COL[name] + i:COL[name] + i + n]

        def w4(ap, r0, r1, c0, c1):
            return ap[r0:r1, c0:c1].rearrange("(k p) c -> p k c", p=128)

        def proj(ap, c0, w):
            return [(w4(ap, 0, 512, c0, c0 + w), 4, w), (w4(ap, 512, 1024, c0, c0 + w), 4, w)]

        def down(ap, kt, n):
            out = [(w4(ap, 128 * kt, 128 * (kt + min(2, n)), 0, D), min(2, n), D)]
            if n > 2:
                out.append((w4(ap, 128 * (kt + 2), 128 * (kt + n), 0, D), n - 2, D))
            return out

        w_in = a["w_in"][0]
        units1 = ([proj(a["w_mod"][0], 512 * i, 512) for i in range(12)]
                  + [proj(w_in, 512 * i, 512) for i in range(6)]
                  + [proj(w_in, OFF_CF + 512 * i, 512) for i in range(2)]
                  + [proj(w_in, OFF_DT, 64)]
                  + [proj(w_in, OFF_Z + 512 * i, 512) for i in range(4)]
                  + [down(a["w_ssd_out"][0], 4 * i, 4) for i in range(4)]
                  + [proj(w_in, OFF_GS + 512 * i, 512) for i in range(2)]
                  + [proj(w_in, OFF_F + 512 * i, 512) for i in range(2)]
                  + [proj(w_in, OFF_GF + 512 * i, 512) for i in range(2)]
                  + [proj(a["w_four_out"][0], 512 * i, 512) for i in range(2)]
                  + [proj(a["w_o"][0], 512 * i, 512) for i in range(2)])

        def chunk2(l, c):
            t0, t1 = CHUNKS2[c]
            return TILES2[t0][0], TILES2[t1 - 1][0] + TILES2[t1 - 1][1] - TILES2[t0][0]

        def units2(l):
            return ([proj(a["w_in_2"][l], *chunk2(l, c)) for c in range(8)]
                    + [proj(a["w_out_2"][l], 512 * i, 512) for i in range(2)])

        jobs = [("tab", (NTAB + 3) // 4), ("xin", 8), ("ss1", 1), ("xb", 32), ("dt", 1), ("seg", 4), ("z", 8),
                ("ytr", 8), ("gs", 8), ("u", 4), ("ff1", 8), ("ff2", 4), ("gf", 8), ("four", 8), ("wo", 8),
                ("ss2", 1), ("rt0", 2), ("wT0", 1), ("wB0", 16), ("ss3", 1)]
        for l in range(2):
            jobs += [(f"p{l}", 32), (f"gate{l}", 1), (f"hn{l}", 4), (f"lr{l}", 6), (f"vmA{l}", l), (f"vmB{l}", 2 * l),
                     (f"kkn{l}", 2), (f"tk{l}", 3), (f"lm{l}", 8), (f"gnA{l}", 2), (f"gnB{l}", 2), (f"rkv{l}", 2),
                     (f"rot{l}", 4), (f"rv{l}", 1), (f"rs{l}", 8), (f"ro{l}", 4), (f"rnA{l}", 2), (f"rnB{l}", 2),
                     (f"out{l}", 8), (f"laA{l}", 1), (f"laB{l}", 1)]
            if l:
                jobs += [("rt1", 2), ("wT1", 1), ("wB1", 4)]
            jobs += [(f"lbA{l}", 1), (f"lbB{l}", 1)]
        jobs += [("fin", 8)]
        START, at = {}, 0
        for name, k in jobs:
            START[name] = at
            at += k

        def expert_halves(which, e):
            if which == "a":
                gu, dn = a["w_gate_up"][0], a["w_down"][0]
                g, d = gu[bass.ds(e, 1)].rearrange("a b c -> (a b) c"), dn[bass.ds(e, 1)].rearrange("a b c -> (a b) c")
                us = []
                for i in range(2):
                    us += [proj(g, 512 * i, 512), proj(g, D + 512 * i, 512)]
                return us + [down(d, 4 * i, 4) for i in range(2)]
            if which == "d":
                off = 1408
                g, u, dn = a["ffn_w_gate_2"][0], a["ffn_w_up_2"][0], a["ffn_w_down_2"][0]
                us = []
                for c0, w in ((0, 512), (512, 512), (1024, 384)):
                    us += [proj(g[:, off * e:off * (e + 1)], c0, w), proj(u[:, off * e:off * (e + 1)], c0, w)]
                return us + [down(dn[off * e:off * (e + 1), :], k, n) for k, n in ((0, 4), (4, 4), (8, 3))]
            g, u, dn = (a[k][0][bass.ds(e, 1)].rearrange("a b c -> (a b) c")
                        for k in ("moe_w_gate_2", "moe_w_up_2", "moe_w_down_2"))
            us = []
            for c0, w in ((0, 512), (512, 512), (1024, 384)):
                us += [proj(g, c0, w), proj(u, c0, w)]
            return us + [down(dn, k, n) for k, n in ((0, 4), (4, 4), (8, 3))]

        SPEC = {"a": (NEXP, 8), "d": (2, FFE), "m": (8, FFE)}

        SSD = [(d, step, ((0, 1, 2, 3), (1, 0, 3, 2))[d][step], g) for d in range(2) for step in range(4) for g in range(4)]
        LEVELS = 6

        block = ctx.enter_context(nc.Block())

        def turns(eng, which, counts):
            count = SPEC[which][0]
            if which == "d":
                yield from range(count)
                return
            with eng.Fori(0, count) as e:
                for c, per in counts:
                    c.enter(e, per)
                yield e
            for c, _ in counts:
                c.leave(count)

        @block.sync
        def _(sp):
            cu = Count()

            def load(unit):
                slot = cu.n % 3
                if cu.n >= 3:
                    sp.wait_ge(S("unit_used"), cu.value(cu.n - 2))
                for h, (src, k, w) in enumerate(unit):
                    dst = WS[:, 2 * slot + h, 0:k * w].rearrange("p (k c) -> p k c", k=k)
                    sp.dma_start(dst, src).then_inc(S(f"w_loaded{slot}"), 16)
                cu.n += 1

            def experts(which):
                for e in turns(sp, which, [(cu, 6 if which == "a" else 9)]):
                    for u in expert_halves(which, e):
                        load(u)

            for u in units1:
                load(u)
            experts("a")
            for l in range(2):
                for u in units2(l):
                    load(u)
                experts("m" if l else "d")
            sp.wait_ge(S("mm_free"), at)
            sp.dma_start(out.rearrange("a (c p) d -> p (a c) d", p=128), res).then_inc(S("out_written"), 16)
            sp.wait_ge(S("out_written"), 16)

        @block.tensor
        def _(pe):
            cu, tick, ffc = Count(), Count(), Count()
            ident = k1("ident")

            def mm(out, lhsT, rhs, start=True, stop=True):
                return nc.tensor.matmul(out, lhsT, rhs, start=start, stop=stop, skip_group_check=True)

            def turn(out, in_):
                return nc.tensor.transpose(out, in_, ident[0:in_.shape[0], 0:in_.shape[0]])

            def unit():
                n = cu.n
                cu.n += 1
                extra = 0 if cu.i is None else cu.i * (cu.per // 3 * 32)
                pe.wait_ge(S(f"w_loaded{n % 3}"), extra + 32 * (n // 3 + 1))
                return n

            def wproj(n, w, k, c0, c1):
                return WS[:, 2 * (n % 3) + k // 4, (k % 4) * w + c0:(k % 4) * w + c1]

            def wdown(n, k, m):
                return WS[:, 2 * (n % 3) + k // 2, (k % 2) * D + 128 * m:(k % 2) * D + 128 * m + 128]

            def job(stage, i):
                n = START[stage] + i
                assert n == tick.n, (stage, i, n, tick.n)
                tick.n += 1
                if i == 0 and n:
                    pe.wait_ge(S("mm_free"), n)
                elif n >= 4:
                    pe.wait_ge(S("mm_free"), n - 3)
                return P[n % 4]

            fences = [0]

            def fence(last):
                fences[0] += 1
                last.then_inc(S("pe_step"), 1)
                pe.wait_ge(S("pe_step"), fences[0])

            def done(last):
                last.then_inc(S("mm_done"), 1)

            def unit_used():
                pe.wait_ge(S("mm_done"), tick.n)
                pe.sem_inc(S("unit_used"), 1)

            def empty_all():
                pe.wait_ge(S("mm_free"), tick.n)

            def columns(out, n, w, c0, c1, rhs):
                for k in range(KT):
                    last = mm(out, wproj(n, w, k, c0, c1), rhs(k), k == 0, k == KT - 1)
                return last

            def acc(m):
                return P[4 + m // 2][:, 256 * (m % 2):256 * (m % 2) + 256]

            def eight(stage, rhs):
                for u in range(2):
                    n = unit()
                    for j in range(4):
                        b = job(stage, 4 * u + j)
                        done(columns(b[:, 0:N], n, 512, 128 * j, 128 * j + 128, rhs))
                    unit_used()

            def total(stage, i, lhsT, srcs):
                b = job(stage, i)
                for k, s in enumerate(srcs):
                    last = mm(b[:, 0:N], lhsT, s, k == 0, k == len(srcs) - 1)
                done(last)

            pe.wait_ge(S("consts"), 16)
            pe.wait_ge(S("vecs"), 16 * len(a["vec_dmas"]))
            for i in range((NTAB + 3) // 4):
                b = job("tab", i)
                for t in range(4 * i, min(NTAB, 4 * i + 4)):
                    last = turn(b[:, 128 * (t % 4):128 * (t % 4) + 128], vload[:, t, :])
                done(last)
            pe.wait_ge(S("xin"), 32)
            for i in range(8):
                b = job("xin", i)
                which, t = i // 4, 2 * (i % 4)
                for tt in range(2):
                    for c in range(2):
                        last = turn(b[:, 256 * tt + 128 * c:256 * tt + 128 * c + 128],
                                    xload[:, 2 * which + c, 128 * (t + tt):128 * (t + tt) + 128])
                done(last)
            b = job("ss1", 0)
            pe.wait_ge(S("sq1"), 2)
            for k in range(KT):
                last = mm(b[:, :], k1("ones"), hT[:, k, :], k == 0, k == KT - 1)
            done(last)
            pe.wait_ge(S("cs_ready"), 1)
            for u in range(12):
                n = unit()
                for j in range(4):
                    m = 4 * u + j
                    last = columns(P[4][:, 2 * m:2 * m + 2], n, 512, 128 * j, 128 * j + 128, lambda k: cs[:, 2 * k:2 * k + 2])
                last.then_inc(S("unit_used"), 1)
            pe.wait_ge(S("h_ready"), 1)

            def turn_tile(j):
                pe.wait_ge(S("conv_out"), j + 1)
                if j >= 2:
                    pe.wait_ge(S("turn_free"), j - 1)
                for c in range(4):
                    last = turn(P[4 + j % 2][:, 128 * c:128 * c + 128], csil[:, j % 2, 128 * c:128 * c + 128])
                last.then_inc(S("turned"), 1)

            for j in range(32):
                if j % 4 == 0:
                    n = unit()
                b = job("xb", j)
                if j < 24:
                    last = columns(b[:, :], n, 512, 128 * (j % 4), 128 * (j % 4) + 128, lambda k: hT[:, k, :])
                else:
                    last = columns(b[:, 0:N], n, 512, 128 * (j % 4), 128 * (j % 4) + 128, lambda k: hT[:, k, N:2 * N])
                done(last)
                if j % 4 == 3:
                    unit_used()
                if 2 <= j < 26:
                    turn_tile(j - 2)
            n = unit()
            b = job("dt", 0)
            for c in range(4):
                for k in range(KT):
                    last = mm(b[:, 64 * c:64 * c + 64], hT[:, k, 128 * c:128 * c + 128], wproj(n, 64, k, 0, 64),
                              k == 0, k == KT - 1)
            done(last)
            unit_used()
            pe.wait_ge(S("dA_ready"), 1)
            for c in range(4):
                b = job("seg", c)
                for q, (f, r) in enumerate((("TU", "TL"), ("SL", "SU"), ("ones", "ones"))):
                    mm(b[:, 64 * q:64 * q + 32], k1(f), dA[:, c, 0:32])
                    last = mm(b[:, 64 * q + 32:64 * q + 64], k1(r), dA[:, c, 32:64])
                done(last)
            empty_all()
            nx = ns = 0
            for d, step, c, g in SSD:
                if step >= 2:
                    tk = slice(128 * (c - 2), 128 * (c - 2) + 128)
                    pe.wait_ge(S("A1_ready"), nx + 1)
                    if nx:
                        pe.wait_ge(S("CB_ready"), nx)
                        pe.wait_ge(S("EX_ready"), nx)
                    mm(P[4][:, 0:128], Bf[:, 4 * d + g, tk], Cf[:, 4 * d + g, tk])
                    for h in range(8):
                        last = mm(P[5 + h // 4][:, 128 * (h % 4):128 * (h % 4) + 128], A1[:, 128 * h:128 * h + 128],
                                  k1("TL" if d else "TU"))
                    last.then_inc(S("seg_done"), 1)
                    pe.wait_ge(S("H_ready"), 12 * d + 4 * (step - 1) + g + 1)
                    if nx:
                        pe.wait_ge(S("yo_used"), nx)
                    mm(P[0][:, :], Cf[:, 4 * d + g, tk], H[:, d, g, :]).then_inc(S("yo_done"), 1)
                if step < 3:
                    pe.wait_ge(S("XW_ready"), ns + 1)
                    if ns:
                        pe.wait_ge(S("H_ready"), ns)
                    mm(P[1][:, :], BT[:, c, 512 * d + 128 * g:512 * d + 128 * g + 128], XW).then_inc(S("st_done"), 1)
                    ns += 1
                if step >= 2:
                    pe.wait_ge(S("XD_ready"), nx + 1)
                    pe.wait_ge(S("MT_ready"), nx + 1)
                    if nx:
                        pe.wait_ge(S("dg_used"), nx)
                    for h in range(8):
                        last = mm(P[7][:, 64 * h:64 * h + 64], MT[:, 128 * h:128 * h + 128], XD[:, 64 * h:64 * h + 64])
                    last.then_inc(S("dg_done"), 1)
                    nx += 1

            def tokens_wide(stage, units):
                for u in range(units):
                    n = unit()
                    for c in range(2):
                        b = job(stage, 2 * u + c)
                        for k in range(KT):
                            last = mm(b[:, :], hT[:, k, N + 128 * c:N + 128 * c + 128], wproj(n, 512, k, 0, 512),
                                      k == 0, k == KT - 1)
                        done(last)
                    unit_used()

            pe.wait_ge(S("dg_used"), nx)
            tokens_wide("z", 4)
            pe.wait_ge(S("yn_ready"), 1)
            for i in range(8):
                b = job("ytr", i)
                for tt in range(2):
                    for c in range(2):
                        last = turn(b[:, 256 * tt + 128 * c:256 * tt + 128 * c + 128],
                                    Y[:, c, 256 * i + 128 * tt:256 * i + 128 * tt + 128])
                done(last)
            empty_all()
            for u in range(4):
                n = unit()
                for k in range(4):
                    for m in range(8):
                        last = mm(acc(m), wdown(n, k, m), YT[:, 4 * u + k, :],
                                  u == 0 and k == 0 and m % 2 == 0, u == 3 and k == 3)
                last.then_inc(S("unit_used"), 1)
            pe.wait_ge(S("unit_used"), cu.n)
            pe.sem_inc(S("acc_done"), 1)
            eight("gs", lambda k: hT[:, k, N:2 * N])
            tokens_wide("u", 2)
            empty_all()
            for f in range(8):
                b = job("ff1", f)
                for c in range(2):
                    last = mm(b[:, :], U[:, c, 128 * f:128 * f + 128], k1("dft")[:, 512 * c:512 * c + 512], c == 0, c == 1)
                done(last)
            empty_all()
            for i in range(4):
                b = job("ff2", i)
                for q in range(2):
                    mm(b[:, 256 * q:256 * q + 256], k1("dfc"), V_[:, 2 * i + q, 0:256], True, False)
                    last = mm(b[:, 256 * q:256 * q + 256], k1("dfs"), V_[:, 2 * i + q, 256:512], False, True)
                done(last)
            eight("gf", lambda k: hT[:, k, N:2 * N])
            eight("four", lambda k: UT[:, k, :])
            pe.wait_ge(S("mx_ready"), 1)
            eight("wo", lambda k: MX[:, k, :])
            pe.wait_ge(S("squares"), 1)
            total("ss2", 0, k1("ones"), [sc1[:, k, :] for k in range(KT)])

            def router(i, ne, src):
                pe.wait_ge(S("router"), ROUTW[i])
                for c in range(2):
                    b = job(f"rt{i}", c)
                    for k in range(KT):
                        last = mm(b[:, 0:ne], src(k)[:, 128 * c:128 * c + 128], wr[:, k, 0:ne], k == 0, k == KT - 1)
                    done(last)
                pe.wait_ge(S("w_ready"), i + 1)
                b = job(f"wT{i}", 0)
                for c in range(2):
                    last = turn(b[0:ne, 128 * c:128 * c + 128], wtok[:, c, 0:ne])
                done(last)
                for q in range(ne // 2):
                    b = job(f"wB{i}", q)
                    for j in range(2):
                        e = 2 * q + j
                        last = mm(b[:, 256 * j:256 * j + 256], ident[0:ne, e:e + 1].to_broadcast([ne, 128]), wTt[0:ne, :])
                    done(last)

            def open_sum(lhsT, rhs):
                for m in range(8):
                    mm(acc(m), lhsT(m), rhs(m), m % 2 == 0, False)

            def experts(which, rhs):
                nf = SPEC[which][1]
                empty_all()
                base = ffc.n
                for e in turns(pe, which, [(cu, 6 if which == "a" else 9), (ffc, nf)]):
                    first = ffc.n
                    for u in range((nf + 3) // 4):
                        gn, un = unit(), unit()
                        w = min(512, 128 * nf - 512 * u)
                        for j in range(4 * u, min(4 * u + 4, nf)):
                            pe.wait_ge(S("ff_free"), ffc.value(1 + (first + j - 3 if j >= 4 else first)))
                            columns(P[j % 4][:, 0:N], gn, w, 128 * (j % 4), 128 * (j % 4) + 128, rhs)
                            columns(P[j % 4][:, N:2 * N], un, w, 128 * (j % 4), 128 * (j % 4) + 128, rhs)\
                                .then_inc(S("ff_done"), 1)
                            ffc.n += 1
                        pe.wait_ge(S("ff_done"), ffc.value(ffc.n))
                        pe.sem_inc(S("unit_used"), 2)
                    for u in range((nf + 3) // 4):
                        n = unit()
                        for k in range(min(4, nf - 4 * u)):
                            pe.wait_ge(S("act_ready"), ffc.value(2 + first + 4 * u + k + 1))
                            for m in range(8):
                                last = mm(acc(m), wdown(n, k, m), act[:, 4 * u + k, :], False, False)
                        last.then_inc(S("unit_used"), 1)
                pe.wait_ge(S("unit_used"), cu.n)
                pe.sem_inc(S("acc_done"), 1)

            pe.wait_ge(S("h2_ready"), KT)
            router(0, NEXP, lambda k: h2[:, k, :])
            open_sum(lambda m: bdn[0:NEXP, 128 * m:128 * m + 128], lambda m: wTt[0:NEXP, :])
            experts("a", lambda k: h2[:, k, :])
            pe.wait_ge(S("squares"), 2)
            total("ss3", 0, k1("ones"), [sqb[:, k, :] for k in range(KT)])

            for l in range(2):
                xk = lambda k: xT[:, k, :]
                pe.wait_ge(S("x_ready"), 2 * l + 1)
                for c in range(8):
                    n = unit()
                    c0, w = chunk2(l, c)
                    for i in range(*CHUNKS2[c]):
                        t0, tw = TILES2[i]
                        b = job(f"p{l}", i)
                        done(columns(b[0:tw, 0:N], n, w, t0 - c0, t0 - c0 + tw, xk))
                    unit_used()
                if not l:
                    pe.wait_ge(S("consts2"), 16)
                empty_all()
                pe.wait_ge(S("lay"), LAYW[l])
                b = job(f"gate{l}", 0)
                done(mm(b[:, 0:N], gw2[0:16, :], PT[0:16, 12, :]))
                for n in range(48):
                    u, v0 = n // 16, 4 * (n % 16)
                    pe.wait_ge(S("qS_ready"), 48 * l + n + 1)
                    for j in range(4):
                        v = v0 + j
                        if u < 2:
                            last = mm(P[4][:, 256 * u:256 * u + 256], k2("zH")[:, 63 - v:191 - v], qS[:, n % 2, j, :],
                                      v == 0, v == 63)
                        else:
                            for q in range(2):
                                last = mm(P[5 + q][:, 0:N], k2("zG")[64 * q:64 * q + 64, 63 - v:191 - v],
                                          qS[64 * q:64 * q + 64, n % 2, j, :], v == 0, v == 63)
                    last.then_inc(S("qS_used"), 1)
                pe.wait_ge(S("hsq"), l + 1)
                for i in range(4):
                    total(f"hn{l}", i, k1("head"), [g1t[:, i, :]])
                pe.wait_ge(S("tanh_ready"), l + 1)
                for i in range(6):
                    b = job(f"lr{l}", i)
                    t = i % 2
                    cc = slice(128 * t, 128 * t + 128)
                    if i < 2:
                        last = mm(b[:, 0:N], w2s[0:64, cc], PT[0:64, 21, :])
                    elif i < 4:
                        last = mm(b[:, 0:N], w2s[64:128, cc], PT[64:128, 21, :])
                    else:
                        mm(b[:, 0:N], g2a[:, cc], PT[:, 22, :], True, False)
                        last = mm(b[:, 0:N], g2b[0:32, cc], PT[0:32, 23, :], False, True)
                    done(last)
                if l:
                    b = job("vmA1", 0)
                    for t in range(2):
                        last = mm(b[0:32, 0:N], v1s[:, t, :], PT[:, 19 + t, :], t == 0, t == 1)
                    done(last)
                    empty_all()
                    for t in range(2):
                        b = job("vmB1", t)
                        done(mm(b[:, 0:N], v2s[0:32, 128 * t:128 * t + 128], tn[0:32, 0, :]))
                pe.wait_ge(S("kk_sq"), l + 1)
                for t in range(2):
                    total(f"kkn{l}", t, k1("head"), [kks[:, t, :]])
                pe.wait_ge(S("abk_ready"), l + 1)
                for i, src in enumerate((Bt, Kt, vv)):
                    b = job(f"tk{l}", i)
                    for c in range(2):
                        for t in range(2):
                            last = turn(b[:, 256 * c + 128 * t:256 * c + 128 * t + 128], src[:, t, 128 * c:128 * c + 128])
                    done(last)
                for i in range(8):
                    b = job(f"lm{l}", i)
                    h, q = i // 2, i % 2
                    hp, t, tk = slice(64 * (h % 2), 64 * (h % 2) + 64), h // 2, slice(128 * q, 128 * q + 128)
                    for w, src in enumerate((Bt, Kt)):
                        for z in range(2):
                            last = mm(b[:, 256 * w + 128 * z:256 * w + 128 * z + 128], src[hp, t, tk], AR[hp, t, z, tk])
                    done(last)
                for lev in range(LEVELS):
                    v = LEVELS * l + lev
                    pe.wait_ge(S("inv_x"), v + 1)
                    for i in range(8):
                        last = mm(P[4 + i // 4][:, 128 * (i % 4):128 * (i % 4) + 128], XI[:, i, :], TI[:, i, :])
                    last.then_inc(S("inv_y"), 1)
                    pe.wait_ge(S("inv_yc"), v + 1)
                    for i in range(8):
                        mm(P[4 + i // 4][:, 128 * (i % 4):128 * (i % 4) + 128], TT[:, i, :], YI[:, i, :])
                        last = mm(P[6 + i // 4][:, 128 * (i % 4):128 * (i % 4) + 128], YI[:, i, :], TT[:, i, :])
                    last.then_inc(S("inv_t"), 1)
                pe.wait_ge(S("inv_end"), l + 1)
                for c in range(4):
                    q, o = c // 2, slice(64 * (c % 2), 64 * (c % 2) + 64)
                    tk, n = slice(64 * c, 64 * c + 64), 4 * l + c
                    pe.wait_ge(S("S_ready"), 5 * l + c + 1)
                    fresh = True
                    for r in range(2):
                        for h in range(4):
                            hp, t, hv = slice(64 * (h % 2), 64 * (h % 2) + 64), h // 2, slice(64 * h, 64 * h + 64)
                            two = [(h % 2, AR[hp, t, 0, tk], Sr[hp, t, :]),
                                   (c % 2, LM[o, 2 * h + q, 256 + 64 * (c % 2):256 + 64 * (c % 2) + 64], tok[o, 2, q, hv])]
                            two = sorted(two, key=lambda x: x[0])
                            for z, (row, lhsT, rhs) in enumerate(two):
                                if row == r:
                                    last = mm(P[4][o, hv], lhsT, rhs, fresh, z == 1)
                                    fresh = False
                        if not r:
                            fence(last)
                    last.then_inc(S("W_done"), 1)
                    pe.wait_ge(S("W_ready"), n + 1)
                    for h in range(4):
                        hv = slice(64 * h, 64 * h + 64)
                        last = mm(P[5][o, hv], TT[o, 2 * h + q, o], Wt[o, hv])
                    last.then_inc(S("U_done"), 1)
                    pe.wait_ge(S("U_ready"), n + 1)
                    fresh = {0, 1}
                    for r in range(2):
                        for h in range(4):
                            hp, t, hv = slice(64 * (h % 2), 64 * (h % 2) + 64), h // 2, slice(64 * h, 64 * h + 64)
                            lo = 64 * (c % 2)
                            three = [(h % 2, Sr[hp, t, :], AR[hp, t, 1, tk]),
                                     (c % 2, Ut[o, hv], LM[o, 2 * h + q, 128 + lo:192 + lo]),
                                     (c % 2, tok[o, 2, q, hv], LM[o, 2 * h + q, 384 + lo:448 + lo])]
                            three = sorted(three, key=lambda x: x[0])
                            for z, (row, lhsT, rhs) in enumerate(three):
                                if row == r:
                                    last = mm(P[6][hp, 256 * t + 64 * c:256 * t + 64 * c + 64], lhsT, rhs,
                                              h % 2 in fresh, z == 2)
                                    fresh -= {h % 2}
                            if c % 2 == r:
                                mm(P[7][hp, 64 * t:64 * t + 64], tok[o, 0, q, hv], Ut[o, hv], t == 0, False)
                                last = mm(P[7][hp, 64 * t:64 * t + 64], tok[o, 1, q, hv], tok[o, 2, q, hv], False, True)
                        if not r:
                            fence(last)
                    last.then_inc(S("SO_done"), 1)
                pe.wait_ge(S("o_ready"), l + 1)
                for t in range(2):
                    total(f"gnA{l}", t, k1("head"), [oT[:, t, :]])
                pe.wait_ge(S("o_sq"), l + 1)
                for t in range(2):
                    total(f"gnB{l}", t, k1("head"), [tm[:, t, :]])
                pe.wait_ge(S("rkr_ready"), l + 1)
                for t in range(2):
                    total(f"rkv{l}", t, k1("head"), [tn[:, t, :]])
                for i in range(4):
                    total(f"rot{l}", i, k2("rot"), [PT[:, 24 + i, :]])
                b = job(f"rv{l}", 0)
                for c in range(2):
                    for t in range(2):
                        last = turn(b[:, 256 * c + 128 * t:256 * c + 128 * t + 128], PT[:, 28 + t, 128 * c:128 * c + 128])
                done(last)
                pe.wait_ge(S("qk_ready"), l + 1)
                for i in range(8):
                    h, q = i // 2, i % 2
                    hp, t = slice(64 * (h % 2), 64 * (h % 2) + 64), h // 2
                    b = job(f"rs{l}", i)
                    done(mm(b[:, 0:256 - 128 * q], qk[hp, 2 + t, 128 * q:128 * q + 128], qk[hp, t, 128 * q:256]))
                empty_all()
                for h in range(4):
                    hp, hv = slice(64 * (h % 2), 64 * (h % 2) + 64), slice(64 * h, 64 * h + 64)
                    b = job(f"ro{l}", h)
                    mm(b[hp, 0:256], vtk[:, 0, hv], sc[:, h, 0:256], True, False)
                    done(mm(b[hp, 128:256], vtk[:, 1, hv], sc[:, h, 256:384], False, True))
                empty_all()
                for t in range(2):
                    total(f"rnA{l}", t, k1("head"), [ro[:, t, :]])
                pe.wait_ge(S("rc_sq"), l + 1)
                for t in range(2):
                    total(f"rnB{l}", t, k1("head"), [rq[:, t, :]])
                pe.wait_ge(S("mix_ready"), l + 1)
                eight(f"out{l}", lambda k: mixT[:, k, :])
                empty_all()
                total(f"laA{l}", 0, k1("ones"), [xT[:, k, :] for k in range(KT)])
                pe.wait_ge(S("squares"), 3 + 2 * l)
                total(f"laB{l}", 0, k1("ones"), [sqb[:, k, :] for k in range(KT)])
                pe.wait_ge(S("x_ready"), 2 * l + 2)
                if l:
                    router(1, 8, xk)
                empty_all()
                open_sum(lambda m: k2("alpha"), lambda m: xT[:, m, :])
                experts("m" if l else "d", xk)
                pe.wait_ge(S("r_ready"), l + 1)
                total(f"lbA{l}", 0, k1("ones"), [xT[:, k, :] for k in range(KT)])
                pe.wait_ge(S("squares"), 4 + 2 * l)
                total(f"lbB{l}", 0, k1("ones"), [sqb[:, k, :] for k in range(KT)])
            pe.wait_ge(S("x_ready"), 5)
            for i in range(8):
                b = job("fin", i)
                for t in range(2):
                    last = turn(b[:, 128 * t:128 * t + 128], xT[:, 2 * (i % 4) + t, 128 * (i // 4):128 * (i // 4) + 128])
                done(last)

        def marker(eng):
            counts = {}

            def mark(ins, name):
                c = counts.setdefault(name, Count())
                c.n += 1
                ins.then_inc(S(name), 1)
                eng.wait_ge(S(name), c.value(c.n))
            return mark, counts

        @block.vector
        def _(dve):
            mark, counts = marker(dve)
            v = nc.vector
            roots = [0]

            def V(ins):
                mark(ins, "dve")

            def F(n, ins):
                ins.then_inc(S("mm_free"), 1)
                dve.wait_ge(S("mm_free"), n + 1)

            def ready(stage, i=0):
                n = START[stage] + i
                dve.wait_ge(S("mm_done"), n + 1)
                return n, P[n % 4]

            def tt(out, a_, b_, op=ALU.mult):
                return v.tensor_tensor(out=out, in0=a_, in1=b_, op=op)

            def ts(out, in_, s1, s2, op0=ALU.mult, op1=ALU.add):
                return v.tensor_scalar(out, in_, s1, s2, op0, op1)

            def stt(out, in0, s, in1, op0=ALU.mult, op1=ALU.mult):
                return v.scalar_tensor_tensor(out=out, in0=in0, scalar=s, in1=in1, op0=op0, op1=op1)

            def flat(x):
                return x.rearrange("p a b -> p (a b)")

            def rsqrt(x):
                roots[0] += 1
                mark(v.memset(st[:, 15:16], 0.0), "to_root")
                dve.wait_ge(S("rooted"), roots[0])
                V(v.reciprocal(x, x))

            def over(k, x):
                return x.unsqueeze(1).to_broadcast([128, k, x.shape[1]])

            v.memset(vload, 0.0).then_inc(S("vload_zero"), 1)
            mark(v.memset(st, 0.0), "ff_free")
            for i in range((NTAB + 3) // 4):
                n, b = ready("tab", i)
                w = 128 * min(4, NTAB - 4 * i)
                F(n, v.tensor_copy(VC[:, 512 * i:512 * i + w], b[:, 0:w]))
            cs3 = cs.rearrange("p (k w) -> p k w", w=2)
            dve.wait_ge(S("sil"), 2)
            V(tt(cs3[:, :, 0], cs3[:, :, 0], col("c", 0, 8)))
            mark(tt(cs3[:, :, 1], cs3[:, :, 1], col("c_ctx", 0, 8)), "cs_ready")
            cT = reg(16384, KT, N)
            for i in range(8):
                n, b = ready("xin", i)
                t = 2 * (i % 4)
                dst = (cT, xT)[i // 4]
                F(n, v.tensor_copy(dst[:, t:t + 2, :], b[:, :].rearrange("p (t n) -> p t n", t=2)))
            mark(tt(hT[:, :, 0:N], cT, cT), "sq1")
            mark(tt(hT[:, :, N:2 * N], xT[:, :, :], xT[:, :, :]), "sq1")
            n, b = ready("ss1")
            F(n, ts(inv, b[:, :], 1.0 / D, 1e-6))
            rsqrt(inv)
            dve.wait_ge(S("unit_used"), 12)
            V(tt(modT[:, :, :], P[4][:, 0:96].rearrange("p (m w) -> p m w", w=2),
                 col("b_mod", 0, 48).unsqueeze(2).to_broadcast([128, 48, 2]), ALU.add))
            for w in range(2):
                V(stt(n1s[:, 8 * w:8 * w + 8], modT[:, 8:16, w], 1.0, col("norm1_w", 0, 8), ALU.add, ALU.mult))
            for w, src, o in ((1, cT, 0), (0, xT, N)):
                for k in range(KT):
                    V(stt(hT[:, k, o:o + N], src[:, k, :], n1s[:, 8 * w + k:8 * w + k + 1], inv[:, o:o + N]))
                    ins = ts(hT[:, k, o:o + N], hT[:, k, o:o + N], modT[:, k, w:w + 1], None, ALU.add, ALU.bypass)
                    if (w, k) == (0, KT - 1):
                        mark(ins, "h_ready")
                    else:
                        V(ins)
            for j in range(32 + 2):
                if j < 32:
                    sl = slice(0, 2) if j < 24 else slice(1, 2)
                    dve.wait_ge(S("mm_free"), START["xb"] + j + 1)
                    r = craw[:, j % 2]
                    ca = cacc[:, j % 2, :].rearrange("p (s n) -> p s n", s=2)[:, sl, :]
                    V(ts(ca, r[:, sl, 0:N], col("conv_w", j), col("conv_b", j)))
                    for tap in range(1, 5):
                        ins = stt(ca, r[:, sl, tap:tap + N], col("conv_w", 32 * tap + j), ca, ALU.mult, ALU.add)
                        if tap < 4:
                            V(ins)
                        else:
                            mark(ins, "conv_done")
                if 1 <= j <= 32:
                    i = j - 1
                    dve.wait_ge(S("conv_sig"), i + 1)
                    c2, s2 = cacc[:, i % 2, :], csil[:, i % 2, :]
                    if i < 16:
                        mark(tt(s2, c2, s2), "conv_out")
                    elif i < 24:
                        V(tt(s2, c2, s2))
                        mark(v.tensor_copy(Bf[:, i - 16, :], s2[:, N:2 * N]), "conv_out")
                    else:
                        mark(tt(Cf[:, i - 24, :], c2[:, N:2 * N], s2[:, N:2 * N]), "conv_out")
                if 2 <= j < 26:
                    i = j - 2
                    dve.wait_ge(S("turned"), i + 1)
                    dst = XT[:, :, 128 * i:128 * i + 128] if i < 16 else BT[:, :, 128 * (i - 16):128 * (i - 16) + 128]
                    mark(v.tensor_copy(dst, P[4 + i % 2][:, :].rearrange("p (c n) -> p c n", c=4)), "turn_free")
            dve.wait_ge(S("rows"), 48)
            n, b = ready("dt")
            F(n, tt(dtt, b[:, 0:256].rearrange("p (c h) -> p c h", c=4), over(4, dtb[:, :]), ALU.add))
            mark(stt(dA, dtt, -1.0, dtt, ALU.mult, ALU.max), "dt_abs")
            dve.wait_ge(S("dt_exp"), 1)
            mark(ts(dA, dA, 1.0, None, ALU.add, ALU.bypass), "dt_one")
            dve.wait_ge(S("dt_ln"), 1)
            V(stt(dtt, dtt, 0.0, dA, ALU.max, ALU.add))
            V(ts(av, av, -1.0, None, ALU.mult, ALU.bypass))
            mark(tt(dA, dtt, over(4, av)), "dA_ready")
            dve.wait_ge(S("mm_free"), START["seg"] + 4)
            mark(tt(wst, dtt, ea[:, :, 64:128]), "wst_ready")
            nx = ns = 0
            dve.wait_ge(S("Y_init"), 2)
            for d, step, c, g in SSD:
                hs = slice(32 * d + 8 * g, 32 * d + 8 * g + 8)
                yg = Y[:, c - 2, 512 * g:512 * g + 512] if step >= 2 else None
                if step >= 2:
                    dve.wait_ge(S("seg_done"), nx + 1)
                    mark(tt(CBm, P[4][:, 0:128], k1("TL" if d else "TU")), "CB_ready")
                    dve.wait_ge(S("EX_ready"), nx + 1)
                    if nx:
                        dve.wait_ge(S("dg_done"), nx)
                    mark(tt(MT.rearrange("p (h l) -> p h l", h=8), EX.rearrange("p (h l) -> p h l", h=8), over(8, CBm)),
                         "MT_ready")
                    dve.wait_ge(S("yo_done"), nx + 1)
                    mark(tt(YO.rearrange("p (h e) -> p h e", h=8), P[0][:, :].rearrange("p (h e) -> p h e", h=8),
                            ea[:, c, hs].unsqueeze(2).to_broadcast([128, 8, 64])), "yo_used")
                    V(tt(yg, yg, YO, ALU.add))
                if step < 3:
                    dve.wait_ge(S("st_done"), ns + 1)
                    if step == 0:
                        mark(v.tensor_copy(H[:, d, g, :], P[1][:, :]), "H_ready")
                    else:
                        hv = H[:, d, g, :].rearrange("p (h e) -> p h e", h=8)
                        V(tt(hv, hv, ea[:, c, 128 + 32 * d + 8 * g:128 + 32 * d + 8 * g + 8].unsqueeze(2)
                             .to_broadcast([128, 8, 64])))
                        mark(tt(H[:, d, g, :], H[:, d, g, :], P[1][:, :], ALU.add), "H_ready")
                    ns += 1
                if step >= 2:
                    dve.wait_ge(S("dg_done"), nx + 1)
                    mark(tt(yg, yg, P[7][:, :], ALU.add), "dg_used")
                    nx += 1
            for i in range(8):
                n, b = ready("z", i)
                u, c = i // 2, i % 2
                dve.wait_ge(S("z_sig"), i + 1)
                F(n, tt(zs[:, i % 2, :], zs[:, i % 2, :], b[:, :]))
                yc = Y[:, c, 512 * u:512 * u + 512]
                mark(tt(yc, yc, zs[:, i % 2, :]), "z_used")
            dve.wait_ge(S("y_sq"), 2)
            V(ts(st[:, 0:2], st[:, 0:2], 1.0 / D_IN, 1e-6))
            rsqrt(st[:, 0:2])
            V(ts(Y[:, 0, :], Y[:, 0, :], st[:, 0:1], None, ALU.mult, ALU.bypass))
            mark(ts(Y[:, 1, :], Y[:, 1, :], st[:, 1:2], None, ALU.mult, ALU.bypass), "yn_ready")
            for i in range(8):
                n, b = ready("ytr", i)
                V(ts(YT[:, 2 * i, :], b[:, 0:N], col("ssd_norm_w", 2 * i), None, ALU.mult, ALU.bypass))
                F(n, ts(YT[:, 2 * i + 1, :], b[:, N:2 * N], col("ssd_norm_w", 2 * i + 1), None, ALU.mult, ALU.bypass))
            dve.wait_ge(S("mm_free"), START["gs"] + 8)
            dve.wait_ge(S("acc_done"), 1)
            for i in range(4):
                ins = tt(MX[:, 2 * i:2 * i + 2, :], P[4 + i][:, :].rearrange("p (t n) -> p t n", t=2), GT[:, 2 * i:2 * i + 2, :])
                if i < 3:
                    V(ins)
                else:
                    mark(ins, "mx_ssd")
            for f in range(8):
                n, b = ready("ff1", f)
                F(n, v.tensor_copy(V_[:, f, :], b[:, :]))
            for i in range(4):
                n, b = ready("ff2", i)
                F(n, v.tensor_copy(UT[:, 2 * i:2 * i + 2, :], b[:, :].rearrange("p (t n) -> p t n", t=2)))
            dve.wait_ge(S("mm_free"), START["gf"] + 8)
            for m in range(8):
                n, b = ready("four", m)
                F(n, tt(zs[:, m % 2, 0:N], b[:, 0:N], GT[:, m, :]))
                ins = tt(MX[:, m, :], MX[:, m, :], zs[:, m % 2, 0:N], ALU.add)
                if m < 7:
                    V(ins)
                else:
                    mark(ins, "mx_ready")
            for m in range(8):
                n, b = ready("wo", m)
                F(n, stt(xT[:, m, :], b[:, 0:N], modT[:, 16 + m, 0:1], xT[:, m, :], ALU.mult, ALU.add))
            iv = inv[:, 0:N]
            mark(tt(sc1, xT[:, :, :], xT[:, :, :]), "squares")
            n, b = ready("ss2")
            F(n, ts(iv, b[:, 0:N], 1.0 / D, 1e-6))
            rsqrt(iv)
            V(stt(n1s[:, 0:8], modT[:, 32:40, 0], 1.0, col("norm2_w", 0, 8), ALU.add, ALU.mult))
            for k in range(KT):
                V(stt(h2[:, k, :], xT[:, k, :], n1s[:, k:k + 1], iv))
                mark(ts(h2[:, k, :], h2[:, k, :], modT[:, 24 + k, 0:1], None, ALU.add, ALU.bypass), "h2_ready")

            def router(i, ne, topk):
                dve.wait_ge(S("router"), ROUTW[i])
                lg, gt, eq, pre, e_, s = (rt[:, q, 0:ne] if q < 5 else rt[:, q, :] for q in range(6))
                top = rt[:, 6, 0:8]
                for c in range(2):
                    n, b = ready(f"rt{i}", c)
                    F(n, tt(lg, b[:, 0:ne], rb[:, 0:ne], ALU.add) if i == 0 else v.tensor_copy(lg, b[:, 0:ne]))
                    V(v.max(out=top, in_=lg))
                    mark(ts(s[:, 0:1], top[:, 0:1], -1.0, None, ALU.mult, ALU.bypass), "lg_ready")
                    V(ts(gt, lg, top[:, topk - 1:topk], None, ALU.is_gt, ALU.bypass))
                    V(ts(eq, lg, top[:, topk - 1:topk], None, ALU.is_equal, ALU.bypass))
                    V(v.reduce_sum(s[:, 1:2], gt, mybir.AxisListType.X))
                    V(ts(s[:, 1:2], s[:, 1:2], -1.0, float(topk)))
                    V(v.tensor_tensor_scan(pre, k1("ones")[:, 0:ne], eq, 0.0, ALU.mult, ALU.add))
                    V(ts(pre, pre, s[:, 1:2], None, ALU.is_le, ALU.bypass))
                    V(tt(pre, pre, eq))
                    V(tt(gt, gt, pre, ALU.add))
                    dve.wait_ge(S("lg_exp"), 2 * i + c + 1)
                    V(tt(gt, gt, e_))
                    V(v.reduce_sum(s[:, 2:3], gt, mybir.AxisListType.X))
                    V(v.reciprocal(s[:, 2:3], s[:, 2:3]))
                    ins = ts(wtok[:, c, 0:ne], gt, s[:, 2:3], None, ALU.mult, ALU.bypass)
                    if c:
                        mark(ins, "w_ready")
                    else:
                        V(ins)
                n, b = ready(f"wT{i}")
                F(n, v.tensor_copy(wTt[0:ne, :], b[0:ne, 0:N]))
                for q in range(ne // 2):
                    n, b = ready(f"wB{i}", q)
                    F(n, v.tensor_copy(wB[:, 2 * q:2 * q + 2, :], b[:, :].rearrange("p (e n) -> p e n", e=2)))

            ffc = Count()

            def experts(which):
                nf = SPEC[which][1]
                loops = [(ffc, nf), (counts["ff_free"], nf)]
                if which == "a":
                    loops.append((counts["dve"], 2 * nf + 1))
                else:
                    loops.append((counts["dve"], nf))
                for e in turns(dve, which, loops):
                    if which == "a":
                        dve.wait_ge(S("act_ready"), 2)
                        V(v.tensor_copy(bge, VC[:, bass.ds(e * 16 + COL["b_gate_up"], 16)]))
                    for j in range(nf):
                        b = P[j % 4]
                        dve.wait_ge(S("ff_done"), ffc.value(ffc.n + 1))
                        dve.wait_ge(S("act_ready"), ffc.value(ffc.n + 1))
                        if which == "a":
                            V(ts(gl[:, j % 2, :], b[:, 0:N], bge[:, j:j + 1], 7.0, ALU.add, ALU.min))
                            V(ts(ul[:, j % 2, :], b[:, N:2 * N], bge[:, 8 + j:9 + j], -7.0, ALU.add, ALU.max))
                            ins = ts(ul[:, j % 2, :], ul[:, j % 2, :], 7.0, 1.0, ALU.min, ALU.add)
                        else:
                            V(v.tensor_copy(gl[:, j % 2, :], b[:, 0:N]))
                            ins = v.tensor_copy(ul[:, j % 2, :], b[:, N:2 * N])
                        mark(ins, "ff_free")
                        ffc.n += 1

            router(0, NEXP, TOPK)
            experts("a")
            dve.wait_ge(S("acc_done"), 2)
            for m in range(8):
                b = P[4 + m // 2][:, N * (m % 2):N * (m % 2) + N]
                V(stt(xT[:, m, :], b, modT[:, 40 + m, 0:1], xT[:, m, :], ALU.mult, ALU.add))
            mark(tt(sqb, xT[:, :, :], xT[:, :, :]), "squares")
            n, b = ready("ss3")
            F(n, ts(iv, b[:, 0:N], 1.0 / D, 1e-6))
            rsqrt(iv)
            for k in range(KT):
                ins = stt(xT[:, k, :], xT[:, k, :], col("final_norm_w", k), iv)
                if k < KT - 1:
                    V(ins)
                else:
                    mark(ins, "x_ready")

            def layer_norm(sa, sb_, g, bb):
                n, b = ready(sa)
                F(n, ts(iv, b[:, 0:N], 1.0 / D, None, ALU.mult, ALU.bypass))
                V(tt(xc, xT[:, :, :], over(KT, iv), ALU.subtract))
                mark(tt(sqb, xc, xc), "squares")
                n, b = ready(sb_)
                F(n, ts(iv, b[:, 0:N], 1.0 / D, 1e-5))
                rsqrt(iv)
                for k in range(KT):
                    V(stt(xT[:, k, :], xc[:, k, :], col(*g(k)), iv))
                    ins = ts(xT[:, k, :], xT[:, k, :], col(*bb(k)), None, ALU.add, ALU.bypass)
                    if k < KT - 1:
                        V(ins)
                    else:
                        mark(ins, "x_ready")

            for l in range(2):
                dve.wait_ge(S("hsig"), l + 1)
                V(tt(qT[:, 0:2, :], qT[:, 0:2, :], PT[:, 0:2, :]))
                if l:
                    V(tt(lbc[:, 0:2], col("hgrn_lb_logits_2", 2, 2), col("hgrn_lb_logits_2", 0, 2), ALU.subtract))
                    mark(v.memset(st[:, 14:15], 0.0), "lb_diff")
                    dve.wait_ge(S("lb_sig"), 1)
                    V(ts(lbc[:, 2:4], lbc[:, 0:2], -1.0, 1.0))
                    for t in range(2):
                        V(ts(fT[:, t, :], fT[:, t, :], lbc[:, 2 + t:3 + t], lbc[:, t:t + 1]))
                V(ts(kT[:, 0:2, :], fT[:, 0:2, :], -1.0, 1.0))
                V(v.tensor_copy(kT[:, 2, :], PT[:, 9, :]))
                V(ts(qT[:, 2, :], PT[:, 8, :], 32.0 ** -0.5, None, ALU.mult, ALU.bypass))
                n, b = ready(f"gate{l}")
                ga_, gb_ = g1t[:, 0, :], g1t[:, 1, :]
                F(n, ts(ga_, b[:, 0:N], col("gla_gate_b_2", l), None, ALU.add, ALU.bypass))
                mark(stt(gb_, ga_, -1.0, ga_, ALU.mult, ALU.max), "ga_abs")
                dve.wait_ge(S("ga_exp"), l + 1)
                mark(ts(gb_, gb_, 1.0, None, ALU.add, ALU.bypass), "ga_one")
                dve.wait_ge(S("ga_ln"), l + 1)
                mark(stt(ga_, ga_, 0.0, gb_, ALU.min, ALU.subtract), "ga_log")
                dve.wait_ge(S("ga_f"), l + 1)
                mark(v.memset(fT[:, :, 0:1], 0.0), "kT_ready")
                for n in range(48):
                    m = 48 * l + n
                    u = n // 16
                    if n % 16 == 0:
                        V(v.tensor_copy(f4.rearrange("p (j n) -> p j n", j=4), over(4, fT[:, u, :])))
                    dve.wait_ge(S("kv_done"), m + 1)
                    mark(v.tensor_tensor_scan(St[:, n % 2].rearrange("p j n -> p (j n)"), f4,
                                              kv[:, n % 2].rearrange("p j n -> p (j n)"), 0.0, ALU.mult, ALU.add), "scan_done")
                    if m >= 2:
                        dve.wait_ge(S("qS_used"), m - 1)
                    mark(tt(qS[:, n % 2], St[:, n % 2], over(4, qT[:, u, :])), "qS_ready")
                dve.wait_ge(S("qS_used"), 48 * (l + 1))
                V(v.tensor_copy(g2t[:, 0:2, :], P[4][:, :].rearrange("p (t n) -> p t n", t=2)))
                V(v.tensor_copy(g2t[:, 2, :], P[5][:, 0:N]))
                V(v.tensor_copy(g2t[:, 3, :], P[6][:, 0:N]))
                mark(tt(g1t, g2t, g2t), "hsq")
                for i in range(4):
                    n, b = ready(f"hn{l}", i)
                    F(n, ts(hr4[:, i, :], b[:, 0:N], 1e-6, None, ALU.add, ALU.bypass))
                rsqrt(flat(hr4))
                dve.wait_ge(S("hg_sig"), l + 1)
                V(tt(hg[:, 0:2, :], hg[:, 0:2, :], PT[:, 6:8, :]))
                V(tt(hg[:, 2:4, :], hg[:, 2:4, :], PT[:, 13:15, :]))
                V(tt(hg, hg, hr4))
                for i in range(4):
                    V(stt(mixT[:, i, :], g2t[:, i, :], col("hgrn_norm_g_2" if i < 2 else "gla_norm_g_2", l), hg[:, i, :]))
                dif = reg(B0 + 5632, 8, N)
                V(tt(dif[:, :, 1:N], PT[:, 15:23, 0:N - 1], PT[:, 15:23, 1:N], ALU.subtract))
                V(ts(dif[:, :, 0:1], PT[:, 15:23, 0:1], -1.0, None, ALU.mult, ALU.bypass))
                for i in range(8):
                    V(stt(PT[:, 15 + i, :], dif[:, i, :], col(f"mu{l}", i), PT[:, 15 + i, :], ALU.mult, ALU.add))
                p9, d9 = PT[0:32, 23, :], dif[0:32, 0, :]
                V(tt(d9[:, 1:N], p9[:, 0:N - 1], p9[:, 1:N], ALU.subtract))
                V(ts(d9[:, 0:1], p9[:, 0:1], -1.0, None, ALU.mult, ALU.bypass))
                mark(stt(p9, d9, col("mus", l)[0:32], p9, ALU.mult, ALU.add), "rw_shift")
                for i in range(6):
                    n, b = ready(f"lr{l}", i)
                    t = i % 2
                    if i < 2:
                        F(n, ts(tm[:, t, :], b[:, 0:N], col("rwkv_w0_2", 2 * l + t), None, ALU.add, ALU.bypass))
                    elif i < 4:
                        F(n, ts(ga[:, t, :], b[:, 0:N], col("rwkv_a0_2", 2 * l + t), None, ALU.add, ALU.bypass))
                    else:
                        F(n, v.tensor_copy(mixT[:, 4 + t, :], b[:, 0:N]))
                mark(v.memset(st[:, 14:15], 0.0), "wa_ready")
                if l:
                    n, b = ready("vmA1")
                    F(n, v.tensor_copy(tn[0:32, 0, :], b[0:32, 0:N]))
                    for t in range(2):
                        n, b = ready("vmB1", t)
                        F(n, ts(vv[:, t, :], b[:, 0:N], col("rwkv_v0_2", t), None, ALU.add, ALU.bypass))
                    mark(tt(t3, vfk, PT[:, 19:21, :], ALU.subtract), "vm")
                    dve.wait_ge(S("vm_sig"), 1)
                    V(tt(vv, vv, t3))
                    V(tt(vv, vv, PT[:, 19:21, :], ALU.add))
                else:
                    V(v.tensor_copy(vv, PT[:, 19:21, :]))
                    V(v.tensor_copy(vfk, PT[:, 19:21, :]))
                for t in range(2):
                    V(ts(kkr[:, t, :], PT[:, 17 + t, :], col("rwkv_k_k_2", 2 * l + t), None, ALU.mult, ALU.bypass))
                mark(tt(kks, kkr, kkr), "kk_sq")
                for t in range(2):
                    n, b = ready(f"kkn{l}", t)
                    F(n, ts(t3[:, t, :], b[:, 0:N], 64.0, 1e-24, ALU.mult, ALU.max))
                rsqrt(flat(t3))
                V(tt(kkr, kkr, t3))
                dve.wait_ge(S("wa_sig"), l + 1)
                V(ts(tm, tm, -float(np.exp(-0.5)), None, ALU.mult, ALU.bypass))
                for t in range(2):
                    ins = v.tensor_tensor_scan(tn[:, t, :], k2("keep"), tm[:, t, :], 0.0, ALU.mult, ALU.add)
                    if t:
                        mark(ins, "cum")
                    else:
                        V(ins)
                dve.wait_ge(S("cum_exp"), l + 1)
                mark(tt(tn, tn, tm, ALU.subtract), "cum_prev")
                for t in range(2):
                    V(ts(t4[:, t, :], ga[:, t, :], -1.0, col("rwkv_k_a_2", 2 * l + t), ALU.add, ALU.mult))
                V(stt(kp, t4, 1.0, PT[:, 17:19, :], ALU.add, ALU.mult))
                V(tt(t4, kkr, ga))
                V(tt(Kt, kp, Bt))
                V(tt(Bt, t4, Bt))
                V(tt(AR[:, :, 1, :], PT[:, 15:17, :], cl))
                dve.wait_ge(S("prev_exp"), l + 1)
                V(stt(AR[:, :, 0, :], kkr, -1.0, tm))
                for t in range(2):
                    ins = stt(tn[:, t, :], PT[:, 15 + t, :], col("rwkv_r_k_2", 2 * l + t), kp[:, t, :])
                    V(ins)
                V(v.memset(Sr, 0.0))
                mark(v.memset(st[:, 14:15], 0.0), "abk_ready")
                for i in range(3):
                    n, b = ready(f"tk{l}", i)
                    F(n, v.tensor_copy(tok[:, i], b[:, :].rearrange("p (c n) -> p c n", c=2)))
                for i in range(8):
                    n, b = ready(f"lm{l}", i)
                    F(n, tt(LM[:, i, :], b[:, :], k2("rwm")))
                V(v.tensor_copy(TI, over(8, k1("ident"))))
                V(v.tensor_copy(TT, over(8, k1("ident"))))
                for lev in range(LEVELS):
                    m = LEVELS * l + lev
                    mark(tt(XI, LM[:, :, 0:128], over(8, k2("lev")[:, 128 * lev:128 * lev + 128])), "inv_x")
                    dve.wait_ge(S("inv_t"), m + 1)
                    for i in range(4):
                        dst = (TI, TT)[i // 2][:, 4 * (i % 2):4 * (i % 2) + 4, :]
                        V(tt(dst, dst, P[4 + i][:, :].rearrange("p (h n) -> p h n", h=4), ALU.add))
                mark(v.memset(st[:, 14:15], 0.0), "inv_end")
                mark(v.memset(st[:, 14:15], 0.0), "S_ready")
                for c in range(4):
                    dve.wait_ge(S("SO_done"), 4 * l + c + 1)
                    V(tt(flat(Sr), flat(Sr), P[7][:, 0:128], ALU.add))
                    V(ts(Sr[:, 0, :], Sr[:, 0, :], cl[:, 0, 64 * c + 63:64 * c + 64], None, ALU.mult, ALU.bypass))
                    mark(ts(Sr[:, 1, :], Sr[:, 1, :], cl[:, 1, 64 * c + 63:64 * c + 64], None, ALU.mult, ALU.bypass), "S_ready")
                mark(v.tensor_copy(flat(oT), P[6][:, :]), "o_ready")
                for t in range(2):
                    n, b = ready(f"gnA{l}", t)
                    F(n, tt(oT[:, t, :], oT[:, t, :], b[:, 0:N], ALU.subtract))
                mark(tt(tm, oT, oT), "o_sq")
                for t in range(2):
                    n, b = ready(f"gnB{l}", t)
                    F(n, ts(t3[:, t, :], b[:, 0:N], 64e-5, None, ALU.add, ALU.bypass))
                rsqrt(flat(t3))
                for t in range(2):
                    V(stt(oT[:, t, :], oT[:, t, :], col("rwkv_lnx_g_2", 2 * l + t), t3[:, t, :]))
                    V(ts(oT[:, t, :], oT[:, t, :], col("rwkv_lnx_b_2", 2 * l + t), None, ALU.add, ALU.bypass))
                mark(v.memset(st[:, 14:15], 0.0), "rkr_ready")
                for t in range(2):
                    n, b = ready(f"rkv{l}", t)
                    F(n, stt(t4[:, t, :], b[:, 0:N], 64.0, vv[:, t, :]))
                V(tt(oT, oT, t4, ALU.add))
                V(tt(mixT[:, 4:6, :], mixT[:, 4:6, :], oT))
                if not l:
                    dve.wait_ge(S("positions"), 16)
                a0, a1, a2 = ang[:, 0, :], ang[:, 1, :], ang[:, 2, :]
                V(v.tensor_copy(a0, posi))
                V(ts(a0, a0, k2("inv"), None, ALU.mult, ALU.bypass))
                V(ts(a1, a0, float(1 / (2 * np.pi)), 12582912.0))
                V(ts(a1, a1, -12582912.0, None, ALU.add, ALU.bypass))
                c1 = 6.28125
                c2 = float(np.float32(2 * np.pi - c1))
                V(stt(a0, a1, -c1, a0, ALU.mult, ALU.add))
                V(stt(a0, a1, -c2, a0, ALU.mult, ALU.add))
                mark(ts(a2, a0, 3.1415925, -3.1415925, ALU.min, ALU.max), "ang_ready")
                dve.wait_ge(S("sin_ready"), l + 1)
                V(tt(cosT, cosT, cosT))
                V(ts(cosT, cosT, -2.0, 1.0))
                V(tt(qk, PT[:, 24:28, :], over(4, cosT)))
                for i in range(4):
                    n, b = ready(f"rot{l}", i)
                    F(n, tt(rsw[:, i, :], b[:, 0:N], sinT))
                mark(tt(qk, qk, rsw, ALU.add), "qk_ready")
                n, b = ready(f"rv{l}")
                F(n, v.tensor_copy(vtk, b[:, :].rearrange("p (c n) -> p c n", c=2)))
                for i in range(8):
                    n, b = ready(f"rs{l}", i)
                    h, q = i // 2, i % 2
                    w = 256 - 128 * q
                    F(n, tt(sc[:, h, 256 * q:256 * q + w], b[:, 0:w], k2("ret")[:, 256 * h:256 * h + w]))
                for h in range(4):
                    n, b = ready(f"ro{l}", h)
                    hp = slice(64 * (h % 2), 64 * (h % 2) + 64)
                    F(n, v.tensor_copy(ro[hp, h // 2, :], b[hp, 0:N]))
                for t in range(2):
                    n, b = ready(f"rnA{l}", t)
                    F(n, tt(rc[:, t, :], ro[:, t, :], b[:, 0:N], ALU.subtract))
                mark(tt(rq, rc, rc), "rc_sq")
                for t in range(2):
                    n, b = ready(f"rnB{l}", t)
                    F(n, ts(ang[:, t, :], b[:, 0:N], 1e-5, None, ALU.add, ALU.bypass))
                rsqrt(flat(ang[:, 0:2, :]))
                V(tt(rc, rc, ang[:, 0:2, :]))
                dve.wait_ge(S("rg_sig"), l + 1)
                V(tt(rsw[:, 0:2, :], rsw[:, 0:2, :], PT[:, 30:32, :]))
                mark(tt(mixT[:, 6:8, :], rc, rsw[:, 0:2, :]), "mix_ready")
                for m in range(8):
                    n, b = ready(f"out{l}", m)
                    F(n, stt(xT[:, m, :], xT[:, m, :], ALPHA, b[:, 0:N], ALU.mult, ALU.add))
                layer_norm(f"laA{l}", f"laB{l}", lambda k: ("ln1_g_2", 8 * l + k), lambda k: ("ln1_b_2", 8 * l + k))
                if l:
                    router(1, 8, 2)
                experts("m" if l else "d")
                dve.wait_ge(S("acc_done"), 3 + l)
                for i in range(4):
                    ins = v.tensor_copy(xT[:, 2 * i:2 * i + 2, :], P[4 + i][:, :].rearrange("p (t n) -> p t n", t=2))
                    if i < 3:
                        V(ins)
                    else:
                        mark(ins, "r_ready")
                layer_norm(f"lbA{l}", f"lbB{l}", lambda k: ("ln2_g_2", 8 * l + k), lambda k: ("ln2_b_2", 8 * l + k))
            for i in range(8):
                n, b = ready("fin", i)
                F(n, v.tensor_copy(res[:, i // 4, N * (i % 4):N * (i % 4) + N], b[:, 0:N]))

        @block.scalar
        def _(act_):
            mark, counts = marker(act_)
            roots = [0]

            def fn(out, in_, f, **kw):
                return nc.scalar.activation(out, in_, f, **kw)

            def A(ins):
                mark(ins, "act")

            def F(n, ins):
                ins.then_inc(S("mm_free"), 1)
                act_.wait_ge(S("mm_free"), n + 1)

            def ready(stage, i=0):
                n = START[stage] + i
                act_.wait_ge(S("mm_done"), n + 1)
                return n, P[n % 4]

            def root(x):
                roots[0] += 1
                act_.wait_ge(S("to_root"), roots[0])
                mark(fn(x, x, ACT.Sqrt), "rooted")

            def flat(x):
                return x.rearrange("p a b -> p (a b)")

            act_.dma_start(C1[:, :], a["const1"]).then_inc(S("consts"), 16)
            act_.dma_start(xload[:, 0:2, :], a["ctx"][0].rearrange("(c p) d -> p c d", p=128)).then_inc(S("xin"), 16)
            act_.dma_start(xload[:, 2:4, :], a["x"][0].rearrange("(c p) d -> p c d", p=128)).then_inc(S("xin"), 16)
            act_.wait_ge(S("vload_zero"), 1)
            for at, lo, src in a["vec_dmas"]:
                r = at % 128
                act_.dma_start(vload[r:r + src.shape[0], at // 128, lo:lo + src.shape[1]], src).then_inc(S("vecs"), 16)
            for dst, src in ((dtb[:, :], a["dt_bias"]), (av, a["a_log"])):
                act_.dma_start(dst, src.rearrange("a b c -> a (b c)").to_broadcast([128, 64])).then_inc(S("rows"), 16)
            act_.dma_start(dskip, a["d_skip"].to_broadcast([128, 32])).then_inc(S("rows"), 16)
            cs3 = cs.rearrange("p (k w) -> p k w", w=2)
            act_.wait_ge(S("mm_free"), START["xin"])
            mark(fn(cs3[:, :, 0], col("c", 0, 8), ACT.Sigmoid), "sil")
            mark(fn(cs3[:, :, 1], col("c_ctx", 0, 8), ACT.Sigmoid), "sil")
            root(inv)
            act_.wait_ge(S("craw_zero"), 1)
            for j in range(33):
                if j < 32:
                    n, b = ready("xb", j)
                    if j >= 2:
                        act_.wait_ge(S("conv_done"), j - 1)
                    if j < 24:
                        F(n, fn(craw[:, j % 2, :, 2:2 + N], b[:, :].rearrange("p (s n) -> p s n", s=2), ACT.Copy))
                    else:
                        F(n, fn(craw[:, j % 2, 1, 2:2 + N], b[:, 0:N], ACT.Copy))
                if j >= 1:
                    i = j - 1
                    act_.wait_ge(S("conv_done"), i + 1)
                    if i >= 2:
                        act_.wait_ge(S("turned"), min(i - 1, 24))
                        act_.wait_ge(S("conv_out"), i - 1)
                    s = slice(0, 2 * N) if i < 24 else slice(N, 2 * N)
                    mark(fn(csil[:, i % 2, s], cacc[:, i % 2, s], ACT.Sigmoid), "conv_sig")
            act_.wait_ge(S("dt_abs"), 1)
            mark(fn(dA, dA, ACT.Exp, scale=-1.0), "dt_exp")
            A(fn(av, av, ACT.Exp))
            act_.wait_ge(S("dt_one"), 1)
            mark(fn(dA, dA, ACT.Ln), "dt_ln")
            for c in range(4):
                n, b = ready("seg", c)
                F(n, fn(ea[:, c, :], b[:, 0:192], ACT.Exp))
            for nx in range(16):
                act_.wait_ge(S("seg_done"), nx + 1)
                if nx:
                    act_.wait_ge(S("MT_ready"), nx)
                A(fn(EX[:, 0:512], P[5][:, :], ACT.Exp))
                mark(fn(EX[:, 512:1024], P[6][:, :], ACT.Exp), "EX_ready")
            for i in range(8):
                n, b = ready("z", i)
                if i >= 2:
                    act_.wait_ge(S("z_used"), i - 1)
                mark(fn(zs[:, i % 2, :], b[:, :], ACT.Sigmoid), "z_sig")
            act_.wait_ge(S("z_used"), 8)
            for c in range(2):
                mark(fn(junk, Y[:, c, :], ACT.Square, accum_out=st[:, c:c + 1]), "y_sq")
            root(st[:, 0:2])
            for m in range(8):
                n, b = ready("gs", m)
                F(n, fn(GT[:, m, :], b[:, 0:N], ACT.Sigmoid))
            for i in range(4):
                n, b = ready("u", i)
                F(n, fn(U[:, i % 2, 512 * (i // 2):512 * (i // 2) + 512], b[:, :], ACT.Copy))
            act_.wait_ge(S("mx_ssd"), 1)
            for m in range(8):
                n, b = ready("gf", m)
                F(n, fn(GT[:, m, :], b[:, 0:N], ACT.Sigmoid))
            root(inv[:, 0:N])

            def router(i, ne):
                for c in range(2):
                    act_.wait_ge(S("lg_ready"), 2 * i + c + 1)
                    mark(fn(rt[:, 4, 0:ne], rt[:, 0, 0:ne], ACT.Exp, bias=rt[:, 5, 0:1]), "lg_exp")

            ffc = Count()

            def experts(which):
                nf = SPEC[which][1]
                for e in turns(act_, which, [(ffc, nf), (counts.setdefault("sg_ready", Count()), nf)]):
                    for j in range(nf):
                        act_.wait_ge(S("ff_free"), ffc.value(ffc.n + 2))
                        mark(fn(sg[:, j % 2, :], gl[:, j % 2, :], ACT.Sigmoid, scale=1.702 if which == "a" else 1.0),
                             "sg_ready")
                        ffc.n += 1

            router(0, NEXP)
            experts("a")
            root(inv[:, 0:N])
            for l in range(2):
                for i in range(32):
                    n, b = ready(f"p{l}", i)
                    w = TILES2[i][1]
                    F(n, fn(PT[0:w, i, :], b[0:w, 0:N], ACT.Copy))
                for i, t in enumerate((4, 5, 10, 11)):
                    act_.dma_start(vd[l, i], PT[:, t, :]).then_inc(S("v_out"), 16)
                A(fn(qT[:, 0:2, :], PT[:, 0:2, :], ACT.Sigmoid))
                mark(fn(fT[:, 0:2, :], PT[:, 2:4, :], ACT.Sigmoid), "hsig")
                if l:
                    act_.wait_ge(S("lb_diff"), 1)
                    mark(fn(lbc[:, 0:2], lbc[:, 0:2], ACT.Sigmoid), "lb_sig")
                act_.wait_ge(S("ga_abs"), l + 1)
                mark(fn(g1t[:, 1, :], g1t[:, 1, :], ACT.Exp, scale=-1.0), "ga_exp")
                act_.wait_ge(S("ga_one"), l + 1)
                mark(fn(g1t[:, 1, :], g1t[:, 1, :], ACT.Ln), "ga_ln")
                act_.wait_ge(S("ga_log"), l + 1)
                mark(fn(fT[:, 2, :], g1t[:, 0, :], ACT.Exp, scale=1.0 / 16), "ga_f")
                act_.wait_ge(S("v_out"), 64 * (l + 1))
                for n in range(48):
                    u, v0, m = n // 16, 4 * (n % 16), 48 * l + n
                    if m >= 2:
                        act_.wait_ge(S("kv_done"), m - 1)
                    for h in range(2 if u < 2 else 4):
                        tile, r = (u, 64 * h) if u < 2 else (2 + h // 2, 64 * (h % 2))
                        w = 64 if u < 2 else 32
                        src = vd[l, tile, r + v0:r + v0 + 4, :].unsqueeze(0).to_broadcast([w, 4, N])
                        act_.dma_start(vb[w * h:w * h + w, n % 2], src).then_inc(S(f"vb_in{n % 2}"), 16)
                act_.wait_ge(S("hsq"), l + 1)
                A(fn(hg[:, 0:2, :], PT[:, 6:8, :], ACT.Sigmoid))
                mark(fn(hg[:, 2:4, :], PT[:, 13:15, :], ACT.Sigmoid), "hg_sig")
                root(flat(hr4))
                act_.wait_ge(S("rw_shift"), l + 1)
                A(fn(PT[0:64, 21, :], PT[0:64, 21, :], ACT.Tanh))
                A(fn(PT[:, 22, :], PT[:, 22, :], ACT.Sigmoid))
                mark(fn(PT[0:32, 23, :], PT[0:32, 23, :], ACT.Sigmoid), "tanh_ready")
                act_.wait_ge(S("wa_ready"), l + 1)
                A(fn(tm, tm, ACT.Sigmoid))
                mark(fn(ga, ga, ACT.Sigmoid), "wa_sig")
                if l:
                    act_.wait_ge(S("vm"), 1)
                    mark(fn(vv, vv, ACT.Sigmoid), "vm_sig")
                root(flat(t3))
                act_.wait_ge(S("cum"), l + 1)
                A(fn(cl, tn, ACT.Exp))
                mark(fn(Bt, tn, ACT.Exp, scale=-1.0), "cum_exp")
                act_.wait_ge(S("cum_prev"), l + 1)
                mark(fn(tm, tn, ACT.Exp), "prev_exp")
                for lev in range(LEVELS):
                    act_.wait_ge(S("inv_y"), LEVELS * l + lev + 1)
                    A(fn(YI[:, 0:4, :], P[4][:, :].rearrange("p (h n) -> p h n", h=4), ACT.Copy))
                    mark(fn(YI[:, 4:8, :], P[5][:, :].rearrange("p (h n) -> p h n", h=4), ACT.Copy), "inv_yc")
                for c in range(4):
                    o = slice(64 * (c % 2), 64 * (c % 2) + 64)
                    act_.wait_ge(S("W_done"), 4 * l + c + 1)
                    mark(fn(Wt[o, :], P[4][o, 0:N], ACT.Copy), "W_ready")
                    act_.wait_ge(S("U_done"), 4 * l + c + 1)
                    mark(fn(Ut[o, :], P[5][o, 0:N], ACT.Copy), "U_ready")
                root(flat(t3))
                act_.wait_ge(S("ang_ready"), l + 1)
                A(fn(sinT, ang[:, 2, :], ACT.Sin))
                mark(fn(cosT, ang[:, 2, :], ACT.Sin, scale=0.5), "sin_ready")
                act_.wait_ge(S("qk_ready"), l + 1)
                mark(fn(rsw[:, 0:2, :], PT[:, 30:32, :], ACT.Sigmoid), "rg_sig")
                root(flat(ang[:, 0:2, :]))
                root(inv[:, 0:N])
                if l:
                    router(1, 8)
                experts("m" if l else "d")
                root(inv[:, 0:N])

        @block.gpsimd
        def _(pool):
            mark, counts = marker(pool)
            g_ = nc.gpsimd

            def G(ins):
                mark(ins, "pool")

            def tt(out, a_, b_, op=ALU.mult):
                return g_.tensor_tensor(out=out, in0=a_, in1=b_, op=op)

            def over(k, x):
                return x.unsqueeze(1).to_broadcast([128, k, x.shape[1]])

            def heads(x):
                return x.unsqueeze(2).to_broadcast([128, 8, 64])

            mark(g_.memset(craw, 0.0), "craw_zero")
            pool.wait_ge(S("wst_ready"), 1)
            for c in range(2):
                mark(tt(Y[:, c, :].rearrange("p (h e) -> p h e", h=32), XT[:, 2 + c, :].rearrange("p (h e) -> p h e", h=32),
                        dskip.unsqueeze(2).to_broadcast([128, 32, 64])), "Y_init")
            nx = ns = 0
            for d, step, c, g in SSD:
                hs = slice(32 * d + 8 * g, 32 * d + 8 * g + 8)
                xg = XT[:, c, 512 * g:512 * g + 512].rearrange("p (h e) -> p h e", h=8)
                if step >= 2:
                    if nx:
                        pool.wait_ge(S("seg_done"), nx)
                    mark(tt(A1.rearrange("p (h l) -> p h l", h=8), dA[:, c, hs].unsqueeze(2).to_broadcast([128, 8, 128]),
                            over(8, k1("SU" if d else "SL"))), "A1_ready")
                if step < 3:
                    if ns:
                        pool.wait_ge(S("st_done"), ns)
                    mark(tt(XW.rearrange("p (h e) -> p h e", h=8), xg, heads(wst[:, c, hs])), "XW_ready")
                    ns += 1
                if step >= 2:
                    if nx:
                        pool.wait_ge(S("dg_done"), nx)
                    mark(tt(XD.rearrange("p (h e) -> p h e", h=8), xg, heads(dtt[:, c, hs])), "XD_ready")
                    nx += 1
            pool.wait_ge(S("squares"), 1)
            w_r = a["w_router"][0].rearrange("(k p) e -> p k e", p=128)
            pool.dma_start(wr, w_r).then_inc(S("router"), 16)
            pool.dma_start(rb, a["b_router"].to_broadcast([128, NEXP])).then_inc(S("router"), 16)
            pool.dma_start(bdn[0:NEXP, :], a["b_down"][0]).then_inc(S("router"), 16)
            pool.dma_start(C2, a["const2"]).then_inc(S("consts2"), 16)
            pool.dma_start(posi, a["positions_2"].to_broadcast([128, N])).then_inc(S("positions"), 16)

            def small_weights(l):
                for dst, src in ((gw2[0:16, :], a["gla_gate_w2_2"][l]), (w2s[0:64, :], a["rwkv_w2_2"][l]),
                                 (w2s[64:128, :], a["rwkv_a2_2"][l]), (g2a, a["rwkv_g2_2"][l][0:128]),
                                 (g2b[0:32, :], a["rwkv_g2_2"][l][128:160])):
                    pool.dma_start(dst, src).then_inc(S("lay"), 16)
                if l:
                    pool.dma_start(v1s, a["rwkv_v1_2"][0].rearrange("(t p) r -> p t r", p=128)).then_inc(S("lay"), 16)
                    pool.dma_start(v2s[0:32, :], a["rwkv_v2_2"][0]).then_inc(S("lay"), 16)

            small_weights(0)
            ffc = Count()
            for _ in range(2):
                mark(g_.memset(act[:, 0, 0:1], 0.0), "act_ready")

            def experts(which):
                nf = SPEC[which][1]
                per = nf * {"a": 2, "m": 2, "d": 1}[which] + (which != "d")
                for e in turns(pool, which, [(ffc, nf), (counts["act_ready"], nf), (counts.setdefault("pool", Count()), per)]):
                    if which != "d":
                        pool.wait_ge(S("act_ready"), 2)
                        G(g_.tensor_copy(wBe, wB.rearrange("p e n -> p (e n)")[:, bass.ds(e * N, N)]))
                    for j in range(nf):
                        pool.wait_ge(S("ff_free"), ffc.value(ffc.n + 2))
                        u_, gg, s_ = ul[:, j % 2, :], gl[:, j % 2, :], sg[:, j % 2, :]
                        G(tt(u_, u_, gg))
                        if which != "d":
                            G(tt(u_, u_, wBe))
                        pool.wait_ge(S("sg_ready"), ffc.value(ffc.n + 1))
                        mark(tt(act[:, j, :], u_, s_), "act_ready")
                        ffc.n += 1

            pool.wait_ge(S("mm_free"), START["ss3"])
            experts("a")
            vb_n = [0, 0]
            for l in range(2):
                pool.wait_ge(S("kT_ready"), l + 1)
                for n in range(48):
                    m, u = 48 * l + n, n // 16
                    vb_n[n % 2] += 32 if u < 2 else 64
                    pool.wait_ge(S(f"vb_in{n % 2}"), vb_n[n % 2])
                    if m >= 2:
                        pool.wait_ge(S("scan_done"), m - 1)
                    mark(tt(kv[:, n % 2], vb[:, n % 2], over(4, kT[:, u, :])), "kv_done")
                pool.wait_ge(S("mix_ready"), l + 1)
                if l == 0:
                    small_weights(1)
                else:
                    pool.dma_start(wr[:, :, 0:8], a["moe_router_2"][0].rearrange("(k p) e -> p k e", p=128))\
                        .then_inc(S("router"), 32)
                    pool.wait_ge(S("mm_free"), START["lbA1"])
                if l == 0:
                    pool.wait_ge(S("x_ready"), 2)
                experts("m" if l else "d")


def kernel(**inputs):
    import concourse.bacc as bacc
    from concourse.bass_utils import run_bass_kernel_spmd

    nc = bacc.Bacc("TRN2", target_bir_lowering=False, num_devices=1)
    (c1, where1), (c2, where2) = constants()
    arrays, aps = {}, {}
    given = {k: np.ascontiguousarray(v) for k, v in inputs.items()}
    given["const1"], given["const2"] = c1, c2
    for name, v in given.items():
        arrays[f"in_{name}"] = v
        aps[name] = nc.dram_tensor(f"in_{name}", v.shape, mybir.dt.from_np(v.dtype), kind="ExternalInput").ap()
    aps["vec_dmas"] = vector_rows(aps)
    out = nc.dram_tensor("out", (1, 256, 1024), F32, kind="ExternalOutput").ap()
    build(nc, aps, out, where1, where2)
    r = run_bass_kernel_spmd(nc, [arrays], core_ids=[0])
    return r.results[0]["out"]
```

```python
import concourse.bass as bass
from concourse import mybir
from contextlib import ExitStack
import numpy as np

F32 = mybir.dt.float32
ALU = mybir.AluOpType
ACT = mybir.ActivationFunctionType

D = 1024
KT = D // 128
N = 256
NHEAD = 32
D_IN = 2048
XB = 3072
OFF_DT, OFF_CF, OFF_Z, OFF_F, OFF_GF, OFF_GS = 3072, 3136, 4160, 6208, 7232, 8256
NEXP, TOPK = 32, 4
FFE = 1408 // 128
ALPHA = 4.0 ** 0.25
GAMMA = [float(np.log(1.0 - 2.0 ** (-5.0 - h))) for h in range(4)]

TILES2 = ([(c, 128) for c in range(0, 1536, 128)] + [(1536, 16), (1552, 128), (1680, 128)]
          + [(1808 + 128 * i, 128) for i in range(8)] + [(2832, 32)] + [(2864 + 128 * i, 128) for i in range(8)])
CHUNKS2 = [(0, 4), (4, 8), (8, 12), (12, 16), (16, 20), (20, 24), (24, 28), (28, 32)]

VECS = [("b_mod", 48), ("c", 8), ("c_ctx", 8), ("norm1_w", 8), ("norm2_w", 8), ("conv_w", 160), ("conv_b", 32),
        ("ssd_norm_w", 16), ("final_norm_w", 8), ("ln1_g_2", 16), ("ln1_b_2", 16), ("ln2_g_2", 16),
        ("ln2_b_2", 16), ("hgrn_lb_logits_2", 4), ("gla_gate_b_2", 2), ("rwkv_w0_2", 4), ("rwkv_a0_2", 4),
        ("rwkv_k_k_2", 4), ("rwkv_k_a_2", 4), ("rwkv_r_k_2", 4), ("rwkv_lnx_g_2", 4), ("rwkv_lnx_b_2", 4),
        ("rwkv_v0_2", 2), ("mu0", 8), ("mu1", 8), ("mus", 2), ("hgrn_norm_g_2", 2), ("gla_norm_g_2", 2),
        ("b_gate_up", 512)]
COL, _at = {}, 0
for _n, _k in VECS:
    COL[_n] = _at
    _at += _k
NTAB = (_at + 127) // 128


def constants():
    i = np.arange(128)
    r, c = i[:, None], i[None, :]
    th = 2 * np.pi * np.outer(np.arange(256), np.arange(256)) / 256
    cs = np.concatenate([np.cos(th), -np.sin(th)], 1) / 16.0
    tf = 2 * np.pi * np.outer(i, i) / 128
    s = 1 / np.sqrt(128.0)
    one = [("ident", r == c), ("TU", r <= c), ("SL", r > c), ("TL", r >= c), ("SU", r < c), ("ones", r >= 0 * c),
           ("head", (r // 64 == c // 64) / 64.0), ("dft", np.concatenate([cs[:128], cs[128:]], 1)),
           ("dfc", np.cos(tf) * s), ("dfs", np.sin(tf) * s), ("iota", 0 * r + c)]
    i2 = np.arange(256)
    rel = i2[None, :] - r
    dec = [np.where(rel >= 0, np.exp(np.minimum(np.maximum(rel, 0) * g, 0)), 0) / 8.0 for g in GAMMA]
    same = (r // 64) == (c // 64)
    su, iu = same & (r < c), same & (r <= c)
    lev = [((c // n) % 2 == 1) & (r // n == c // n - 1) for n in (1, 2, 4, 8, 16, 32)]
    z = np.arange(192)[None, :]
    rot = np.zeros((128, 128))
    for m in range(128):
        if m % 64 < 32:
            rot[m + 32, m] = -1
        else:
            rot[m - 32, m] = 1
    inv = (10000.0 ** (-(np.arange(32, dtype=np.float32)) / np.float32(32))).astype(np.float32)
    two = [("ret", np.concatenate(dec, 1)), ("rwm", np.concatenate([su, iu, su, iu], 1)),
           ("lev", np.concatenate(lev, 1)), ("keep", np.broadcast_to(i2[None, :] % 64 != 0, (128, 256))),
           ("zH", z == 64 * (r // 64) + 63), ("zG", np.arange(320)[None, :] == 64 * (r // 32) + 63), ("rot", rot),
           ("inv", np.tile(inv, 4)[:, None]), ("alpha", (r == c) * ALPHA)]
    out = []
    for part in (one, two):
        at, where, cols = 0, {}, []
        for n, v in part:
            v = np.asarray(v, np.float32)
            where[n] = (at, v.shape[1])
            at += v.shape[1]
            cols.append(v)
        out.append((np.ascontiguousarray(np.concatenate(cols, 1)), where))
    return out

def vector_rows(a):
    def rows(ap):
        names = " ".join("abc"[:len(ap.shape)])
        flat = ap.rearrange(f"{names} -> ({names})") if len(ap.shape) > 1 else ap
        return flat.rearrange("(r w) -> r w", w=128)

    out = []

    def add(at, ap, lo=0):
        while ap.shape[0]:
            k = min(ap.shape[0], 128 - at % 128)
            out.append((at, lo, ap[0:k]))
            if k == ap.shape[0]:
                return
            at, ap = at + k, ap[k:]

    for name, k in VECS:
        if name in ("mu0", "mu1"):
            l = int(name[2])
            add(COL[name], rows(a["rwkv_mu_2"][l:l + 1, 0:1024]))
        elif name == "mus":
            add(COL[name], a["rwkv_mu_2"][:, 1024:1056])
        elif name in ("hgrn_norm_g_2", "gla_norm_g_2"):
            add(COL[name], a[name])
            add(COL[name], a[name], 64)
        else:
            add(COL[name], rows(a[name]))
    return out


class Count:
    def __init__(self):
        self.n, self.i, self.per, self.at = 0, None, 0, 0

    def enter(self, i, per):
        self.i, self.per, self.at = i, per, self.n

    def leave(self, times):
        assert self.n - self.at == self.per, (self.n - self.at, self.per)
        self.n = self.at + self.per * times
        self.i = None

    def value(self, n):
        return n if self.i is None else self.i * self.per + n


def build(nc, a, out, where1, where2):
    ctx = ExitStack()
    with ctx:
        def sb(name, shape):
            return ctx.enter_context(nc.sbuf_tensor(name, shape, F32))[tuple(slice(None) for _ in shape)]

        sems = {}

        def S(name):
            if name not in sems:
                sems[name] = ctx.enter_context(nc.semaphore(name))
            return sems[name]

        P = [ctx.enter_context(nc.psum_tensor(f"P{i}", [128, 512], F32)) for i in range(8)]

        WS = sb("WS", [128, 6, 2048])
        xT = sb("xT", [128, KT, N])
        VC = sb("VC", [128, NTAB * 128])
        C1 = sb("C1", [128, a["const1"].shape[1]])
        modT = sb("modT", [128, 48, 2])
        small = sb("small", [128, 1024])
        R = sb("R", [128, 33410])

        def k1(n):
            at, w = where1[n]
            return C1[:, at:at + w]

        def reg(at, *dims):
            v = R[:, at:at + int(np.prod(dims))]
            if len(dims) == 2:
                v = v.rearrange("p (a b) -> p a b", a=dims[0])
            if len(dims) == 3:
                v = v.rearrange("p (a b c) -> p a b c", a=dims[0], b=dims[1])
            return v

        hT = reg(0, KT, 2 * N)
        XT = reg(4096, 4, D_IN)
        BT = reg(12288, 4, 1024)
        Bf = reg(16384, 8, N)
        Cf = reg(18432, 8, N)
        Y = reg(20480, 2, D_IN)
        H = reg(24576, 2, 4, 512)
        SCR = 28672
        craw = reg(SCR, 2, 2, 260)
        cacc = reg(SCR + 1040, 2, 512)
        csil = reg(SCR + 2064, 2, 512)
        xload = reg(12288, 4, D)
        vload = reg(20480, NTAB, 128)
        modR = reg(4096, 48 * 128)
        sq = reg(24576, 2, 512)
        A1 = reg(SCR, 1024)
        EX = reg(SCR + 1024, 1024)
        MT = reg(SCR + 2048, 1024)
        XD = reg(SCR + 3072, 512)
        XW = reg(SCR + 3584, 512)
        YO = reg(SCR + 4096, 512)
        dtt = small[:, 0:256].rearrange("p (c h) -> p c h", c=4)
        dA = small[:, 256:512].rearrange("p (c h) -> p c h", c=4)
        wst = small[:, 512:768].rearrange("p (c h) -> p c h", c=4)
        CBm = small[:, 768:896]
        av = small[:, 896:960]
        dskip = small[:, 960:992]
        ea = sb("ea", [128, 4, 192])
        dtb = sb("dtb", [128, 64])
        n1s = sb("n1s", [128, 2 * KT])
        cs = sb("cs", [128, 2 * KT])
        st = sb("st", [128, 16])
        inv = ea.rearrange("p c h -> p (c h)")[:, 0:512]
        vd = nc.dram_tensor("value_rows", [2, 4, 128, N], F32, kind="Internal").ap()
        zs = reg(SCR, 2, 512)
        junk = reg(SCR + 1024, 2048)
        YT = reg(4096, 16, N)
        GT = reg(8192, KT, N)
        MX = reg(10240, KT, N)
        U = reg(12288, 2, D)
        V_ = reg(14336, 8, 512)
        UT = reg(18432, 8, N)
        SPB = 2048 + 32 * N + 2048 + a["const2"].shape[1]
        B0 = SPB
        h2 = reg(0, KT, N)
        sqb = reg(0, KT, N)
        WX = reg(2048, 6, 2048)
        rt = reg(B0, 8, 32)
        wr = reg(B0 + 256, KT, 32)
        wTt = reg(B0 + 512, N)
        bdn = reg(B0 + 768, D)
        rb = reg(B0 + 1792, 32)
        wtok = reg(B0 + 1824, 2, 32)
        lgs = reg(B0 + 1888, 2, 32)
        msk = reg(B0 + 1952, 2, 32)
        keys = reg(B0 + 2016, 66)
        kw = reg(B0 + 2082, 66)
        cnt = reg(B0 + 2148, 32)
        cnti = cnt.bitcast(mybir.dt.int32)
        bge = reg(B0 + 2180, 16)
        xtok = reg(B0 + 2196, 2, D)
        XG = reg(B0 + 4244, KT, 128)
        G = reg(B0 + 5268, 2, 128)
        Gw = reg(B0 + 5524, 2, 128)
        ST = reg(B0 + 5780, N)
        ys = reg(B0 + 6036, D)
        act = reg(B0 + 7060, FFE, N)
        acte = reg(B0 + 7060, FFE, 128)
        gl = reg(B0 + 9876, 2, N)
        ul = reg(B0 + 10388, 2, N)
        sg = reg(B0 + 10900, 2, N)
        xc = reg(B0 + 11412, KT, N)
        sc1 = reg(B0 + 13460, 8, N)
        PT = reg(2048, 32, N)
        mixT = reg(10240, KT, N)
        C2 = reg(12288, a["const2"].shape[1])

        def k2(n):
            at, w = where2[n]
            return C2[:, at:at + w]

        fT = reg(B0, 3, N)
        kT = reg(B0 + 768, 3, N)
        qT = reg(B0 + 1536, 3, N)
        f4 = reg(B0 + 2304, 1024)
        vb = [reg(x, 4, N) for x in (B0 + 3328, B0 + 4352, B0 + 13568)]
        kv = reg(B0 + 5376, 2, 4, N)
        St = reg(B0 + 7424, 2, 4, N)
        qS = reg(B0 + 9472, 2, 4, N)
        g1t = reg(B0 + 11520, 4, N)
        g2t = reg(B0 + 12544, 4, N)
        r2 = reg(B0, 2, N)
        kp = reg(B0 + 512, 2, N)
        vv = reg(B0 + 1024, 2, N)
        AR = reg(B0 + 1536, 2, 2, N)
        Bt = reg(B0 + 2560, 2, N)
        Kt = reg(B0 + 3072, 2, N)
        cl = reg(B0 + 3584, 2, N)
        ga = reg(B0 + 4096, 2, N)
        tm = reg(B0 + 4608, 2, N)
        tn = reg(B0 + 5120, 2, N)
        LM = reg(B0 + 5632, 8, 512)
        TI = reg(B0 + 9728, 8, 128)
        TT = reg(B0 + 10752, 8, 128)
        XI = reg(B0 + 11776, 8, 128)
        YI = reg(B0 + 12800, 8, 128)
        tok = reg(B0 + 13824, 3, 2, N)
        Wt = reg(B0 + 15360, N)
        Ut = reg(B0 + 15616, N)
        Sr = reg(B0 + 15872, 2, 64)
        oT = reg(B0 + 16000, 2, N)
        cosT = reg(0, N)
        sinT = reg(256, N)
        ang = reg(512, 3, N)
        qk = reg(B0 + 1280, 4, N)
        rsw = reg(B0 + 2304, 4, N)
        vtk = reg(B0 + 3328, 2, N)
        sc = reg(B0 + 3840, 4, 384)
        ro = reg(B0 + 5376, 2, N)
        rc = reg(B0 + 5888, 2, N)
        rq = reg(B0 + 6400, 2, N)
        res = reg(2048, 2, D)
        kkr = reg(B0 + 9728, 2, N)
        kks = reg(B0 + 10752, 2, N)
        t3 = reg(B0 + 11776, 2, N)
        t4 = reg(B0 + 12800, 2, N)
        vfk = reg(B0 + 16512, 2, N)
        w2s = reg(B0 + 17024, N)
        g2a = reg(B0 + 17280, N)
        g2b = reg(B0 + 17536, N)
        hg = kv.rearrange("p a b c -> p (a b) c")[:, 0:4, :]
        hr4 = St.rearrange("p a b c -> p (a b) c")[:, 0:4, :]
        v1s = small[:, 0:64].rearrange("p (t r) -> p t r", t=2)
        v2s = small[:, 64:320]
        gw2 = small[:, 320:448]
        posi = small[:, 704:960].bitcast(mybir.dt.int32)
        lbc = small[:, 960:964]
        LAYW = [16 * 5, 16 * 12]
        ROUTW = [16 * 3, 16 * 4]

        def col(name, i=0, n=1):
            return VC[:, COL[name] + i:COL[name] + i + n]

        def w4(ap, r0, r1, c0, c1):
            return ap[r0:r1, c0:c1].rearrange("(k p) c -> p k c", p=128)

        def proj(ap, c0, w):
            return [(w4(ap, 0, 512, c0, c0 + w), 4, w), (w4(ap, 512, 1024, c0, c0 + w), 4, w)]

        def down(ap, kt, n):
            out = [(w4(ap, 128 * kt, 128 * (kt + min(2, n)), 0, D), min(2, n), D)]
            if n > 2:
                out.append((w4(ap, 128 * (kt + 2), 128 * (kt + n), 0, D), n - 2, D))
            return out

        w_in = a["w_in"][0]
        units1 = ([proj(a["w_mod"][0], 512 * i, 512) for i in range(12)]
                  + [proj(w_in, 512 * i, 512) for i in range(6)]
                  + [proj(w_in, OFF_CF + 512 * i, 512) for i in range(2)]
                  + [proj(w_in, OFF_DT, 64)]
                  + [proj(w_in, OFF_Z + 512 * i, 512) for i in range(4)]
                  + [down(a["w_ssd_out"][0], 4 * i, 4) for i in range(4)]
                  + [proj(w_in, OFF_GS + 512 * i, 512) for i in range(2)]
                  + [proj(w_in, OFF_F + 512 * i, 512) for i in range(2)]
                  + [proj(w_in, OFF_GF + 512 * i, 512) for i in range(2)]
                  + [proj(a["w_four_out"][0], 512 * i, 512) for i in range(2)]
                  + [proj(a["w_o"][0], 512 * i, 512) for i in range(2)])

        def chunk2(l, c):
            t0, t1 = CHUNKS2[c]
            return TILES2[t0][0], TILES2[t1 - 1][0] + TILES2[t1 - 1][1] - TILES2[t0][0]

        def units2(l):
            return ([proj(a["w_in_2"][l], *chunk2(l, c)) for c in range(8)]
                    + [proj(a["w_out_2"][l], 512 * i, 512) for i in range(2)])

        jobs = [("tab", (NTAB + 3) // 4), ("xin", 8), ("ss1", 1), ("xb", 32), ("dt", 1), ("seg", 4), ("z", 8),
                ("ytr", 8), ("gs", 8), ("u", 4), ("ff1", 8), ("ff2", 4), ("gf", 8), ("four", 8), ("wo", 8),
                ("ss2", 1), ("rt0", 2), ("ht0", 4), ("wT0", 1), ("rkn0", 1), ("ss3", 1)]
        for l in range(2):
            jobs += [(f"p{l}", 32), (f"gate{l}", 1), (f"hn{l}", 4), (f"lr{l}", 6), (f"vmA{l}", l), (f"vmB{l}", 2 * l),
                     (f"kkn{l}", 2), (f"tk{l}", 3), (f"lm{l}", 8), (f"gnA{l}", 2), (f"gnB{l}", 2), (f"rkv{l}", 2),
                     (f"rot{l}", 4), (f"rv{l}", 1), (f"rs{l}", 8), (f"ro{l}", 4), (f"rnA{l}", 2), (f"rnB{l}", 2),
                     (f"out{l}", 8), (f"laA{l}", 1), (f"laB{l}", 1)]
            if l:
                jobs += [("rt1", 2), ("ht1", 4), ("rkn1", 1)]
            jobs += [(f"lbA{l}", 1), (f"lbB{l}", 1)]
        jobs += [("fin", 8)]
        START, at = {}, 0
        for name, k in jobs:
            START[name] = at
            at += k

        def expert_halves(which, e):
            if which == "a":
                gu, dn = a["w_gate_up"][0], a["w_down"][0]
                g, d = gu[bass.ds(e, 1)].rearrange("a b c -> (a b) c"), dn[bass.ds(e, 1)].rearrange("a b c -> (a b) c")
                us = []
                for i in range(2):
                    us += [proj(g, 512 * i, 512), proj(g, D + 512 * i, 512)]
                return us + [down(d, 4 * i, 4) for i in range(2)]
            g, u, dn = (a[k][0][bass.ds(e, 1)].rearrange("a b c -> (a b) c")
                        for k in ("moe_w_gate_2", "moe_w_up_2", "moe_w_down_2"))
            us = []
            for c0, w in ((0, 512), (512, 512), (1024, 384)):
                us += [proj(g, c0, w), proj(u, c0, w)]
            return us + [down(dn, k, n) for k, n in ((0, 4), (4, 4), (8, 3))]

        def dense_halves(e):
            off = 128 * FFE
            cols = slice(off * e, off * (e + 1))
            us = []
            for c0 in range(0, off, 256):
                w = min(256, off - c0)
                us.append([(a[k][0][:, cols][:, c0:c0 + w].rearrange("(k p) c -> p k c", p=128), KT, w)
                           for k in ("ffn_w_gate_2", "ffn_w_up_2")])
            return us + [down(a["ffn_w_down_2"][0][cols, :], k, n) for k, n in ((0, 4), (4, 4), (8, 3))]

        SPEC = {"a": (NEXP, 8, 6, 1), "m": (8, FFE, 9, 2)}
        CAP = 128

        SSD = [(d, step, ((0, 1, 2, 3), (1, 0, 3, 2))[d][step], g) for d in range(2) for step in range(4) for g in range(4)]
        STEPS = ["ang_ready", "rw_shift", "hsq", "wa_ready", "vm", "kk_sq", "cum", "cum_prev", "abk_ready", "inv_end",
                 "o_ready", "o_sq", "rkr_ready", "qk_ready", "rc_sq", "mix_ready"]

        def mixed(name, l):
            return len(STEPS) * l + STEPS.index(name) + 1

        LEVELS = 6

        block = ctx.enter_context(nc.Block())

        def half(slot, h):
            return WS[:, 2 * slot + h] if slot < 3 else WX[:, 2 * (slot - 3) + h]

        def turns(eng, which, counts):
            ne, _, _, two = SPEC[which]
            with eng.Fori(0, ne // two) as i:
                for c, per in counts:
                    c.enter(i, per * two)
                for s in range(two):
                    yield i * two + s
            for c, _ in counts:
                c.leave(ne // two)

        def adds(which, name):
            ne, nf, nu, _ = SPEC[which]
            pairs = ne * ((nf + 1) // 2)
            if name.startswith("loaded"):
                return 32 * ne * nu // 6
            return {"used": 6 + ne * nu, "G": ne + 1, "gathered": ne + 1, "xgA": ne + 1, "xgB": ne + 1,
                    "turned": ne, "st": ne, "free": pairs, "pair": pairs, "act": pairs + 2, "down": 2 * ne,
                    "yA": ne, "yB": ne, "spread": ne, "end": 1, "sig": pairs, "pool": pairs,
                    "dve": 3 + ne * own_steps(which)}[name]

        def own_steps(which):
            nf = SPEC[which][1]
            return 3 + (1 + 2 * nf if which == "a" else (nf + 1) // 2)

        flags = st[:, 8:10].bitcast(mybir.dt.int32)

        class Pass:
            def __init__(self, which, second, before):
                self.which, self.second, self.before = which, second, before

            def sem(self, name):
                return S(("second_" if self.second else "first_") + name)

            def wait(self, eng, name, value):
                if self.which == "m":
                    t = adds("a", name) + (self.second and name == "dve")
                    value = value + (self.before * t if self.second else t)
                eng.wait_ge(self.sem(name), value)

        def passes(eng, which, run, seen):
            i = "am".index(which)
            first = Pass(which, False, None)
            run(which, first)
            eng.wait_ge(S("cnt_ready"), i + 1)
            flag = eng.value_load(flags[0:1, i:i + 1], min_val=0, max_val=1)
            seen.append(flag)
            with eng.If(flag > 0):
                first.wait(eng, "end", 1)
                run(which, Pass(which, True, seen[0]))

        @block.sync
        def _(sp):
            cu = Count()

            def load(unit):
                slot = cu.n % 3
                if cu.n >= 3:
                    sp.wait_ge(S("unit_used"), cu.value(cu.n - 2))
                for h, (src, k, w) in enumerate(unit):
                    dst = WS[:, 2 * slot + h, 0:k * w].rearrange("p (k c) -> p k c", k=k)
                    sp.dma_start(dst, src).then_inc(S(f"w_loaded{slot}"), 16)
                cu.n += 1

            def routed(which, p_):
                un = Count()
                for e in turns(sp, which, [(un, SPEC[which][2])]):
                    for unit in expert_halves(which, e):
                        slot = un.n % 6
                        p_.wait(sp, "used", un.value(un.n + 1))
                        for h, (src, k, w) in enumerate(unit):
                            sp.dma_start(half(slot, h)[:, 0:k * w].rearrange("p (k c) -> p k c", k=k), src)\
                                .then_inc(p_.sem(f"loaded{slot}"), 16)
                        un.n += 1

            seen = []
            for u in units1:
                load(u)
            passes(sp, "a", routed, seen)
            sp.wait_ge(S("acc_done"), 2)
            for l in range(2):
                for u in units2(l):
                    load(u)
                if l == 0:
                    for e in range(2):
                        for u in dense_halves(e):
                            load(u)
                else:
                    passes(sp, "m", routed, seen)
            sp.wait_ge(S("mm_free"), at)
            sp.dma_start(out.rearrange("a (c p) d -> p (a c) d", p=128), res).then_inc(S("out_written"), 16)
            sp.wait_ge(S("out_written"), 16)

        @block.tensor
        def _(pe):
            cu, tick, ffc = Count(), Count(), Count()
            ident = k1("ident")
            seen = []

            def mm(out, lhsT, rhs, start=True, stop=True):
                return nc.tensor.matmul(out, lhsT, rhs, start=start, stop=stop, skip_group_check=True)

            def turn(out, in_):
                return nc.tensor.transpose(out, in_, ident[0:in_.shape[0], 0:in_.shape[0]])

            def unit():
                n = cu.n
                cu.n += 1
                extra = 0 if cu.i is None else cu.i * (cu.per // 3 * 32)
                pe.wait_ge(S(f"w_loaded{n % 3}"), extra + 32 * (n // 3 + 1))
                return n

            def wproj(n, w, k, c0, c1):
                return WS[:, 2 * (n % 3) + k // 4, (k % 4) * w + c0:(k % 4) * w + c1]

            def wdown(n, k, m):
                return WS[:, 2 * (n % 3) + k // 2, (k % 2) * D + 128 * m:(k % 2) * D + 128 * m + 128]

            def job(stage, i):
                n = START[stage] + i
                assert n == tick.n, (stage, i, n, tick.n)
                tick.n += 1
                if i == 0 and n:
                    pe.wait_ge(S("mm_free"), n)
                elif n >= 4:
                    pe.wait_ge(S("mm_free"), n - 3)
                return P[n % 4]

            fences = [0]

            def fence(last):
                fences[0] += 1
                last.then_inc(S("pe_step"), 1)
                pe.wait_ge(S("pe_step"), fences[0])

            def done(last):
                last.then_inc(S("mm_done"), 1)

            def unit_used():
                pe.wait_ge(S("mm_done"), tick.n)
                pe.sem_inc(S("unit_used"), 1)

            def empty_all():
                pe.wait_ge(S("mm_free"), tick.n)

            def columns(out, n, w, c0, c1, rhs):
                for k in range(KT):
                    last = mm(out, wproj(n, w, k, c0, c1), rhs(k), k == 0, k == KT - 1)
                return last

            def acc(m):
                return P[4 + m // 2][:, 256 * (m % 2):256 * (m % 2) + 256]

            def eight(stage, rhs):
                for u in range(2):
                    n = unit()
                    for j in range(4):
                        b = job(stage, 4 * u + j)
                        done(columns(b[:, 0:N], n, 512, 128 * j, 128 * j + 128, rhs))
                    unit_used()

            def total(stage, i, lhsT, srcs):
                b = job(stage, i)
                for k, s in enumerate(srcs):
                    last = mm(b[:, 0:N], lhsT, s, k == 0, k == len(srcs) - 1)
                done(last)

            pe.wait_ge(S("consts"), 16)
            pe.wait_ge(S("vecs"), 16 * len(a["vec_dmas"]))
            for i in range((NTAB + 3) // 4):
                b = job("tab", i)
                for t in range(4 * i, min(NTAB, 4 * i + 4)):
                    last = turn(b[:, 128 * (t % 4):128 * (t % 4) + 128], vload[:, t, :])
                done(last)
            pe.wait_ge(S("xin"), 32)
            for i in range(8):
                b = job("xin", i)
                which, t = i // 4, 2 * (i % 4)
                for tt in range(2):
                    for c in range(2):
                        last = turn(b[:, 256 * tt + 128 * c:256 * tt + 128 * c + 128],
                                    xload[:, 2 * which + c, 128 * (t + tt):128 * (t + tt) + 128])
                done(last)
            b = job("ss1", 0)
            pe.wait_ge(S("sq1"), 2)
            for k in range(KT):
                last = mm(b[:, :], k1("ones"), hT[:, k, :], k == 0, k == KT - 1)
            done(last)
            pe.wait_ge(S("cs_ready"), 1)

            def turn_mod(u):
                pe.wait_ge(S("mod_row"), u + 1)
                for m in range(4 * u, 4 * u + 4):
                    last = turn(P[4][:, 2 * m:2 * m + 2], modR[0:2, 128 * m:128 * m + 128])
                return last

            for u in range(12):
                n = unit()
                for k in range(KT):
                    last = mm(P[5 + u % 2][0:2, :], cs[:, 2 * k:2 * k + 2], wproj(n, 512, k, 0, 512), k == 0, k == KT - 1)
                last.then_inc(S("unit_used"), 1)
                if u:
                    turn_mod(u - 1)
            turn_mod(11).then_inc(S("mod_done"), 1)
            pe.wait_ge(S("h_ready"), 1)

            def turn_tile(j):
                pe.wait_ge(S("conv_out"), j + 1)
                if j >= 2:
                    pe.wait_ge(S("turn_free"), j - 1)
                for c in range(4):
                    last = turn(P[4 + j % 2][:, 128 * c:128 * c + 128], csil[:, j % 2, 128 * c:128 * c + 128])
                last.then_inc(S("turned"), 1)

            for j in range(32):
                if j % 4 == 0:
                    n = unit()
                b = job("xb", j)
                if j < 24:
                    last = columns(b[:, :], n, 512, 128 * (j % 4), 128 * (j % 4) + 128, lambda k: hT[:, k, :])
                else:
                    last = columns(b[:, 0:N], n, 512, 128 * (j % 4), 128 * (j % 4) + 128, lambda k: hT[:, k, N:2 * N])
                done(last)
                if j % 4 == 3:
                    unit_used()
                if 2 <= j < 26:
                    turn_tile(j - 2)
            n = unit()
            b = job("dt", 0)
            for c in range(4):
                for k in range(KT):
                    last = mm(b[:, 64 * c:64 * c + 64], hT[:, k, 128 * c:128 * c + 128], wproj(n, 64, k, 0, 64),
                              k == 0, k == KT - 1)
            done(last)
            unit_used()
            pe.wait_ge(S("dA_ready"), 1)
            for c in range(4):
                b = job("seg", c)
                for q, (f, r) in enumerate((("TU", "TL"), ("SL", "SU"), ("ones", "ones"))):
                    mm(b[:, 64 * q:64 * q + 32], k1(f), dA[:, c, 0:32])
                    last = mm(b[:, 64 * q + 32:64 * q + 64], k1(r), dA[:, c, 32:64])
                done(last)
            empty_all()
            nx = ns = 0

            def decays(i, nx):
                d, step, c, g = SSD[i]
                tk = slice(128 * (c - 2), 128 * (c - 2) + 128)
                pe.wait_ge(S("A1_ready"), nx + 1)
                if nx:
                    pe.wait_ge(S("CB_ready"), nx)
                    pe.wait_ge(S("EX_ready"), nx)
                mm(P[4][:, 0:128], Bf[:, 4 * d + g, tk], Cf[:, 4 * d + g, tk])
                for h in range(8):
                    last = mm(P[5 + h // 4][:, 128 * (h % 4):128 * (h % 4) + 128], A1[:, 128 * h:128 * h + 128],
                              k1("TL" if d else "TU"))
                last.then_inc(S("seg_done"), 1)

            for i, (d, step, c, g) in enumerate(SSD):
                if step >= 2:
                    tk = slice(128 * (c - 2), 128 * (c - 2) + 128)
                    if SSD[i - 1][1] < 2:
                        decays(i, nx)
                    pe.wait_ge(S("H_ready"), 12 * d + 4 * (step - 1) + g + 1)
                    if nx:
                        pe.wait_ge(S("yo_used"), nx)
                    mm(P[0][:, :], Cf[:, 4 * d + g, tk], H[:, d, g, :]).then_inc(S("yo_done"), 1)
                if step < 3:
                    pe.wait_ge(S("XW_ready"), ns + 1)
                    if ns:
                        pe.wait_ge(S("H_ready"), ns)
                    mm(P[1][:, :], BT[:, c, 512 * d + 128 * g:512 * d + 128 * g + 128], XW).then_inc(S("st_done"), 1)
                    ns += 1
                if step >= 2:
                    if i + 1 < len(SSD) and SSD[i + 1][1] >= 2:
                        decays(i + 1, nx + 1)
                    pe.wait_ge(S("XD_ready"), nx + 1)
                    pe.wait_ge(S("MT_ready"), nx + 1)
                    if nx:
                        pe.wait_ge(S("dg_used"), nx)
                    for h in range(8):
                        last = mm(P[7][:, 64 * h:64 * h + 64], MT[:, 128 * h:128 * h + 128], XD[:, 64 * h:64 * h + 64])
                    last.then_inc(S("dg_done"), 1)
                    nx += 1

            def tokens_wide(stage, units):
                for u in range(units):
                    n = unit()
                    for c in range(2):
                        b = job(stage, 2 * u + c)
                        for k in range(KT):
                            last = mm(b[:, :], hT[:, k, N + 128 * c:N + 128 * c + 128], wproj(n, 512, k, 0, 512),
                                      k == 0, k == KT - 1)
                        done(last)
                    unit_used()

            pe.wait_ge(S("dg_used"), nx)
            tokens_wide("z", 4)
            pe.wait_ge(S("yn_ready"), 1)
            for i in range(8):
                b = job("ytr", i)
                for tt in range(2):
                    for c in range(2):
                        last = turn(b[:, 256 * tt + 128 * c:256 * tt + 128 * c + 128],
                                    Y[:, c, 256 * i + 128 * tt:256 * i + 128 * tt + 128])
                done(last)
            empty_all()
            for u in range(4):
                n = unit()
                for k in range(4):
                    for m in range(8):
                        last = mm(acc(m), wdown(n, k, m), YT[:, 4 * u + k, :],
                                  u == 0 and k == 0 and m % 2 == 0, u == 3 and k == 3)
                last.then_inc(S("unit_used"), 1)
            pe.wait_ge(S("unit_used"), cu.n)
            pe.sem_inc(S("acc_done"), 1)
            eight("gs", lambda k: hT[:, k, N:2 * N])
            tokens_wide("u", 2)
            empty_all()
            for f in range(8):
                b = job("ff1", f)
                for c in range(2):
                    last = mm(b[:, :], U[:, c, 128 * f:128 * f + 128], k1("dft")[:, 512 * c:512 * c + 512], c == 0, c == 1)
                done(last)
            empty_all()
            for i in range(4):
                b = job("ff2", i)
                for q in range(2):
                    mm(b[:, 256 * q:256 * q + 256], k1("dfc"), V_[:, 2 * i + q, 0:256], True, False)
                    last = mm(b[:, 256 * q:256 * q + 256], k1("dfs"), V_[:, 2 * i + q, 256:512], False, True)
                done(last)
            eight("gf", lambda k: hT[:, k, N:2 * N])
            eight("four", lambda k: UT[:, k, :])
            pe.wait_ge(S("mx_ready"), 1)
            eight("wo", lambda k: MX[:, k, :])
            pe.wait_ge(S("squares"), 1)
            total("ss2", 0, k1("ones"), [sc1[:, k, :] for k in range(KT)])

            def router(i, ne, src):
                pe.wait_ge(S("router"), ROUTW[i])
                for c in range(2):
                    b = job(f"rt{i}", c)
                    for k in range(KT):
                        last = mm(b[:, 0:ne], src(k)[:, 128 * c:128 * c + 128], wr[:, k, 0:ne], k == 0, k == KT - 1)
                    done(last)
                for q in range(4):
                    b = job(f"ht{i}", q)
                    for t in range(4):
                        last = turn(b[:, 128 * t:128 * t + 128], src(4 * (q // 2) + t)[:, 128 * (q % 2):128 * (q % 2) + 128])
                    done(last)
                pe.wait_ge(S("w_ready"), i + 1)
                if i == 0:
                    b = job("wT0", 0)
                    for c in range(2):
                        last = turn(b[0:ne, 128 * c:128 * c + 128], wtok[:, c, 0:ne])
                    done(last)
                b = job(f"rkn{i}", 0)
                mm(b[:, 0:ne], k1("TU"), msk[:, 0, 0:ne])
                mm(b[:, 32:32 + ne], k1("ones"), msk[:, 0, 0:ne], True, False)
                mm(b[:, 32:32 + ne], k1("TU"), msk[:, 1, 0:ne], False, True)
                mm(b[:, 64:64 + ne], k1("ones"), msk[:, 0, 0:ne], True, False)
                done(mm(b[:, 64:64 + ne], k1("ones"), msk[:, 1, 0:ne], False, True))

            def open_sum(lhsT, rhs):
                for m in range(8):
                    mm(acc(m), lhsT(m), rhs(m), m % 2 == 0, False)

            def routed(which, p_):
                ne, nf, nu, _ = SPEC[which]
                un, pr, ex = Count(), Count(), Count()

                def unit():
                    n = un.n
                    un.n += 1
                    extra = un.i * (un.per // 6 * 32)
                    p_.wait(pe, f"loaded{n % 6}", extra + 32 * (n // 6 + 1))
                    return n % 6

                def gather():
                    for k in range(KT):
                        o = P[2 + k // 4][:, 128 * (k % 4):128 * (k % 4) + 128]
                        for c in range(2):
                            last = mm(o, xtok[:, c, 128 * k:128 * k + 128], G[:, c, :], c == 0, c == 1)
                    last.then_inc(p_.sem("gathered"), 1)

                pe.sem_inc(p_.sem("used"), 6)
                p_.wait(pe, "G", 1)
                gather()
                for e in turns(pe, which, [(un, nu), (pr, (nf + 1) // 2), (ex, 1)]):
                    x = ex.n
                    p_.wait(pe, "xgA", ex.value(x + 1))
                    p_.wait(pe, "xgB", ex.value(x + 1))
                    for c in range(2):
                        last = turn(P[2][:, 128 * c:128 * c + 128], Gw[:, c, :])
                    last.then_inc(p_.sem("turned"), 1)
                    for u in range((nf + 3) // 4):
                        gs, us = unit(), unit()
                        w = min(512, 128 * nf - 512 * u)
                        for j in range(4 * u, min(4 * u + 4, nf)):
                            p, o = j // 2, 256 * (j % 2)
                            if j % 2 == 0 and p >= 2:
                                p_.wait(pe, "free", pr.value(pr.n - 1))
                            for s_, oo in ((gs, o), (us, o + 128)):
                                for k in range(KT):
                                    c0 = (k % 4) * w + 128 * (j % 4)
                                    last = mm(P[p % 2][:, oo:oo + 128], half(s_, k // 4)[:, c0:c0 + 128], XG[:, k, :],
                                              k == 0, k == KT - 1)
                            if j % 2 or j == nf - 1:
                                last.then_inc(p_.sem("pair"), 1)
                                pr.n += 1
                        p_.wait(pe, "pair", pr.value(pr.n))
                        pe.sem_inc(p_.sem("used"), 2)
                    p_.wait(pe, "G", ex.value(x + 2))
                    p_.wait(pe, "st", ex.value(x + 1))
                    gather()
                    ds = [unit() for _ in range((nf + 3) // 4)]
                    p_.wait(pe, "act", pr.value(pr.n + 2))
                    for n in range(2):
                        for k in range(nf):
                            last = mm(P[n][:, :], acte[:, k, :],
                                      half(ds[k // 4], k % 4 // 2)[:, (k % 2) * D + 512 * n:(k % 2) * D + 512 * n + 512],
                                      k == 0, k == nf - 1)
                        last.then_inc(p_.sem("down"), 1)
                    for n in range(2):
                        p_.wait(pe, "y" + "AB"[n], ex.value(x + 1))
                        if n:
                            pe.sem_inc(p_.sem("used"), len(ds))
                        for m in range(4 * n, 4 * n + 4):
                            last = mm(acc(m), ys[:, 128 * m:128 * m + 128], ST, False, False)
                    last.then_inc(p_.sem("spread"), 1)
                    ex.n += 1
                p_.wait(pe, "spread", ne)
                pe.sem_inc(p_.sem("end"), 1)

            def dense(rhs):
                nf = FFE
                for e in range(2):
                    first = ffc.n
                    for u in range((nf + 1) // 2):
                        n = unit()
                        w = 128 * min(2, nf - 2 * u)
                        for j in range(2 * u, min(2 * u + 2, nf)):
                            if ffc.n >= 4:
                                pe.wait_ge(S("ff_free"), first + j - 3 if j >= 4 else first)
                            for h in range(2):
                                for k in range(KT):
                                    c0 = k * w + 128 * (j % 2)
                                    last = mm(P[j % 4][:, N * h:N * h + N], half(n % 3, h)[:, c0:c0 + 128], rhs(k),
                                              k == 0, k == KT - 1)
                            last.then_inc(S("ff_done"), 1)
                            ffc.n += 1
                        pe.wait_ge(S("ff_done"), ffc.n)
                        pe.sem_inc(S("unit_used"), 1)
                    for u in range((nf + 3) // 4):
                        n = unit()
                        for k in range(min(4, nf - 4 * u)):
                            pe.wait_ge(S("act_ready"), first + 4 * u + k + 1)
                            for m in range(8):
                                last = mm(acc(m), wdown(n, k, m), act[:, 4 * u + k, :], False, False)
                        last.then_inc(S("unit_used"), 1)
                pe.wait_ge(S("unit_used"), cu.n)

            pe.wait_ge(S("h2_ready"), KT)
            router(0, NEXP, lambda k: h2[:, k, :])
            open_sum(lambda m: bdn[0:NEXP, 128 * m:128 * m + 128], lambda m: wTt[0:NEXP, :])
            empty_all()
            passes(pe, "a", routed, seen)
            pe.sem_inc(S("acc_done"), 1)
            pe.wait_ge(S("squares"), 2)
            total("ss3", 0, k1("ones"), [sqb[:, k, :] for k in range(KT)])

            for l in range(2):
                xk = lambda k: xT[:, k, :]
                pe.wait_ge(S("x_ready"), 2 * l + 1)
                for c in range(8):
                    n = unit()
                    c0, w = chunk2(l, c)
                    for i in range(*CHUNKS2[c]):
                        t0, tw = TILES2[i]
                        b = job(f"p{l}", i)
                        done(columns(b[0:tw, 0:N], n, w, t0 - c0, t0 - c0 + tw, xk))
                    unit_used()
                if not l:
                    pe.wait_ge(S("consts2"), 16)
                empty_all()
                pe.wait_ge(S("lay"), LAYW[l])
                b = job(f"gate{l}", 0)
                done(mm(b[:, 0:N], gw2[0:16, :], PT[0:16, 12, :]))
                for n in range(48):
                    u, v0 = n // 16, 4 * (n % 16)
                    pe.wait_ge(S("qS_ready"), 48 * l + n + 1)
                    for j in range(4):
                        v = v0 + j
                        if u < 2:
                            last = mm(P[4][:, 256 * u:256 * u + 256], k2("zH")[:, 63 - v:191 - v], qS[:, n % 2, j, :],
                                      v == 0, v == 63)
                        else:
                            for q in range(2):
                                last = mm(P[5 + q][:, 0:N], k2("zG")[:, 63 - v + 128 * q:191 - v + 128 * q],
                                          qS[:, n % 2, j, :], v == 0, v == 63)
                    last.then_inc(S("qS_used"), 1)
                pe.wait_ge(S("vector_step"), mixed("hsq", l))
                for i in range(4):
                    total(f"hn{l}", i, k1("head"), [g1t[:, i, :]])
                pe.wait_ge(S("tanh_ready"), l + 1)
                for i in range(6):
                    b = job(f"lr{l}", i)
                    t = i % 2
                    cc = slice(128 * t, 128 * t + 128)
                    if i < 2:
                        last = mm(b[:, 0:N], w2s[0:64, cc], PT[0:64, 21, :])
                    elif i < 4:
                        last = mm(b[:, 0:N], w2s[64:128, cc], PT[64:128, 21, :])
                    else:
                        mm(b[:, 0:N], g2a[:, cc], PT[:, 22, :], True, False)
                        last = mm(b[:, 0:N], g2b[0:32, cc], PT[0:32, 23, :], False, True)
                    done(last)
                if l:
                    b = job("vmA1", 0)
                    for t in range(2):
                        last = mm(b[0:32, 0:N], v1s[:, t, :], PT[:, 19 + t, :], t == 0, t == 1)
                    done(last)
                    empty_all()
                    for t in range(2):
                        b = job("vmB1", t)
                        done(mm(b[:, 0:N], v2s[0:32, 128 * t:128 * t + 128], tn[0:32, 0, :]))
                pe.wait_ge(S("vector_step"), mixed("kk_sq", l))
                for t in range(2):
                    total(f"kkn{l}", t, k1("head"), [kks[:, t, :]])
                pe.wait_ge(S("vector_step"), mixed("abk_ready", l))
                for i, src in enumerate((Bt, Kt, vv)):
                    b = job(f"tk{l}", i)
                    for c in range(2):
                        for t in range(2):
                            last = turn(b[:, 256 * c + 128 * t:256 * c + 128 * t + 128], src[:, t, 128 * c:128 * c + 128])
                    done(last)
                for i in range(8):
                    b = job(f"lm{l}", i)
                    h, q = i // 2, i % 2
                    hp, t, tk = slice(64 * (h % 2), 64 * (h % 2) + 64), h // 2, slice(128 * q, 128 * q + 128)
                    for w, src in enumerate((Bt, Kt)):
                        for z in range(2):
                            last = mm(b[:, 256 * w + 128 * z:256 * w + 128 * z + 128], src[hp, t, tk], AR[hp, t, z, tk])
                    done(last)
                for lev in range(LEVELS):
                    v = 2 * (LEVELS * l + lev)
                    for s_ in range(2):
                        pe.wait_ge(S("inv_x"), v + s_ + 1)
                        for i in range(4 * s_, 4 * s_ + 4):
                            last = mm(P[4 + s_][:, 128 * (i % 4):128 * (i % 4) + 128], XI[:, i, :], TI[:, i, :])
                        last.then_inc(S("inv_y"), 1)
                    for s_ in range(2):
                        pe.wait_ge(S("inv_yc"), v + s_ + 1)
                        for i in range(4 * s_, 4 * s_ + 4):
                            mm(P[4 + s_][:, 128 * (i % 4):128 * (i % 4) + 128], TT[:, i, :], YI[:, i, :])
                            last = mm(P[6 + s_][:, 128 * (i % 4):128 * (i % 4) + 128], YI[:, i, :], TT[:, i, :])
                        last.then_inc(S("inv_t"), 1)
                pe.wait_ge(S("vector_step"), mixed("inv_end", l))
                for c in range(4):
                    q, o = c // 2, slice(64 * (c % 2), 64 * (c % 2) + 64)
                    tk, n = slice(64 * c, 64 * c + 64), 4 * l + c
                    pe.wait_ge(S("S_ready"), 5 * l + c + 1)
                    fresh = True
                    for r in range(2):
                        for h in range(4):
                            hp, t, hv = slice(64 * (h % 2), 64 * (h % 2) + 64), h // 2, slice(64 * h, 64 * h + 64)
                            two = [(h % 2, AR[hp, t, 0, tk], Sr[hp, t, :]),
                                   (c % 2, LM[o, 2 * h + q, 256 + 64 * (c % 2):256 + 64 * (c % 2) + 64], tok[o, 2, q, hv])]
                            two = sorted(two, key=lambda x: x[0])
                            for z, (row, lhsT, rhs) in enumerate(two):
                                if row == r:
                                    last = mm(P[4][o, hv], lhsT, rhs, fresh, z == 1)
                                    fresh = False
                        if not r:
                            fence(last)
                    last.then_inc(S("W_done"), 1)
                    pe.wait_ge(S("W_ready"), n + 1)
                    for h in range(4):
                        hv = slice(64 * h, 64 * h + 64)
                        last = mm(P[5][o, hv], TT[o, 2 * h + q, o], Wt[o, hv])
                    last.then_inc(S("U_done"), 1)
                    pe.wait_ge(S("U_ready"), n + 1)
                    fresh = {0, 1}
                    for r in range(2):
                        for h in range(4):
                            hp, t, hv = slice(64 * (h % 2), 64 * (h % 2) + 64), h // 2, slice(64 * h, 64 * h + 64)
                            lo = 64 * (c % 2)
                            three = [(h % 2, Sr[hp, t, :], AR[hp, t, 1, tk]),
                                     (c % 2, Ut[o, hv], LM[o, 2 * h + q, 128 + lo:192 + lo]),
                                     (c % 2, tok[o, 2, q, hv], LM[o, 2 * h + q, 384 + lo:448 + lo])]
                            three = sorted(three, key=lambda x: x[0])
                            for z, (row, lhsT, rhs) in enumerate(three):
                                if row == r:
                                    last = mm(P[6][hp, 256 * t + 64 * c:256 * t + 64 * c + 64], lhsT, rhs,
                                              h % 2 in fresh, z == 2)
                                    fresh -= {h % 2}
                            if c % 2 == r:
                                mm(P[7][hp, 64 * t:64 * t + 64], tok[o, 0, q, hv], Ut[o, hv], t == 0, False)
                                last = mm(P[7][hp, 64 * t:64 * t + 64], tok[o, 1, q, hv], tok[o, 2, q, hv], False, True)
                        if not r:
                            fence(last)
                    last.then_inc(S("SO_done"), 1)
                pe.wait_ge(S("vector_step"), mixed("o_ready", l))
                for t in range(2):
                    total(f"gnA{l}", t, k1("head"), [oT[:, t, :]])
                pe.wait_ge(S("vector_step"), mixed("o_sq", l))
                for t in range(2):
                    total(f"gnB{l}", t, k1("head"), [tm[:, t, :]])
                pe.wait_ge(S("vector_step"), mixed("rkr_ready", l))
                for t in range(2):
                    total(f"rkv{l}", t, k1("head"), [tn[:, t, :]])
                for i in range(4):
                    total(f"rot{l}", i, k2("rot"), [PT[:, 24 + i, :]])
                b = job(f"rv{l}", 0)
                for c in range(2):
                    for t in range(2):
                        last = turn(b[:, 256 * c + 128 * t:256 * c + 128 * t + 128], PT[:, 28 + t, 128 * c:128 * c + 128])
                done(last)
                pe.wait_ge(S("vector_step"), mixed("qk_ready", l))
                for i in range(8):
                    h, q = i // 2, i % 2
                    hp, t = slice(64 * (h % 2), 64 * (h % 2) + 64), h // 2
                    b = job(f"rs{l}", i)
                    done(mm(b[:, 0:256 - 128 * q], qk[hp, 2 + t, 128 * q:128 * q + 128], qk[hp, t, 128 * q:256]))
                empty_all()
                for h in range(4):
                    hp, hv = slice(64 * (h % 2), 64 * (h % 2) + 64), slice(64 * h, 64 * h + 64)
                    b = job(f"ro{l}", h)
                    mm(b[hp, 0:256], vtk[:, 0, hv], sc[:, h, 0:256], True, False)
                    done(mm(b[hp, 128:256], vtk[:, 1, hv], sc[:, h, 256:384], False, True))
                empty_all()
                for t in range(2):
                    total(f"rnA{l}", t, k1("head"), [ro[:, t, :]])
                pe.wait_ge(S("vector_step"), mixed("rc_sq", l))
                for t in range(2):
                    total(f"rnB{l}", t, k1("head"), [rq[:, t, :]])
                pe.wait_ge(S("vector_step"), mixed("mix_ready", l))
                eight(f"out{l}", lambda k: mixT[:, k, :])
                empty_all()
                total(f"laA{l}", 0, k1("ones"), [xT[:, k, :] for k in range(KT)])
                pe.wait_ge(S("squares"), 3 + 2 * l)
                total(f"laB{l}", 0, k1("ones"), [sqb[:, k, :] for k in range(KT)])
                pe.wait_ge(S("x_ready"), 2 * l + 2)
                if l:
                    router(1, 8, xk)
                empty_all()
                open_sum(lambda m: k2("alpha"), lambda m: xT[:, m, :])
                if l:
                    fence(mm(P[0][0:1, 0:1], ident[:, 0:1], ident[:, 0:1]))
                    passes(pe, "m", routed, seen)
                else:
                    dense(xk)
                pe.sem_inc(S("acc_done"), 1)
                pe.wait_ge(S("r_ready"), l + 1)
                total(f"lbA{l}", 0, k1("ones"), [xT[:, k, :] for k in range(KT)])
                pe.wait_ge(S("squares"), 4 + 2 * l)
                total(f"lbB{l}", 0, k1("ones"), [sqb[:, k, :] for k in range(KT)])
            pe.wait_ge(S("x_ready"), 5)
            for i in range(8):
                b = job("fin", i)
                for t in range(2):
                    last = turn(b[:, 128 * t:128 * t + 128], xT[:, 2 * (i % 4) + t, 128 * (i // 4):128 * (i // 4) + 128])
                done(last)

        def twice(c, n):
            return 2 * n if c.i is None else c.i * (2 * c.per) + 2 * n

        def marker(eng):
            counts = {}

            def mark(ins, name):
                c = counts.setdefault(name, Count())
                c.n += 1
                ins.then_inc(S(name), 1)
                eng.wait_ge(S(name), c.value(c.n))
            return mark, counts

        @block.vector
        def _(dve):
            mark, counts = marker(dve)
            seen = []
            v = nc.vector
            roots = [0]

            def V(ins):
                mark(ins, "dve")

            def F(n, ins):
                ins.then_inc(S("mm_free"), 1)
                dve.wait_ge(S("mm_free"), n + 1)

            def ready(stage, i=0):
                n = START[stage] + i
                dve.wait_ge(S("mm_done"), n + 1)
                return n, P[n % 4]

            def tt(out, a_, b_, op=ALU.mult):
                return v.tensor_tensor(out=out, in0=a_, in1=b_, op=op)

            def ts(out, in_, s1, s2, op0=ALU.mult, op1=ALU.add):
                return v.tensor_scalar(out, in_, s1, s2, op0, op1)

            def stt(out, in0, s, in1, op0=ALU.mult, op1=ALU.mult):
                return v.scalar_tensor_tensor(out=out, in0=in0, scalar=s, in1=in1, op0=op0, op1=op1)

            def flat(x):
                return x.rearrange("p a b -> p (a b)")

            def rsqrt(x):
                roots[0] += 1
                mark(v.memset(st[:, 15:16], 0.0), "to_root")
                dve.wait_ge(S("rooted"), roots[0])
                V(v.reciprocal(x, x))

            def over(k, x):
                return x.unsqueeze(1).to_broadcast([128, k, x.shape[1]])

            v.memset(vload, 0.0).then_inc(S("vload_zero"), 1)
            V(v.memset(st, 0.0))
            for i in range((NTAB + 3) // 4):
                n, b = ready("tab", i)
                w = 128 * min(4, NTAB - 4 * i)
                F(n, v.tensor_copy(VC[:, 512 * i:512 * i + w], b[:, 0:w]))
            cs3 = cs.rearrange("p (k w) -> p k w", w=2)
            dve.wait_ge(S("sil"), 2)
            V(tt(cs3[:, :, 0], cs3[:, :, 0], col("c", 0, 8)))
            mark(tt(cs3[:, :, 1], cs3[:, :, 1], col("c_ctx", 0, 8)), "cs_ready")
            cT = reg(16384, KT, N)
            for i in range(8):
                n, b = ready("xin", i)
                t = 2 * (i % 4)
                dst = (cT, xT)[i // 4]
                F(n, v.tensor_copy(dst[:, t:t + 2, :], b[:, :].rearrange("p (t n) -> p t n", t=2)))
            mark(tt(hT[:, :, 0:N], cT, cT), "sq1")
            mark(tt(hT[:, :, N:2 * N], xT[:, :, :], xT[:, :, :]), "sq1")
            n, b = ready("ss1")
            F(n, ts(inv, b[:, :], 1.0 / D, 1e-6))
            rsqrt(inv)
            for u in range(12):
                dve.wait_ge(S("unit_used"), u + 1)
                mark(v.tensor_copy(modR[0:2, 512 * u:512 * u + 512], P[5 + u % 2][0:2, :]), "mod_row")
            dve.wait_ge(S("mod_done"), 1)
            V(tt(modT[:, :, :], P[4][:, 0:96].rearrange("p (m w) -> p m w", w=2),
                 col("b_mod", 0, 48).unsqueeze(2).to_broadcast([128, 48, 2]), ALU.add))
            for w in range(2):
                V(stt(n1s[:, 8 * w:8 * w + 8], modT[:, 8:16, w], 1.0, col("norm1_w", 0, 8), ALU.add, ALU.mult))
            for w, src, o in ((1, cT, 0), (0, xT, N)):
                for k in range(KT):
                    V(stt(hT[:, k, o:o + N], src[:, k, :], n1s[:, 8 * w + k:8 * w + k + 1], inv[:, o:o + N]))
                    ins = ts(hT[:, k, o:o + N], hT[:, k, o:o + N], modT[:, k, w:w + 1], None, ALU.add, ALU.bypass)
                    if (w, k) == (0, KT - 1):
                        mark(ins, "h_ready")
                    else:
                        V(ins)
            for j in range(32 + 2):
                if j < 32:
                    sl = slice(0, 2) if j < 24 else slice(1, 2)
                    dve.wait_ge(S("mm_free"), START["xb"] + j + 1)
                    r = craw[:, j % 2]
                    ca = cacc[:, j % 2, :].rearrange("p (s n) -> p s n", s=2)[:, sl, :]
                    V(ts(ca, r[:, sl, 0:N], col("conv_w", j), col("conv_b", j)))
                    for tap in range(1, 5):
                        ins = stt(ca, r[:, sl, tap:tap + N], col("conv_w", 32 * tap + j), ca, ALU.mult, ALU.add)
                        if tap < 4:
                            V(ins)
                        else:
                            mark(ins, "conv_done")
                if 1 <= j <= 32:
                    i = j - 1
                    dve.wait_ge(S("conv_sig"), i + 1)
                    c2, s2 = cacc[:, i % 2, :], csil[:, i % 2, :]
                    if i < 16:
                        mark(tt(s2, c2, s2), "conv_out")
                    elif i < 24:
                        V(tt(s2, c2, s2))
                        mark(v.tensor_copy(Bf[:, i - 16, :], s2[:, N:2 * N]), "conv_out")
                    else:
                        mark(tt(Cf[:, i - 24, :], c2[:, N:2 * N], s2[:, N:2 * N]), "conv_out")
                if 2 <= j < 26:
                    i = j - 2
                    dve.wait_ge(S("turned"), i + 1)
                    dst = XT[:, :, 128 * i:128 * i + 128] if i < 16 else BT[:, :, 128 * (i - 16):128 * (i - 16) + 128]
                    mark(v.tensor_copy(dst, P[4 + i % 2][:, :].rearrange("p (c n) -> p c n", c=4)), "turn_free")
            dve.wait_ge(S("rows"), 48)
            n, b = ready("dt")
            F(n, tt(dtt, b[:, 0:256].rearrange("p (c h) -> p c h", c=4), over(4, dtb[:, :]), ALU.add))
            mark(stt(dA, dtt, -1.0, dtt, ALU.mult, ALU.max), "abs")
            dve.wait_ge(S("exp_neg"), 1)
            mark(ts(dA, dA, 1.0, None, ALU.add, ALU.bypass), "one_more")
            dve.wait_ge(S("ln"), 1)
            V(stt(dtt, dtt, 0.0, dA, ALU.max, ALU.add))
            V(ts(av, av, -1.0, None, ALU.mult, ALU.bypass))
            mark(tt(dA, dtt, over(4, av)), "dA_ready")
            dve.wait_ge(S("mm_free"), START["seg"] + 4)
            mark(tt(wst, dtt, ea[:, :, 64:128]), "wst_ready")
            nx = ns = 0
            dve.wait_ge(S("Y_init"), 2)
            for d, step, c, g in SSD:
                hs = slice(32 * d + 8 * g, 32 * d + 8 * g + 8)
                yg = Y[:, c - 2, 512 * g:512 * g + 512] if step >= 2 else None
                if step >= 2:
                    dve.wait_ge(S("seg_done"), nx + 1)
                    mark(tt(CBm, P[4][:, 0:128], k1("TL" if d else "TU")), "CB_ready")
                    dve.wait_ge(S("EX_ready"), nx + 1)
                    if nx:
                        dve.wait_ge(S("dg_done"), nx)
                    mark(tt(MT.rearrange("p (h l) -> p h l", h=8), EX.rearrange("p (h l) -> p h l", h=8), over(8, CBm)),
                         "MT_ready")
                    dve.wait_ge(S("yo_done"), nx + 1)
                    mark(tt(YO.rearrange("p (h e) -> p h e", h=8), P[0][:, :].rearrange("p (h e) -> p h e", h=8),
                            ea[:, c, hs].unsqueeze(2).to_broadcast([128, 8, 64])), "yo_used")
                    V(tt(yg, yg, YO, ALU.add))
                if step < 3:
                    dve.wait_ge(S("st_done"), ns + 1)
                    if step == 0:
                        mark(v.tensor_copy(H[:, d, g, :], P[1][:, :]), "H_ready")
                    else:
                        hv = H[:, d, g, :].rearrange("p (h e) -> p h e", h=8)
                        V(tt(hv, hv, ea[:, c, 128 + 32 * d + 8 * g:128 + 32 * d + 8 * g + 8].unsqueeze(2)
                             .to_broadcast([128, 8, 64])))
                        mark(tt(H[:, d, g, :], H[:, d, g, :], P[1][:, :], ALU.add), "H_ready")
                    ns += 1
                if step >= 2:
                    dve.wait_ge(S("dg_done"), nx + 1)
                    mark(tt(yg, yg, P[7][:, :], ALU.add), "dg_used")
                    nx += 1
            for i in range(8):
                n, b = ready("z", i)
                u, c = i // 2, i % 2
                dve.wait_ge(S("z_sig"), i + 1)
                F(n, tt(zs[:, i % 2, :], zs[:, i % 2, :], b[:, :]))
                yc = Y[:, c, 512 * u:512 * u + 512]
                mark(tt(yc, yc, zs[:, i % 2, :]), "z_used")
            dve.wait_ge(S("y_sq"), 2)
            V(ts(st[:, 0:2], st[:, 0:2], 1.0 / D_IN, 1e-6))
            rsqrt(st[:, 0:2])
            V(ts(Y[:, 0, :], Y[:, 0, :], st[:, 0:1], None, ALU.mult, ALU.bypass))
            mark(ts(Y[:, 1, :], Y[:, 1, :], st[:, 1:2], None, ALU.mult, ALU.bypass), "yn_ready")
            for i in range(8):
                n, b = ready("ytr", i)
                V(ts(YT[:, 2 * i, :], b[:, 0:N], col("ssd_norm_w", 2 * i), None, ALU.mult, ALU.bypass))
                F(n, ts(YT[:, 2 * i + 1, :], b[:, N:2 * N], col("ssd_norm_w", 2 * i + 1), None, ALU.mult, ALU.bypass))
            dve.wait_ge(S("mm_free"), START["gs"] + 8)
            dve.wait_ge(S("acc_done"), 1)
            for i in range(4):
                ins = tt(MX[:, 2 * i:2 * i + 2, :], P[4 + i][:, :].rearrange("p (t n) -> p t n", t=2), GT[:, 2 * i:2 * i + 2, :])
                if i < 3:
                    V(ins)
                else:
                    mark(ins, "mx_ssd")
            for f in range(8):
                n, b = ready("ff1", f)
                F(n, v.tensor_copy(V_[:, f, :], b[:, :]))
            for i in range(4):
                n, b = ready("ff2", i)
                F(n, v.tensor_copy(UT[:, 2 * i:2 * i + 2, :], b[:, :].rearrange("p (t n) -> p t n", t=2)))
            dve.wait_ge(S("mm_free"), START["gf"] + 8)
            for m in range(8):
                n, b = ready("four", m)
                F(n, tt(zs[:, m % 2, 0:N], b[:, 0:N], GT[:, m, :]))
                ins = tt(MX[:, m, :], MX[:, m, :], zs[:, m % 2, 0:N], ALU.add)
                if m < 7:
                    V(ins)
                else:
                    mark(ins, "mx_ready")
            for m in range(8):
                n, b = ready("wo", m)
                F(n, stt(xT[:, m, :], b[:, 0:N], modT[:, 16 + m, 0:1], xT[:, m, :], ALU.mult, ALU.add))
            iv = inv[:, 0:N]
            mark(tt(sc1, xT[:, :, :], xT[:, :, :]), "squares")
            n, b = ready("ss2")
            F(n, ts(iv, b[:, 0:N], 1.0 / D, 1e-6))
            rsqrt(iv)
            V(stt(n1s[:, 0:8], modT[:, 32:40, 0], 1.0, col("norm2_w", 0, 8), ALU.add, ALU.mult))
            for k in range(KT):
                V(stt(h2[:, k, :], xT[:, k, :], n1s[:, k:k + 1], iv))
                mark(ts(h2[:, k, :], h2[:, k, :], modT[:, 24 + k, 0:1], None, ALU.add, ALU.bypass), "h2_ready")

            def router(i, ne, topk):
                dve.wait_ge(S("router"), ROUTW[i])
                gt, eq, pre, s = rt[:, 0, 0:ne], rt[:, 1, 0:ne], rt[:, 2, 0:ne], rt[:, 3, :]
                top = rt[:, 4, 0:8]
                for c in range(2):
                    n, b = ready(f"rt{i}", c)
                    F(n, tt(lgs[:, c, 0:ne], b[:, 0:ne], rb[:, 0:ne], ALU.add) if i == 0
                      else v.tensor_copy(lgs[:, c, 0:ne], b[:, 0:ne]))
                for c in range(2):
                    lg, e_ = lgs[:, c, 0:ne], rt[:, 5 + c, 0:ne]
                    V(v.max(out=top, in_=lg))
                    mark(ts(s[:, 8 * c:8 * c + 1], top[:, 0:1], -1.0, None, ALU.mult, ALU.bypass), "lg_ready")
                    V(ts(gt, lg, top[:, topk - 1:topk], None, ALU.is_gt, ALU.bypass))
                    V(ts(eq, lg, top[:, topk - 1:topk], None, ALU.is_equal, ALU.bypass))
                    V(v.reduce_sum(s[:, 1:2], gt, mybir.AxisListType.X))
                    V(ts(s[:, 1:2], s[:, 1:2], -1.0, float(topk)))
                    V(v.tensor_tensor_scan(pre, k1("ones")[:, 0:ne], eq, 0.0, ALU.mult, ALU.add))
                    V(ts(pre, pre, s[:, 1:2], None, ALU.is_le, ALU.bypass))
                    V(tt(pre, pre, eq))
                    V(tt(msk[:, c, 0:ne], gt, pre, ALU.add))
                    dve.wait_ge(S("lg_exp"), 2 * i + c + 1)
                    V(tt(gt, msk[:, c, 0:ne], e_))
                    V(v.reduce_sum(s[:, 2:3], gt, mybir.AxisListType.X))
                    V(v.reciprocal(s[:, 2:3], s[:, 2:3]))
                    ins = ts(wtok[:, c, 0:ne], gt, s[:, 2:3], None, ALU.mult, ALU.bypass)
                    if c:
                        mark(ins, "w_ready")
                    else:
                        V(ins)
                if i == 0:
                    n, b = ready("wT0")
                    F(n, v.tensor_copy(wTt[0:ne, :], b[0:ne, 0:N]))
                V(v.memset(keys, -512.0))
                V(v.memset(kw, 0.0))
                n, b = ready(f"rkn{i}")
                for c in range(2):
                    V(tt(keys[:, 33 * c:33 * c + ne], b[:, 32 * c:32 * c + ne], msk[:, c, 0:ne]))
                    V(ts(keys[:, 33 * c:33 * c + ne], keys[:, 33 * c:33 * c + ne], -1.0, None, ALU.add, ALU.bypass))
                    V(v.tensor_copy(kw[:, 33 * c:33 * c + ne], wtok[:, c, 0:ne]))
                F(n, v.reduce_max(s[:, 3:4], b[:, 64:64 + ne], mybir.AxisListType.X))
                mark(ts(flags[:, i:i + 1], s[:, 3:4], float(CAP), None, ALU.is_gt, ALU.bypass), "cnt_ready")

            def routed(which, p_):
                ne, nf, _, _ = SPEC[which]
                pr, ex, c1 = Count(), Count(), Count()

                def Vr(ins):
                    c1.n += 1
                    ins.then_inc(p_.sem("dve"), 1)
                    p_.wait(dve, "dve", c1.value(c1.n))

                def sig(ins, name):
                    ins.then_inc(p_.sem(name), 1)

                def choose(e):
                    for c in range(2):
                        key, w = keys[:, bass.ds(e + 33 * c, 1)], kw[:, bass.ds(e + 33 * c, 1)]
                        Vr(ts(G[:, c, :], k1("iota"), key, None, ALU.is_equal, ALU.bypass))
                        last = ts(Gw[:, c, :], k1("iota"), key, w, ALU.is_equal, ALU.mult)
                        if c == 0:
                            Vr(last)
                    sig(last, "G")

                if p_.second:
                    Vr(ts(keys, keys, -float(CAP), None, ALU.add, ALU.bypass))
                for c in range(2):
                    Vr(ts(G[:, c, :], k1("iota"), keys[:, 33 * c:33 * c + 1], None, ALU.is_equal, ALU.bypass))
                    last = ts(Gw[:, c, :], k1("iota"), keys[:, 33 * c:33 * c + 1], kw[:, 33 * c:33 * c + 1],
                              ALU.is_equal, ALU.mult)
                    if c == 0:
                        Vr(last)
                sig(last, "G")
                p_.wait(dve, "gathered", 1)
                sig(v.tensor_copy(XG[:, 0:4, :], P[2][:, :].rearrange("p (k n) -> p k n", k=4)), "xgA")
                for e in turns(dve, which, [(pr, (nf + 1) // 2), (ex, 1), (c1, own_steps(which))]):
                    x = ex.n
                    p_.wait(dve, "turned", ex.value(x + 1))
                    sig(v.tensor_copy(ST, P[2][:, 0:N]), "st")
                    if which == "a":
                        dve.wait_ge(S("cnt_ready"), 1)
                        Vr(v.tensor_copy(bge, VC[:, bass.ds(e * 16 + COL["b_gate_up"], 16)]))
                    choose(e + 1)
                    for p in range((nf + 1) // 2):
                        b = P[p % 2][:, :].rearrange("p (t w n) -> p t w n", t=2, w=2)
                        nt = min(2, nf - 2 * p)
                        g3 = gl[:, p % 2, :].rearrange("p (t n) -> p t n", t=2)
                        u3 = ul[:, p % 2, :].rearrange("p (t n) -> p t n", t=2)
                        p_.wait(dve, "pair", pr.value(pr.n + 1))
                        p_.wait(dve, "act", pr.value(pr.n + 1))
                        if which == "a":
                            for t in range(2):
                                j = 2 * p + t
                                Vr(ts(g3[:, t, :], b[:, t, 0, :], bge[:, j:j + 1], 7.0, ALU.add, ALU.min))
                                Vr(ts(u3[:, t, :], b[:, t, 1, :], bge[:, 8 + j:9 + j], -7.0, ALU.add, ALU.max))
                            last = ts(ul[:, p % 2, :], ul[:, p % 2, :], 7.0, 1.0, ALU.min, ALU.add)
                        else:
                            Vr(v.tensor_copy(g3[:, 0:nt, :], b[:, 0:nt, 0, :]))
                            last = v.tensor_copy(u3[:, 0:nt, :], b[:, 0:nt, 1, :])
                        sig(last, "free")
                        pr.n += 1
                    p_.wait(dve, "gathered", ex.value(x + 2))
                    sig(v.tensor_copy(XG[:, 0:4, :], P[2][:, :].rearrange("p (k n) -> p k n", k=4)), "xgA")
                    p_.wait(dve, "down", twice(ex, x) + 1)
                    sig(v.tensor_copy(ys[:, 0:512], P[0][:, :]), "yA")
                    ex.n += 1

            ffc = Count()

            def dense():
                for e in range(2):
                    for j in range(FFE):
                        b = P[j % 4]
                        n = ffc.n
                        dve.wait_ge(S("ff_done"), n + 1)
                        if n >= 2:
                            dve.wait_ge(S("act_ready"), n - 1)
                        V(v.tensor_copy(gl[:, j % 2, :], b[:, 0:N]))
                        mark(v.tensor_copy(ul[:, j % 2, :], b[:, N:2 * N]), "ff_free")
                        ffc.n += 1

            router(0, NEXP, TOPK)
            passes(dve, "a", routed, seen)
            dve.wait_ge(S("acc_done"), 2)
            for m in range(8):
                b = P[4 + m // 2][:, N * (m % 2):N * (m % 2) + N]
                V(stt(xT[:, m, :], b, modT[:, 40 + m, 0:1], xT[:, m, :], ALU.mult, ALU.add))
            mark(tt(sqb, xT[:, :, :], xT[:, :, :]), "squares")
            n, b = ready("ss3")
            F(n, ts(iv, b[:, 0:N], 1.0 / D, 1e-6))
            rsqrt(iv)
            for k in range(KT):
                ins = stt(xT[:, k, :], xT[:, k, :], col("final_norm_w", k), iv)
                if k < KT - 1:
                    V(ins)
                else:
                    mark(ins, "x_ready")

            def layer_norm(sa, sb_, g, bb):
                n, b = ready(sa)
                F(n, ts(iv, b[:, 0:N], 1.0 / D, None, ALU.mult, ALU.bypass))
                V(tt(xc, xT[:, :, :], over(KT, iv), ALU.subtract))
                mark(tt(sqb, xc, xc), "squares")
                n, b = ready(sb_)
                F(n, ts(iv, b[:, 0:N], 1.0 / D, 1e-5))
                rsqrt(iv)
                for k in range(KT):
                    V(stt(xT[:, k, :], xc[:, k, :], col(*g(k)), iv))
                    ins = ts(xT[:, k, :], xT[:, k, :], col(*bb(k)), None, ALU.add, ALU.bypass)
                    if k < KT - 1:
                        V(ins)
                    else:
                        mark(ins, "x_ready")

            for l in range(2):
                if not l:
                    dve.wait_ge(S("positions"), 16)
                    dve.wait_ge(S("consts2"), 16)
                a0, a1, a2 = ang[:, 0, :], ang[:, 1, :], ang[:, 2, :]
                V(v.tensor_copy(a0, posi))
                V(ts(a0, a0, k2("inv"), None, ALU.mult, ALU.bypass))
                V(ts(a1, a0, float(1 / (2 * np.pi)), 12582912.0))
                V(ts(a1, a1, -12582912.0, None, ALU.add, ALU.bypass))
                c1 = 6.28125
                c2 = float(np.float32(2 * np.pi - c1))
                V(stt(a0, a1, -c1, a0, ALU.mult, ALU.add))
                V(stt(a0, a1, -c2, a0, ALU.mult, ALU.add))
                mark(ts(a2, a0, 3.1415925, -3.1415925, ALU.min, ALU.max), "vector_step")
                dve.wait_ge(S("mm_free"), START[f"p{l}"] + 24)
                dif = reg(B0 + 5632, 8, N)
                V(tt(dif[:, :, 1:N], PT[:, 15:23, 0:N - 1], PT[:, 15:23, 1:N], ALU.subtract))
                V(ts(dif[:, :, 0:1], PT[:, 15:23, 0:1], -1.0, None, ALU.mult, ALU.bypass))
                for i in range(8):
                    V(stt(PT[:, 15 + i, :], dif[:, i, :], col(f"mu{l}", i), PT[:, 15 + i, :], ALU.mult, ALU.add))
                p9, d9 = PT[0:32, 23, :], dif[0:32, 0, :]
                V(tt(d9[:, 1:N], p9[:, 0:N - 1], p9[:, 1:N], ALU.subtract))
                V(ts(d9[:, 0:1], p9[:, 0:1], -1.0, None, ALU.mult, ALU.bypass))
                mark(stt(p9, d9, col("mus", l)[0:32], p9, ALU.mult, ALU.add), "vector_step")
                dve.wait_ge(S("hsig"), l + 1)
                V(tt(qT[:, 0:2, :], qT[:, 0:2, :], PT[:, 0:2, :]))
                if l:
                    V(tt(lbc[:, 0:2], col("hgrn_lb_logits_2", 2, 2), col("hgrn_lb_logits_2", 0, 2), ALU.subtract))
                    mark(v.memset(st[:, 14:15], 0.0), "lb_diff")
                    dve.wait_ge(S("lb_sig"), 1)
                    V(ts(lbc[:, 2:4], lbc[:, 0:2], -1.0, 1.0))
                    for t in range(2):
                        V(ts(fT[:, t, :], fT[:, t, :], lbc[:, 2 + t:3 + t], lbc[:, t:t + 1]))
                V(ts(kT[:, 0:2, :], fT[:, 0:2, :], -1.0, 1.0))
                V(v.tensor_copy(kT[:, 2, :], PT[:, 9, :]))
                V(ts(qT[:, 2, :], PT[:, 8, :], 32.0 ** -0.5, None, ALU.mult, ALU.bypass))
                n, b = ready(f"gate{l}")
                ga_, gb_ = g1t[:, 0, :], g1t[:, 1, :]
                F(n, ts(ga_, b[:, 0:N], col("gla_gate_b_2", l), None, ALU.add, ALU.bypass))
                mark(stt(gb_, ga_, -1.0, ga_, ALU.mult, ALU.max), "abs")
                dve.wait_ge(S("exp_neg"), l + 2)
                mark(ts(gb_, gb_, 1.0, None, ALU.add, ALU.bypass), "one_more")
                dve.wait_ge(S("ln"), l + 2)
                mark(stt(ga_, ga_, 0.0, gb_, ALU.min, ALU.subtract), "ga_log")
                dve.wait_ge(S("ga_f"), l + 1)
                mark(v.memset(fT[:, :, 0:1], 0.0), "kT_ready")
                for n in range(48):
                    m = 48 * l + n
                    u = n // 16
                    if n % 16 == 0:
                        V(v.tensor_copy(f4.rearrange("p (j n) -> p j n", j=4), over(4, fT[:, u, :])))
                    dve.wait_ge(S("kv_done"), m + 1)
                    mark(v.tensor_tensor_scan(St[:, n % 2].rearrange("p j n -> p (j n)"), f4,
                                              kv[:, n % 2].rearrange("p j n -> p (j n)"), 0.0, ALU.mult, ALU.add), "scan_done")
                    if m >= 2:
                        dve.wait_ge(S("qS_used"), m - 1)
                    mark(tt(qS[:, n % 2], St[:, n % 2], over(4, qT[:, u, :])), "qS_ready")
                dve.wait_ge(S("qS_used"), 48 * (l + 1))
                V(v.tensor_copy(g2t[:, 0:2, :], P[4][:, :].rearrange("p (t n) -> p t n", t=2)))
                V(v.tensor_copy(g2t[:, 2, :], P[5][:, 0:N]))
                V(v.tensor_copy(g2t[:, 3, :], P[6][:, 0:N]))
                mark(tt(g1t, g2t, g2t), "vector_step")
                for i in range(4):
                    n, b = ready(f"hn{l}", i)
                    F(n, ts(hr4[:, i, :], b[:, 0:N], 1e-6, None, ALU.add, ALU.bypass))
                rsqrt(flat(hr4))
                dve.wait_ge(S("hg_sig"), l + 1)
                V(tt(hg[:, 0:2, :], hg[:, 0:2, :], PT[:, 6:8, :]))
                V(tt(hg[:, 2:4, :], hg[:, 2:4, :], PT[:, 13:15, :]))
                V(tt(hg, hg, hr4))
                for i in range(4):
                    V(stt(mixT[:, i, :], g2t[:, i, :], col("hgrn_norm_g_2" if i < 2 else "gla_norm_g_2", l), hg[:, i, :]))
                for i in range(6):
                    n, b = ready(f"lr{l}", i)
                    t = i % 2
                    if i < 2:
                        F(n, ts(tm[:, t, :], b[:, 0:N], col("rwkv_w0_2", 2 * l + t), None, ALU.add, ALU.bypass))
                    elif i < 4:
                        F(n, ts(ga[:, t, :], b[:, 0:N], col("rwkv_a0_2", 2 * l + t), None, ALU.add, ALU.bypass))
                    else:
                        F(n, v.tensor_copy(mixT[:, 4 + t, :], b[:, 0:N]))
                mark(v.memset(st[:, 14:15], 0.0), "vector_step")
                if l:
                    n, b = ready("vmA1")
                    F(n, v.tensor_copy(tn[0:32, 0, :], b[0:32, 0:N]))
                    for t in range(2):
                        n, b = ready("vmB1", t)
                        F(n, ts(vv[:, t, :], b[:, 0:N], col("rwkv_v0_2", t), None, ALU.add, ALU.bypass))
                    mark(tt(t3, vfk, PT[:, 19:21, :], ALU.subtract), "vector_step")
                    dve.wait_ge(S("vm_sig"), 1)
                    V(tt(vv, vv, t3))
                    V(tt(vv, vv, PT[:, 19:21, :], ALU.add))
                else:
                    V(v.tensor_copy(vv, PT[:, 19:21, :]))
                    mark(v.tensor_copy(vfk, PT[:, 19:21, :]), "vector_step")
                for t in range(2):
                    V(ts(kkr[:, t, :], PT[:, 17 + t, :], col("rwkv_k_k_2", 2 * l + t), None, ALU.mult, ALU.bypass))
                mark(tt(kks, kkr, kkr), "vector_step")
                for t in range(2):
                    n, b = ready(f"kkn{l}", t)
                    F(n, ts(t3[:, t, :], b[:, 0:N], 64.0, 1e-24, ALU.mult, ALU.max))
                rsqrt(flat(t3))
                V(tt(kkr, kkr, t3))
                dve.wait_ge(S("wa_sig"), l + 1)
                V(ts(tm, tm, -float(np.exp(-0.5)), None, ALU.mult, ALU.bypass))
                for t in range(2):
                    ins = v.tensor_tensor_scan(tn[:, t, :], k2("keep"), tm[:, t, :], 0.0, ALU.mult, ALU.add)
                    if t:
                        mark(ins, "vector_step")
                    else:
                        V(ins)
                dve.wait_ge(S("cum_exp"), l + 1)
                mark(tt(tn, tn, tm, ALU.subtract), "vector_step")
                for t in range(2):
                    V(ts(t4[:, t, :], ga[:, t, :], -1.0, col("rwkv_k_a_2", 2 * l + t), ALU.add, ALU.mult))
                V(stt(kp, t4, 1.0, PT[:, 17:19, :], ALU.add, ALU.mult))
                V(tt(t4, kkr, ga))
                V(tt(Kt, kp, Bt))
                V(tt(Bt, t4, Bt))
                V(tt(AR[:, :, 1, :], PT[:, 15:17, :], cl))
                dve.wait_ge(S("prev_exp"), l + 1)
                V(stt(AR[:, :, 0, :], kkr, -1.0, tm))
                for t in range(2):
                    ins = stt(tn[:, t, :], PT[:, 15 + t, :], col("rwkv_r_k_2", 2 * l + t), kp[:, t, :])
                    V(ins)
                V(v.memset(Sr, 0.0))
                mark(v.memset(st[:, 14:15], 0.0), "vector_step")
                for i in range(3):
                    n, b = ready(f"tk{l}", i)
                    F(n, v.tensor_copy(tok[:, i], b[:, :].rearrange("p (c n) -> p c n", c=2)))
                for i in range(8):
                    n, b = ready(f"lm{l}", i)
                    F(n, tt(LM[:, i, :], b[:, :], k2("rwm")))
                V(v.tensor_copy(TI, over(8, k1("ident"))))
                V(v.tensor_copy(TT, over(8, k1("ident"))))
                for lev in range(LEVELS + 1):
                    m = 2 * (LEVELS * l + lev)
                    for s_ in range(2):
                        four = slice(4 * s_, 4 * s_ + 4)
                        if lev < LEVELS:
                            if lev:
                                dve.wait_ge(S("inv_y"), m + s_ - 1)
                            x_ = tt(XI[:, four, :], LM[:, four, 0:128], over(4, k2("lev")[:, 128 * lev:128 * lev + 128]))
                            if lev:
                                V(x_)
                            else:
                                mark(x_, "inv_x")
                        if lev:
                            dve.wait_ge(S("inv_t"), m + s_ - 1)
                            V(tt(TI[:, four, :], TI[:, four, :], P[4 + s_][:, :].rearrange("p (h n) -> p h n", h=4), ALU.add))
                            t_ = tt(TT[:, four, :], TT[:, four, :], P[6 + s_][:, :].rearrange("p (h n) -> p h n", h=4), ALU.add)
                            if lev < LEVELS:
                                mark(t_, "inv_x")
                            else:
                                V(t_)
                mark(v.memset(st[:, 14:15], 0.0), "vector_step")
                mark(v.memset(st[:, 14:15], 0.0), "S_ready")
                for c in range(4):
                    dve.wait_ge(S("SO_done"), 4 * l + c + 1)
                    V(tt(flat(Sr), flat(Sr), P[7][:, 0:128], ALU.add))
                    V(ts(Sr[:, 0, :], Sr[:, 0, :], cl[:, 0, 64 * c + 63:64 * c + 64], None, ALU.mult, ALU.bypass))
                    mark(ts(Sr[:, 1, :], Sr[:, 1, :], cl[:, 1, 64 * c + 63:64 * c + 64], None, ALU.mult, ALU.bypass), "S_ready")
                mark(v.tensor_copy(flat(oT), P[6][:, :]), "vector_step")
                for t in range(2):
                    n, b = ready(f"gnA{l}", t)
                    F(n, tt(oT[:, t, :], oT[:, t, :], b[:, 0:N], ALU.subtract))
                mark(tt(tm, oT, oT), "vector_step")
                for t in range(2):
                    n, b = ready(f"gnB{l}", t)
                    F(n, ts(t3[:, t, :], b[:, 0:N], 64e-5, None, ALU.add, ALU.bypass))
                rsqrt(flat(t3))
                for t in range(2):
                    V(stt(oT[:, t, :], oT[:, t, :], col("rwkv_lnx_g_2", 2 * l + t), t3[:, t, :]))
                    V(ts(oT[:, t, :], oT[:, t, :], col("rwkv_lnx_b_2", 2 * l + t), None, ALU.add, ALU.bypass))
                mark(v.memset(st[:, 14:15], 0.0), "vector_step")
                for t in range(2):
                    n, b = ready(f"rkv{l}", t)
                    F(n, stt(t4[:, t, :], b[:, 0:N], 64.0, vv[:, t, :]))
                V(tt(oT, oT, t4, ALU.add))
                V(tt(mixT[:, 4:6, :], mixT[:, 4:6, :], oT))
                dve.wait_ge(S("sin_ready"), l + 1)
                V(tt(cosT, cosT, cosT))
                V(ts(cosT, cosT, -2.0, 1.0))
                V(tt(qk, PT[:, 24:28, :], over(4, cosT)))
                for i in range(4):
                    n, b = ready(f"rot{l}", i)
                    F(n, tt(rsw[:, i, :], b[:, 0:N], sinT))
                mark(tt(qk, qk, rsw, ALU.add), "vector_step")
                n, b = ready(f"rv{l}")
                F(n, v.tensor_copy(vtk, b[:, :].rearrange("p (c n) -> p c n", c=2)))
                for i in range(8):
                    n, b = ready(f"rs{l}", i)
                    h, q = i // 2, i % 2
                    w = 256 - 128 * q
                    F(n, tt(sc[:, h, 256 * q:256 * q + w], b[:, 0:w], k2("ret")[:, 256 * h:256 * h + w]))
                for h in range(4):
                    n, b = ready(f"ro{l}", h)
                    hp = slice(64 * (h % 2), 64 * (h % 2) + 64)
                    F(n, v.tensor_copy(ro[hp, h // 2, :], b[hp, 0:N]))
                for t in range(2):
                    n, b = ready(f"rnA{l}", t)
                    F(n, tt(rc[:, t, :], ro[:, t, :], b[:, 0:N], ALU.subtract))
                mark(tt(rq, rc, rc), "vector_step")
                for t in range(2):
                    n, b = ready(f"rnB{l}", t)
                    F(n, ts(ang[:, t, :], b[:, 0:N], 1e-5, None, ALU.add, ALU.bypass))
                rsqrt(flat(ang[:, 0:2, :]))
                V(tt(rc, rc, ang[:, 0:2, :]))
                dve.wait_ge(S("rg_sig"), l + 1)
                V(tt(rsw[:, 0:2, :], rsw[:, 0:2, :], PT[:, 30:32, :]))
                mark(tt(mixT[:, 6:8, :], rc, rsw[:, 0:2, :]), "vector_step")
                for m in range(8):
                    n, b = ready(f"out{l}", m)
                    F(n, stt(xT[:, m, :], xT[:, m, :], ALPHA, b[:, 0:N], ALU.mult, ALU.add))
                layer_norm(f"laA{l}", f"laB{l}", lambda k: ("ln1_g_2", 8 * l + k), lambda k: ("ln1_b_2", 8 * l + k))
                if l:
                    router(1, 8, 2)
                if l:
                    passes(dve, "m", routed, seen)
                else:
                    dense()
                dve.wait_ge(S("acc_done"), 3 + l)
                for i in range(4):
                    ins = v.tensor_copy(xT[:, 2 * i:2 * i + 2, :], P[4 + i][:, :].rearrange("p (t n) -> p t n", t=2))
                    if i < 3:
                        V(ins)
                    else:
                        mark(ins, "r_ready")
                layer_norm(f"lbA{l}", f"lbB{l}", lambda k: ("ln2_g_2", 8 * l + k), lambda k: ("ln2_b_2", 8 * l + k))
            for i in range(8):
                n, b = ready("fin", i)
                F(n, v.tensor_copy(res[:, i // 4, N * (i % 4):N * (i % 4) + N], b[:, 0:N]))

        @block.scalar
        def _(act_):
            mark, counts = marker(act_)
            seen = []
            roots = [0]

            def fn(out, in_, f, **kw):
                return nc.scalar.activation(out, in_, f, **kw)

            def A(ins):
                mark(ins, "act")

            def F(n, ins):
                ins.then_inc(S("mm_free"), 1)
                act_.wait_ge(S("mm_free"), n + 1)

            def ready(stage, i=0):
                n = START[stage] + i
                act_.wait_ge(S("mm_done"), n + 1)
                return n, P[n % 4]

            def root(x):
                roots[0] += 1
                act_.wait_ge(S("to_root"), roots[0])
                mark(fn(x, x, ACT.Sqrt), "rooted")

            def flat(x):
                return x.rearrange("p a b -> p (a b)")

            act_.dma_start(C1[:, :], a["const1"]).then_inc(S("consts"), 16)
            act_.dma_start(xload[:, 0:2, :], a["ctx"][0].rearrange("(c p) d -> p c d", p=128)).then_inc(S("xin"), 16)
            act_.dma_start(xload[:, 2:4, :], a["x"][0].rearrange("(c p) d -> p c d", p=128)).then_inc(S("xin"), 16)
            act_.wait_ge(S("vload_zero"), 1)
            for at, lo, src in a["vec_dmas"]:
                r = at % 128
                act_.dma_start(vload[r:r + src.shape[0], at // 128, lo:lo + src.shape[1]], src).then_inc(S("vecs"), 16)
            for dst, src in ((dtb[:, :], a["dt_bias"]), (av, a["a_log"])):
                act_.dma_start(dst, src.rearrange("a b c -> a (b c)").to_broadcast([128, 64])).then_inc(S("rows"), 16)
            act_.dma_start(dskip, a["d_skip"].to_broadcast([128, 32])).then_inc(S("rows"), 16)
            cs3 = cs.rearrange("p (k w) -> p k w", w=2)
            act_.wait_ge(S("mm_free"), START["xin"])
            mark(fn(cs3[:, :, 0], col("c", 0, 8), ACT.Sigmoid), "sil")
            mark(fn(cs3[:, :, 1], col("c_ctx", 0, 8), ACT.Sigmoid), "sil")
            root(inv)
            act_.wait_ge(S("craw_zero"), 1)
            for j in range(33):
                if j < 32:
                    n, b = ready("xb", j)
                    if j >= 2:
                        act_.wait_ge(S("conv_done"), j - 1)
                    if j < 24:
                        F(n, fn(craw[:, j % 2, :, 2:2 + N], b[:, :].rearrange("p (s n) -> p s n", s=2), ACT.Copy))
                    else:
                        F(n, fn(craw[:, j % 2, 1, 2:2 + N], b[:, 0:N], ACT.Copy))
                if j >= 1:
                    i = j - 1
                    act_.wait_ge(S("conv_done"), i + 1)
                    if i >= 2:
                        act_.wait_ge(S("turned"), min(i - 1, 24))
                        act_.wait_ge(S("conv_out"), i - 1)
                    s = slice(0, 2 * N) if i < 24 else slice(N, 2 * N)
                    mark(fn(csil[:, i % 2, s], cacc[:, i % 2, s], ACT.Sigmoid), "conv_sig")
            act_.wait_ge(S("abs"), 1)
            mark(fn(dA, dA, ACT.Exp, scale=-1.0), "exp_neg")
            A(fn(av, av, ACT.Exp))
            act_.wait_ge(S("one_more"), 1)
            mark(fn(dA, dA, ACT.Ln), "ln")
            for c in range(4):
                n, b = ready("seg", c)
                F(n, fn(ea[:, c, :], b[:, 0:192], ACT.Exp))
            for nx in range(16):
                act_.wait_ge(S("seg_done"), nx + 1)
                if nx:
                    act_.wait_ge(S("MT_ready"), nx)
                A(fn(EX[:, 0:512], P[5][:, :], ACT.Exp))
                mark(fn(EX[:, 512:1024], P[6][:, :], ACT.Exp), "EX_ready")
            for i in range(8):
                n, b = ready("z", i)
                if i >= 2:
                    act_.wait_ge(S("z_used"), i - 1)
                mark(fn(zs[:, i % 2, :], b[:, :], ACT.Sigmoid), "z_sig")
            act_.wait_ge(S("z_used"), 8)
            for c in range(2):
                mark(fn(junk, Y[:, c, :], ACT.Square, accum_out=st[:, c:c + 1]), "y_sq")
            root(st[:, 0:2])
            for m in range(8):
                n, b = ready("gs", m)
                F(n, fn(GT[:, m, :], b[:, 0:N], ACT.Sigmoid))
            for i in range(4):
                n, b = ready("u", i)
                F(n, fn(U[:, i % 2, 512 * (i // 2):512 * (i // 2) + 512], b[:, :], ACT.Copy))
            act_.wait_ge(S("mx_ssd"), 1)
            for m in range(8):
                n, b = ready("gf", m)
                F(n, fn(GT[:, m, :], b[:, 0:N], ACT.Sigmoid))
            root(inv[:, 0:N])

            def router(i, ne):
                for q in range(4):
                    n, b = ready(f"ht{i}", q)
                    F(n, fn(xtok[:, q % 2, 512 * (q // 2):512 * (q // 2) + 512], b[:, :], ACT.Copy))
                for c in range(2):
                    act_.wait_ge(S("lg_ready"), 2 * i + c + 1)
                    mark(fn(rt[:, 5 + c, 0:ne], lgs[:, c, 0:ne], ACT.Exp, bias=rt[:, 3, 8 * c:8 * c + 1]), "lg_exp")

            def routed(which, p_):
                ne, nf, _, _ = SPEC[which]
                pr, ex = Count(), Count()

                def xg_half():
                    fn(XG[:, 4:8, :], P[3][:, :].rearrange("p (k n) -> p k n", k=4), ACT.Copy)\
                        .then_inc(p_.sem("xgB"), 1)

                p_.wait(act_, "gathered", 1)
                xg_half()
                for e in turns(act_, which, [(pr, (nf + 1) // 2), (ex, 1)]):
                    x = ex.n
                    for p in range((nf + 1) // 2):
                        w = 128 * min(2, nf - 2 * p)
                        p_.wait(act_, "free", pr.value(pr.n + 1))
                        fn(sg[:, p % 2, 0:w], gl[:, p % 2, 0:w], ACT.Sigmoid, scale=1.702 if which == "a" else 1.0)\
                            .then_inc(p_.sem("sig"), 1)
                        pr.n += 1
                    p_.wait(act_, "gathered", ex.value(x + 2))
                    xg_half()
                    p_.wait(act_, "down", twice(ex, x) + 2)
                    fn(ys[:, 512:1024], P[1][:, :], ACT.Copy).then_inc(p_.sem("yB"), 1)
                    ex.n += 1

            def dense():
                for n in range(2 * FFE):
                    j = n % FFE
                    act_.wait_ge(S("ff_free"), n + 1)
                    mark(fn(sg[:, j % 2, :], gl[:, j % 2, :], ACT.Sigmoid), "sg_ready")

            router(0, NEXP)
            passes(act_, "a", routed, seen)
            root(inv[:, 0:N])
            for l in range(2):
                for i in range(32):
                    n, b = ready(f"p{l}", i)
                    w = TILES2[i][1]
                    F(n, fn(PT[0:w, i, :], b[0:w, 0:N], ACT.Copy))
                    if i == 12:
                        act_.wait_ge(S("vector_step"), mixed("ang_ready", l))
                        A(fn(sinT, ang[:, 2, :], ACT.Sin))
                        mark(fn(cosT, ang[:, 2, :], ACT.Sin, scale=0.5), "sin_ready")
                    if i == 28:
                        act_.wait_ge(S("vector_step"), mixed("rw_shift", l))
                        A(fn(PT[0:64, 21, :], PT[0:64, 21, :], ACT.Tanh))
                        A(fn(PT[:, 22, :], PT[:, 22, :], ACT.Sigmoid))
                        mark(fn(PT[0:32, 23, :], PT[0:32, 23, :], ACT.Sigmoid), "tanh_ready")
                for i, t in enumerate((4, 5, 10, 11)):
                    act_.dma_start(vd[l, i], PT[:, t, :]).then_inc(S("v_out"), 16)
                A(fn(qT[:, 0:2, :], PT[:, 0:2, :], ACT.Sigmoid))
                mark(fn(fT[:, 0:2, :], PT[:, 2:4, :], ACT.Sigmoid), "hsig")
                if l:
                    act_.wait_ge(S("lb_diff"), 1)
                    mark(fn(lbc[:, 0:2], lbc[:, 0:2], ACT.Sigmoid), "lb_sig")
                act_.wait_ge(S("abs"), l + 2)
                mark(fn(g1t[:, 1, :], g1t[:, 1, :], ACT.Exp, scale=-1.0), "exp_neg")
                act_.wait_ge(S("one_more"), l + 2)
                mark(fn(g1t[:, 1, :], g1t[:, 1, :], ACT.Ln), "ln")
                act_.wait_ge(S("ga_log"), l + 1)
                mark(fn(fT[:, 2, :], g1t[:, 0, :], ACT.Exp, scale=1.0 / 16), "ga_f")
                act_.wait_ge(S("v_out"), 64 * (l + 1))
                for n in range(48):
                    u, v0, m = n // 16, 4 * (n % 16), 48 * l + n
                    if m >= 3:
                        act_.wait_ge(S("kv_done"), m - 2)
                    for h in range(2 if u < 2 else 4):
                        tile, r = (u, 64 * h) if u < 2 else (2 + h // 2, 64 * (h % 2))
                        w = 64 if u < 2 else 32
                        src = vd[l, tile, r + v0:r + v0 + 4, :].unsqueeze(0).to_broadcast([w, 4, N])
                        act_.dma_start(vb[n % 3][w * h:w * h + w], src).then_inc(S(f"vb_in{n % 3}"), 16)
                act_.wait_ge(S("vector_step"), mixed("hsq", l))
                A(fn(hg[:, 0:2, :], PT[:, 6:8, :], ACT.Sigmoid))
                mark(fn(hg[:, 2:4, :], PT[:, 13:15, :], ACT.Sigmoid), "hg_sig")
                root(flat(hr4))
                act_.wait_ge(S("vector_step"), mixed("wa_ready", l))
                A(fn(tm, tm, ACT.Sigmoid))
                mark(fn(ga, ga, ACT.Sigmoid), "wa_sig")
                if l:
                    act_.wait_ge(S("vector_step"), mixed("vm", l))
                    mark(fn(vv, vv, ACT.Sigmoid), "vm_sig")
                root(flat(t3))
                act_.wait_ge(S("vector_step"), mixed("cum", l))
                A(fn(cl, tn, ACT.Exp))
                mark(fn(Bt, tn, ACT.Exp, scale=-1.0), "cum_exp")
                act_.wait_ge(S("vector_step"), mixed("cum_prev", l))
                mark(fn(tm, tn, ACT.Exp), "prev_exp")
                for lev in range(LEVELS):
                    for s_ in range(2):
                        act_.wait_ge(S("inv_y"), 2 * (LEVELS * l + lev) + s_ + 1)
                        mark(fn(YI[:, 4 * s_:4 * s_ + 4, :], P[4 + s_][:, :].rearrange("p (h n) -> p h n", h=4), ACT.Copy),
                             "inv_yc")
                for c in range(4):
                    o = slice(64 * (c % 2), 64 * (c % 2) + 64)
                    act_.wait_ge(S("W_done"), 4 * l + c + 1)
                    mark(fn(Wt[o, :], P[4][o, 0:N], ACT.Copy), "W_ready")
                    act_.wait_ge(S("U_done"), 4 * l + c + 1)
                    mark(fn(Ut[o, :], P[5][o, 0:N], ACT.Copy), "U_ready")
                root(flat(t3))
                act_.wait_ge(S("vector_step"), mixed("qk_ready", l))
                mark(fn(rsw[:, 0:2, :], PT[:, 30:32, :], ACT.Sigmoid), "rg_sig")
                root(flat(ang[:, 0:2, :]))
                root(inv[:, 0:N])
                if l:
                    router(1, 8)
                    passes(act_, "m", routed, seen)
                else:
                    dense()
                root(inv[:, 0:N])

        @block.gpsimd
        def _(pool):
            mark, counts = marker(pool)
            seen = []
            g_ = nc.gpsimd

            def Gm(ins):
                mark(ins, "pool")

            def tt(out, a_, b_, op=ALU.mult):
                return g_.tensor_tensor(out=out, in0=a_, in1=b_, op=op)

            def over(k, x):
                return x.unsqueeze(1).to_broadcast([128, k, x.shape[1]])

            def heads(x):
                return x.unsqueeze(2).to_broadcast([128, 8, 64])

            mark(g_.memset(craw, 0.0), "craw_zero")
            pool.wait_ge(S("wst_ready"), 1)
            for c in range(2):
                mark(tt(Y[:, c, :].rearrange("p (h e) -> p h e", h=32), XT[:, 2 + c, :].rearrange("p (h e) -> p h e", h=32),
                        dskip.unsqueeze(2).to_broadcast([128, 32, 64])), "Y_init")
            nx = ns = 0

            def steps(i, nx):
                d, step, c, g = SSD[i]
                hs = slice(32 * d + 8 * g, 32 * d + 8 * g + 8)
                if nx:
                    pool.wait_ge(S("seg_done"), nx)
                mark(tt(A1.rearrange("p (h l) -> p h l", h=8), dA[:, c, hs].unsqueeze(2).to_broadcast([128, 8, 128]),
                        over(8, k1("SU" if d else "SL"))), "A1_ready")

            for i, (d, step, c, g) in enumerate(SSD):
                hs = slice(32 * d + 8 * g, 32 * d + 8 * g + 8)
                xg = XT[:, c, 512 * g:512 * g + 512].rearrange("p (h e) -> p h e", h=8)
                if step >= 2 and SSD[i - 1][1] < 2:
                    steps(i, nx)
                if step < 3:
                    if ns:
                        pool.wait_ge(S("st_done"), ns)
                    mark(tt(XW.rearrange("p (h e) -> p h e", h=8), xg, heads(wst[:, c, hs])), "XW_ready")
                    ns += 1
                if step >= 2:
                    if i + 1 < len(SSD) and SSD[i + 1][1] >= 2:
                        steps(i + 1, nx + 1)
                    if nx:
                        pool.wait_ge(S("dg_done"), nx)
                    mark(tt(XD.rearrange("p (h e) -> p h e", h=8), xg, heads(dtt[:, c, hs])), "XD_ready")
                    nx += 1
            pool.wait_ge(S("squares"), 1)
            w_r = a["w_router"][0].rearrange("(k p) e -> p k e", p=128)
            pool.dma_start(wr, w_r).then_inc(S("router"), 16)
            pool.dma_start(rb, a["b_router"].to_broadcast([128, NEXP])).then_inc(S("router"), 16)
            pool.dma_start(bdn[0:NEXP, :], a["b_down"][0]).then_inc(S("router"), 16)

            def small_weights(l):
                for dst, src in ((gw2[0:16, :], a["gla_gate_w2_2"][l]), (w2s[0:64, :], a["rwkv_w2_2"][l]),
                                 (w2s[64:128, :], a["rwkv_a2_2"][l]), (g2a, a["rwkv_g2_2"][l][0:128]),
                                 (g2b[0:32, :], a["rwkv_g2_2"][l][128:160])):
                    pool.dma_start(dst, src).then_inc(S("lay"), 16)
                if l:
                    pool.dma_start(v1s, a["rwkv_v1_2"][0].rearrange("(t p) r -> p t r", p=128)).then_inc(S("lay"), 16)
                    pool.dma_start(v2s[0:32, :], a["rwkv_v2_2"][0]).then_inc(S("lay"), 16)

            def routed(which, p_):
                nf = SPEC[which][1]
                pr, c1 = Count(), Count()
                pool.sem_inc(p_.sem("act"), 2)
                for e in turns(pool, which, [(pr, (nf + 1) // 2), (c1, (nf + 1) // 2)]):
                    for p in range((nf + 1) // 2):
                        w = 128 * min(2, nf - 2 * p)
                        u_, gg, s_ = ul[:, p % 2, 0:w], gl[:, p % 2, 0:w], sg[:, p % 2, 0:w]
                        p_.wait(pool, "free", pr.value(pr.n + 1))
                        tt(u_, u_, gg).then_inc(p_.sem("pool"), 1)
                        c1.n += 1
                        p_.wait(pool, "pool", c1.value(c1.n))
                        p_.wait(pool, "sig", pr.value(pr.n + 1))
                        tt(acte[:, 2 * p:2 * p + w // 128, :].rearrange("p t n -> p (t n)"), u_, s_)\
                            .then_inc(p_.sem("act"), 1)
                        pr.n += 1

            def dense():
                for n in range(2 * FFE):
                    j = n % FFE
                    pool.wait_ge(S("ff_free"), n + 1)
                    u_ = ul[:, j % 2, :]
                    Gm(tt(u_, u_, gl[:, j % 2, :]))
                    pool.wait_ge(S("sg_ready"), n + 1)
                    mark(tt(act[:, j, :], u_, sg[:, j % 2, :]), "act_ready")

            passes(pool, "a", routed, seen)
            pool.wait_ge(S("acc_done"), 2)
            pool.dma_start(C2, a["const2"]).then_inc(S("consts2"), 16)
            pool.dma_start(posi, a["positions_2"].to_broadcast([128, N])).then_inc(S("positions"), 16)
            small_weights(0)
            vb_n = [0, 0, 0]
            for l in range(2):
                pool.wait_ge(S("kT_ready"), l + 1)
                for n in range(48):
                    m, u = 48 * l + n, n // 16
                    vb_n[n % 3] += 32 if u < 2 else 64
                    pool.wait_ge(S(f"vb_in{n % 3}"), vb_n[n % 3])
                    if m >= 2:
                        pool.wait_ge(S("scan_done"), m - 1)
                    mark(tt(kv[:, n % 2], vb[n % 3], over(4, kT[:, u, :])), "kv_done")
                pool.wait_ge(S("vector_step"), mixed("mix_ready", l))
                if l == 0:
                    small_weights(1)
                else:
                    pool.dma_start(wr[:, :, 0:8], a["moe_router_2"][0].rearrange("(k p) e -> p k e", p=128))\
                        .then_inc(S("router"), 16)
                if l:
                    pool.wait_ge(S("w_ready"), 2)
                    passes(pool, "m", routed, seen)
                else:
                    dense()


def kernel(**inputs):
    import concourse.bacc as bacc
    from concourse.bass_utils import run_bass_kernel_spmd

    nc = bacc.Bacc("TRN2", target_bir_lowering=False, num_devices=1)
    (c1, where1), (c2, where2) = constants()
    arrays, aps = {}, {}
    given = {k: np.ascontiguousarray(v) for k, v in inputs.items()}
    given["const1"], given["const2"] = c1, c2
    for name, v in given.items():
        arrays[f"in_{name}"] = v
        aps[name] = nc.dram_tensor(f"in_{name}", v.shape, mybir.dt.from_np(v.dtype), kind="ExternalInput").ap()
    aps["vec_dmas"] = vector_rows(aps)
    out = nc.dram_tensor("out", (1, 256, 1024), F32, kind="ExternalOutput").ap()
    build(nc, aps, out, where1, where2)
    r = run_bass_kernel_spmd(nc, [arrays], core_ids=[0])
    return r.results[0]["out"]
```
